# Optimizing a Trainium2 kernel written in Bass

```python
import jax
import jax.numpy as jnp
from jax import lax
import numpy as np

D_MODEL = 4096
BATCH = 1
SEQ = 256
DEPTH = 1

POOL_WINDOWS = (2, 4, 8, 16)
POOL_GROUPS = 4
POOL_WIDTH = D_MODEL // 2
POOL_GROUP_DIM = POOL_WIDTH // POOL_GROUPS
HEAD_DIM = 128
N_Q_HEADS = D_MODEL // 256
N_KV_HEADS = N_Q_HEADS // 4
GQA_GROUP = N_Q_HEADS // N_KV_HEADS
NSA_WIDTH = N_Q_HEADS * HEAD_DIM
KV_WIDTH = N_KV_HEADS * HEAD_DIM
N_NSA_BRANCHES = 3
CMP_BLOCK = 32
CMP_STRIDE = 16
SLC_BLOCK = 64
SLC_TOPK = 16
WINDOW = 512
Q_BLOCK = 128
N_MERGE = 2
IN_WIDTHS = (POOL_WIDTH, POOL_WIDTH, NSA_WIDTH, NSA_WIDTH, KV_WIDTH, KV_WIDTH, KV_WIDTH, KV_WIDTH, KV_WIDTH, KV_WIDTH, N_NSA_BRANCHES * N_Q_HEADS, N_MERGE * D_MODEL)
IN_WIDTH = 2 * POOL_WIDTH + 2 * NSA_WIDTH + 6 * KV_WIDTH + N_NSA_BRANCHES * N_Q_HEADS + N_MERGE * D_MODEL
EPS = 1e-6
NEG_INF = -1e30
FORCED_SCORE = 1e6

kernel_name = 'hybrid_pool_nsa_gated_trunk'

def rms_norm(x, g):
    xf = x.astype(jnp.float32)
    y = xf * lax.rsqrt(jnp.mean(xf * xf, axis=-1, keepdims=True) + EPS)
    return (y * g.astype(jnp.float32)).astype(x.dtype)

def masked_softmax(s, mask):
    p = jax.nn.softmax(jnp.where(mask, s, NEG_INF), axis=-1)
    return p * mask.astype(p.dtype)

def alibi_slopes():
    h = jnp.arange(1, N_Q_HEADS + 1, dtype=jnp.float32)
    return jnp.exp2(-8.0 * h / N_Q_HEADS).reshape(N_KV_HEADS, GQA_GROUP)

def split_points():
    return np.cumsum(np.array(IN_WIDTHS))[:-1].tolist()

def pool_mixer(u, w_grp, scale):
    B, T, _ = u.shape
    uf = u.astype(jnp.float32)
    c = jnp.concatenate([jnp.zeros((B, 1, POOL_WIDTH), jnp.float32), jnp.cumsum(uf, axis=1)], axis=1)
    t = jnp.arange(T)
    outs = []
    for gi, w in enumerate(POOL_WINDOWS):
        sl = slice(gi * POOL_GROUP_DIM, (gi + 1) * POOL_GROUP_DIM)
        lo = jnp.maximum(t + 1 - w, 0)
        win_sum = c[:, 1:, sl] - c[:, lo][..., sl]
        cnt = (t + 1 - lo).astype(jnp.float32)[None, :, None]
        outs.append(win_sum / cnt - uf[..., sl])
    m = jnp.stack(outs, axis=2).astype(u.dtype)
    m = jnp.einsum('btgc,gcd->btgd', m, w_grp).reshape(B, T, POOL_WIDTH)
    return m * scale

def compress(k, pe, w1, b1, w2):
    T = k.shape[0]
    r = CMP_BLOCK // CMP_STRIDE
    n_chunks = T // CMP_STRIDE
    kr = k.reshape(n_chunks, CMP_STRIDE, N_KV_HEADS, HEAD_DIM)
    blocks = jnp.concatenate([kr[i:n_chunks - r + 1 + i] for i in range(r)], axis=1)
    blocks = blocks + pe[None, :, None, :]
    flat = jnp.transpose(blocks, (0, 2, 1, 3)).reshape(-1, N_KV_HEADS, CMP_BLOCK * HEAD_DIM)
    return jax.nn.silu(flat @ w1 + b1) @ w2

def cmp_to_slc(nc, ns):
    cs = jnp.arange(nc)[:, None] * CMP_STRIDE
    ss = jnp.arange(ns)[None, :] * SLC_BLOCK
    ov = jnp.maximum(jnp.minimum(cs + CMP_BLOCK, ss + SLC_BLOCK) - jnp.maximum(cs, ss), 0)
    return ov.astype(jnp.float32) / CMP_STRIDE

def nsa_sequence(q, kc, vc, ks, vs, kw, vw, gates):
    T = q.shape[0]
    nc = kc.shape[0]
    ns = T // SLC_BLOCK
    nb = T // Q_BLOCK
    topk = min(SLC_TOPK, ns)
    scale = HEAD_DIM ** -0.5
    slopes = alibi_slopes()
    ovl = cmp_to_slc(nc, ns)
    cmp_end = jnp.arange(nc) * CMP_STRIDE + CMP_BLOCK - 1
    ks_blk = jnp.transpose(ks.reshape(ns, SLC_BLOCK, N_KV_HEADS, HEAD_DIM), (2, 0, 1, 3))
    vs_blk = jnp.transpose(vs.reshape(ns, SLC_BLOCK, N_KV_HEADS, HEAD_DIM), (2, 0, 1, 3))
    pad = jnp.zeros((WINDOW, N_KV_HEADS, HEAD_DIM), kw.dtype)
    kw_p = jnp.concatenate([pad, kw], axis=0)
    vw_p = jnp.concatenate([pad, vw], axis=0)
    qb = q.reshape(nb, Q_BLOCK, N_KV_HEADS, GQA_GROUP, HEAD_DIM)
    gb = gates.reshape(nb, Q_BLOCK, N_KV_HEADS, GQA_GROUP, N_NSA_BRANCHES)

    def block(args):
        b, qi, gi = args
        t = b * Q_BLOCK + jnp.arange(Q_BLOCK)
        s = jnp.einsum('qhgd,nhd->qhgn', qi, kc).astype(jnp.float32) * scale
        dist = (t[:, None] - cmp_end[None, :]).astype(jnp.float32)
        s = s - slopes[None, :, :, None] * dist[:, None, None, :]
        mask_c = (cmp_end[None, :] <= t[:, None])[:, None, None, :]
        p_c = masked_softmax(s, mask_c)
        o_c = jnp.einsum('qhgn,nhd->qhgd', p_c.astype(vc.dtype), vc)
        imp = jnp.einsum('qhn,nj->qhj', p_c.sum(axis=2), ovl)
        j = jnp.arange(ns)[None, :]
        cur = (t // SLC_BLOCK)[:, None]
        valid = j <= cur
        forced = (j == 0) | (j == cur) | (j == cur - 1)
        score = jnp.where(valid[:, None, :], jnp.where(forced[:, None, :], FORCED_SCORE, imp), -1.0)
        vals, idx = lax.top_k(score, topk)
        sel_ok = vals >= 0.0
        idx_h = jnp.transpose(idx, (1, 0, 2))
        k_sel = jax.vmap(lambda kb, ib: kb[ib])(ks_blk, idx_h)
        v_sel = jax.vmap(lambda vb, ib: vb[ib])(vs_blk, idx_h)
        pos = idx[..., None] * SLC_BLOCK + jnp.arange(SLC_BLOCK)
        s = jnp.einsum('qhgd,hqnld->qhgnl', qi, k_sel).astype(jnp.float32) * scale
        dist = (t[:, None, None, None] - pos).astype(jnp.float32)
        s = s - slopes[None, :, :, None, None] * dist[:, :, None]
        mask_s = (sel_ok[..., None] & (pos <= t[:, None, None, None]))[:, :, None]
        s = s.reshape(Q_BLOCK, N_KV_HEADS, GQA_GROUP, topk * SLC_BLOCK)
        mask_s = mask_s.reshape(Q_BLOCK, N_KV_HEADS, 1, topk * SLC_BLOCK)
        p_s = masked_softmax(s, mask_s)
        v_flat = v_sel.reshape(N_KV_HEADS, Q_BLOCK, topk * SLC_BLOCK, HEAD_DIM)
        o_s = jnp.einsum('qhgm,hqmd->qhgd', p_s.astype(v_flat.dtype), v_flat)
        kwin = lax.dynamic_slice_in_dim(kw_p, b * Q_BLOCK, Q_BLOCK + WINDOW, axis=0)
        vwin = lax.dynamic_slice_in_dim(vw_p, b * Q_BLOCK, Q_BLOCK + WINDOW, axis=0)
        spos = b * Q_BLOCK - WINDOW + jnp.arange(Q_BLOCK + WINDOW)
        s = jnp.einsum('qhgd,khd->qhgk', qi, kwin).astype(jnp.float32) * scale
        dist = t[:, None] - spos[None, :]
        s = s - slopes[None, :, :, None] * dist.astype(jnp.float32)[:, None, None, :]
        mask_w = ((dist >= 0) & (dist < WINDOW) & (spos[None, :] >= 0))[:, None, None, :]
        p_w = masked_softmax(s, mask_w)
        o_w = jnp.einsum('qhgk,khd->qhgd', p_w.astype(vwin.dtype), vwin)
        g = jax.nn.sigmoid(gi.astype(jnp.float32))
        o = g[..., 0:1] * o_c + g[..., 1:2] * o_s + g[..., 2:3] * o_w
        return o.astype(q.dtype)

    out = lax.map(block, (jnp.arange(nb), qb, gb))
    return out.reshape(T, NSA_WIDTH)

def hybrid_layer(x, norm_g, w_in, merge_bias, pool_w, pool_scale, q_norm_g, k_norm_g, cmp_pe, cmp_w1, cmp_b1, cmp_w2, w_pool_up, w_nsa_up, w_out):
    B, T, _ = x.shape
    h = rms_norm(x, norm_g)
    proj = h @ w_in
    pool_u, pool_z, q, nsa_z, kc, vc, ks, vs, kw, vw, nsa_g, merge_g = jnp.split(proj, split_points(), axis=-1)
    pool_out = pool_mixer(pool_u, pool_w, pool_scale) * jax.nn.silu(pool_z)
    heads = lambda a: a.reshape(B, T, N_KV_HEADS, HEAD_DIM)
    q = rms_norm(q.reshape(B, T, N_Q_HEADS, HEAD_DIM), q_norm_g)
    comp = jax.vmap(compress, in_axes=(0, None, None, None, None))
    kc = rms_norm(comp(heads(kc), cmp_pe[0], cmp_w1[0], cmp_b1[0], cmp_w2[0]), k_norm_g[0])
    vc = comp(heads(vc), cmp_pe[1], cmp_w1[1], cmp_b1[1], cmp_w2[1])
    ks = rms_norm(heads(ks), k_norm_g[1])
    kw = rms_norm(heads(kw), k_norm_g[2])
    gates = nsa_g.reshape(B, T, N_Q_HEADS, N_NSA_BRANCHES)
    o = jax.vmap(nsa_sequence)(q, kc, vc, ks, heads(vs), kw, heads(vw), gates)
    nsa_out = o * jax.nn.silu(nsa_z)
    gm = jax.nn.sigmoid(merge_g.reshape(B, T, N_MERGE, D_MODEL) + merge_bias)
    y = gm[:, :, 0] * (pool_out @ w_pool_up) + gm[:, :, 1] * (nsa_out @ w_nsa_up)
    return x + (y.astype(x.dtype) @ w_out)

def setup_inputs(seed: int = 0) -> dict:
    key = jax.random.key(seed)
    ks = jax.random.split(key, 16)

    def nrm(k, shape, s):
        return jax.random.normal(k, shape, jnp.float32) * s

    return {
        'x': nrm(ks[0], (BATCH, SEQ, D_MODEL), 1.0),
        'norm_g': 1.0 + nrm(ks[1], (DEPTH, D_MODEL), 0.02),
        'w_in': nrm(ks[2], (DEPTH, D_MODEL, IN_WIDTH), D_MODEL ** -0.5),
        'merge_bias': nrm(ks[3], (DEPTH, N_MERGE, D_MODEL), 0.01),
        'pool_w': nrm(ks[4], (DEPTH, POOL_GROUPS, POOL_GROUP_DIM, POOL_GROUP_DIM), POOL_GROUP_DIM ** -0.5),
        'pool_scale': 1.0 + nrm(ks[5], (DEPTH, POOL_WIDTH), 0.1),
        'q_norm_g': 1.0 + nrm(ks[6], (DEPTH, HEAD_DIM), 0.02),
        'k_norm_g': 1.0 + nrm(ks[7], (DEPTH, N_NSA_BRANCHES, HEAD_DIM), 0.02),
        'cmp_pe': nrm(ks[8], (DEPTH, 2, CMP_BLOCK, HEAD_DIM), 0.1),
        'cmp_w1': nrm(ks[9], (DEPTH, 2, CMP_BLOCK * HEAD_DIM, HEAD_DIM), (CMP_BLOCK * HEAD_DIM) ** -0.5),
        'cmp_b1': nrm(ks[10], (DEPTH, 2, HEAD_DIM), 0.01),
        'cmp_w2': nrm(ks[11], (DEPTH, 2, HEAD_DIM, HEAD_DIM), HEAD_DIM ** -0.5),
        'w_pool_up': nrm(ks[12], (DEPTH, POOL_WIDTH, D_MODEL), POOL_WIDTH ** -0.5),
        'w_nsa_up': nrm(ks[13], (DEPTH, NSA_WIDTH, D_MODEL), NSA_WIDTH ** -0.5),
        'w_out': nrm(ks[14], (DEPTH, D_MODEL, D_MODEL), D_MODEL ** -0.5),
    }

def reference(x, norm_g, w_in, merge_bias, pool_w, pool_scale, q_norm_g, k_norm_g, cmp_pe, cmp_w1, cmp_b1, cmp_w2, w_pool_up, w_nsa_up, w_out):
    for l in range(DEPTH):
        x = hybrid_layer(x, norm_g[l], w_in[l], merge_bias[l], pool_w[l], pool_scale[l], q_norm_g[l], k_norm_g[l], cmp_pe[l], cmp_w1[l], cmp_b1[l], cmp_w2[l], w_pool_up[l], w_nsa_up[l], w_out[l])
    return x


_drawn_inputs = setup_inputs


def setup_inputs(seed=0):
    import zlib

    import numpy as np

    out = dict(_drawn_inputs(seed))
    spreads = {}
    factors = {'norm_g': 6.14,
     'merge_bias': 36.201,
     'q_norm_g': 8.0,
     'k_norm_g': 8.0,
     'cmp_pe': 6.917,
     'cmp_b1': 27.772}
    for name, (base, spread) in spreads.items():
        noise = np.random.default_rng([zlib.crc32(name.encode()), seed]).standard_normal(out[name].shape)
        drawn = base * np.exp(spread * noise) if base else spread * noise
        out[name] = jnp.asarray(drawn.astype(out[name].dtype))
    for name, factor in factors.items():
        out[name] = (out[name] * factor).astype(out[name].dtype)
    return out
```

```python
import math

import concourse.bass as bass
from concourse import mybir
from concourse.alu_op_type import AluOpType as ALU

ACT = mybir.ActivationFunctionType
AX = mybir.AxisListType
F32 = mybir.dt.float32
F32R = mybir.dt.float32r

P = 128
BANK = 512
WIDTH = 1024
RING = 4
LEAD = 2
EPS = 1e-6
MASKED = -1e36
WINDOWS = (2, 4, 8, 16)
CMP_BLOCK, CMP_STRIDE = 32, 16


def trunk(nc, x, norm_g, w_in, merge_bias, pool_w, pool_scale, q_norm_g, k_norm_g, cmp_pe, cmp_w1,
          cmp_b1, cmp_w2, w_pool_up, w_nsa_up, w_out, out):
    _, T, D = x.shape
    HD = q_norm_g.shape[1]
    TT = T // P
    KT = D // P
    POOL = pool_scale.shape[1]
    PG = POOL // len(WINDOWS)
    QW = w_nsa_up.shape[1]
    H = QW // HD
    KVH = H // 4
    GQ = H // KVH
    KVW = KVH * HD
    NBR = 3
    NC = (T - CMP_BLOCK) // CMP_STRIDE + 1
    UT = POOL // P
    NH = WIDTH // BANK
    GATES = NBR * H
    assert (T, D, HD, KVH, PG, QW, KVW) == (256, 4096, 128, 4, 512, 2048, 512)

    COL_U, COL_Z = 0, POOL
    COL_Q = 2 * POOL
    COL_NZ = COL_Q + QW
    COL_KV = COL_NZ + QW
    COL_G = COL_KV + 6 * KVW
    COL_M = COL_G + GATES
    assert COL_Z == 2 * WIDTH

    N_A = 5
    CH_L2 = N_A * KT
    CH_TL = CH_L2 + KVH * KT
    CH_P3 = CH_TL + 4 * KT
    PER3 = 2 * UT + 2 * KT
    N_Y = D // WIDTH
    CH_EP = CH_P3 + (N_Y - 1) * PER3
    CH_P4 = CH_EP + 2 * UT
    CHUNKS = CH_P4 + N_Y * KT
    Q_L2, Q_TL, Q_P3 = N_A, N_A + KVH, N_A + KVH + 4
    Q_EP = Q_P3 + 4 * (N_Y - 1)
    Q_P4 = Q_EP + 2

    w_in, w_pu, w_nu, w_o = w_in[0], w_pool_up[0], w_nsa_up[0], w_out[0]
    x_pt = x[0].rearrange("(t p) c -> p t c", p=P)
    out_pt = out[0].rearrange("(t p) c -> p t c", p=P)

    at = [(nc.sbuf_base + 63) // 64 * 64]

    def region(size):
        start = at[0]
        at[0] += (size + 31) // 32 * 32
        return start

    def view(name, start, shape, dt=F32):
        return nc.alloc_sbuf_tensor_at(name, shape, dt, offset=start)

    def sized(name, shape, dt=F32):
        return view(name, region(4 * math.prod(shape[1:])), shape, dt)

    act_hi = sized("act_hi", [P, KT, T], F32R)
    act_lo = sized("act_lo", [P, KT, T], F32R)
    raw = sized("raw", [P, RING, WIDTH])
    w_hi = sized("w_hi", [P, RING, WIDTH], F32R)
    w_lo = sized("w_lo", [P, RING, WIDTH], F32R)
    ident = sized("ident", [P, P])
    vec_t = sized("vec_t", [P, P])
    rstd = sized("rstd", [P, TT])
    row_ss = sized("row_ss", [P, TT])
    neg_half = sized("neg_half", [P, 12])
    scale_g = sized("scale_g", [P, 4])
    bias_at = region(4 * WIDTH)
    bias = view("bias", bias_at, [P, WIDTH])
    vec_rows = view("vec_rows", bias_at, [P, P])
    reg_a = region(32768)
    reg_t = region(16384)
    reg_k = region(24576)
    reg_q = region(16384)
    reg_n = region(16384)
    assert at[0] <= nc.sbuf_usable_end, (at[0], nc.sbuf_usable_end)

    x_tok = view("x_tok", reg_a, [P, TT, D])
    w1 = view("w1", reg_a, [P, 2, CMP_BLOCK, HD])
    uz = view("uz", reg_a, [P, 8, TT, PG])
    pool_hi = view("pool_hi", reg_a, [P, UT, T], F32R)
    pool_lo = view("pool_lo", reg_a + 16384, [P, UT, T], F32R)
    x_out = view("x_out", reg_a, [P, N_Y, TT, WIDTH])
    ys = view("ys", reg_t, [P, 1 + N_Y, TT, WIDTH])
    kvq = view("kvq", reg_k, [P, 6 + KVH, TT, KVW])
    nsa_hi = view("nsa_hi", reg_q, [P, UT, T], F32R)
    nsa_lo = view("nsa_lo", reg_n, [P, UT, T], F32R)
    u_g = view("u_g", reg_k, [P, TT, PG])
    mix_t = view("mix_t", reg_k, [P, PG // P, T])
    z_g = view("z_g", reg_k + 4096, [P, TT, PG])
    silu_zt = view("silu_zt", reg_k + 4096, [P, PG // P, T])
    pw = view("pw", reg_k + 8192, [P, PG // P, PG])
    n_tok = view("n_tok", reg_k + 16384, [P, TT, WIDTH])
    band = view("band", reg_t, [P, 4, 3 * P])
    t_at = [reg_t]

    def in_t(name, shape, dt=F32):
        start = t_at[0]
        t_at[0] += (4 * math.prod(shape[1:]) + 31) // 32 * 32
        assert t_at[0] <= reg_t + 16384, name
        return view(name, start, shape, dt)

    n_at = [reg_n]

    def in_n(name, shape, dt=F32):
        start = n_at[0]
        n_at[0] += (4 * math.prod(shape[1:]) + 31) // 32 * 32
        assert n_at[0] <= reg_n + 16384, name
        return view(name, start, shape, dt)

    dist = in_t("dist", [P, GQ, 3 * P])
    dist_c = in_t("dist_c", [P, GQ, TT, NC])
    kc_t = in_t("kc_t", [P, KVH * NC])
    vc = in_t("vc", [NC, KVH, HD])
    gate6 = in_t("gate6", [P, H, 6])
    row_mask = in_t("row_mask", [P, 1])
    t_mark = t_at[0]
    stat_ss = in_t("stat_ss", [P, 12])
    stat_rs = in_t("stat_rs", [P, 12])
    neg_max = in_t("neg_max", [P, 6])
    sums = in_t("sums", [P, 6])
    inv = in_t("inv", [P, 6])
    wgt = in_t("wgt", [P, 6])
    s_cmp = in_t("s_cmp", [P, TT, NC])
    prob_ct = in_t("prob_ct", [NC, TT, P])
    prob_t = in_t("prob_t", [P, 2, 3 * P])
    qk = in_n("qk", [P, TT, 6, HD])
    qk_t = in_n("qk_t", [P, 6, T])
    s = in_n("s", [P, 2, 3 * P])
    wg = view("wg", reg_n, [P, KT, GATES])
    kb_v = view("kb_v", reg_n, [P, CMP_STRIDE, KVH + 1, CMP_STRIDE])
    wg_hi = view("wg_hi", reg_n + 6144, [P, KT, GATES], F32R)
    kb_k = view("kb_k", reg_q + 8192, [P, CMP_STRIDE, KVH + 1, CMP_STRIDE])
    wg_lo = view("wg_lo", reg_t + 16384 - 6144, [P, KT, GATES], F32R)
    assert t_mark <= reg_t + 16384 - 6144
    w2 = view("w2", reg_n + 12288, [P, 2, HD])
    hid_b = view("hid_b", reg_n + 13312, [P, 2])
    hid_x = view("hid_x", reg_n + 13344, [P, 2, KVH * NC])
    hid_s = view("hid_s", reg_n + 13824, [P, 2, KVH * NC])
    hid = view("hid", reg_n + 14304, [P, 2, KVH * NC])
    kc_n = view("kc_n", reg_n + 14784, [KVH * NC, HD])
    kc_sq = view("kc_sq", reg_n + 15296, [KVH * NC, HD])
    kc_ss = view("kc_ss", reg_n + 15808, [KVH * NC, 1])
    kc_rs = view("kc_rs", reg_n + 15840, [KVH * NC, 1])

    V_NORM = 0
    V_SCALE = V_NORM + KT
    V_QG = V_SCALE + UT
    V_KG = V_QG + 1
    V_PE = V_KG + NBR
    V_B1 = V_PE + 2 * CMP_BLOCK
    V_END = V_B1 + 2

    ps = nc.alloc_psum_tensor("ps", [P, 8, BANK], F32)

    sems = {}

    def sem(name):
        sems[name] = nc.alloc_semaphore(name)
        return sems[name]

    vec_landed = sem("vec_landed")
    x_landed = [sem(f"x_landed{i}") for i in range(4)]
    raw_landed = [sem(f"raw_landed{i}") for i in range(RING)]
    wg_landed = sem("wg_landed")
    w1_landed = sem("w1_landed")
    bias_landed = sem("bias_landed")
    pw_landed = sem("pw_landed")
    xo_landed = sem("xo_landed")
    out_stored = sem("out_stored")
    hi_done = sem("hi_done")
    split_done = sem("split_done")
    weights_free = sem("weights_free")
    acc_done = sem("acc_done")
    acc_free = [sem("acc_free0"), sem("acc_free1")]
    const_pool = sem("const_pool")
    const_ready = sem("const_ready")
    band_built = sem("band_built")
    vec_psum = sem("vec_psum")
    vec_ready = sem("vec_ready")
    x_psum = sem("x_psum")
    xt_hi = sem("xt_hi")
    xt_lo = sem("xt_lo")
    sq_act = sem("sq_act")
    sq_dve = sem("sq_dve")
    row_ms = sem("row_ms")
    rstd_ready = sem("rstd_ready")
    wg_hi_done = sem("wg_hi_done")
    wg_lo_done = sem("wg_lo_done")
    ct_psum = sem("ct_psum")
    ct_sbuf = sem("ct_sbuf")
    kb_zero = sem("kb_zero")
    kb_pos = sem("kb_pos")
    hid_psum = sem("hid_psum")
    hid_step = sem("hid_step")
    hid_sig = sem("hid_sig")
    w2_psum = sem("w2_psum")
    kc_step = sem("kc_step")
    kc_rstd = sem("kc_rstd")
    kct_psum = sem("kct_psum")
    kct_ready = sem("kct_ready")
    vc_ready = sem("vc_ready")
    gate_psum = sem("gate_psum")
    gate_sig = sem("gate_sig")
    gate_ready = sem("gate_ready")
    qk_sq = sem("qk_sq")
    qk_ss = sem("qk_ss")
    qk_ms = sem("qk_ms")
    qk_rstd = sem("qk_rstd")
    qk_normed = sem("qk_normed")
    qkt_psum = sem("qkt_psum")
    qkt_act = sem("qkt_act")
    qkt_dve = sem("qkt_dve")
    scores_done = sem("scores_done")
    biased = sem("biased")
    head_max = sem("head_max")
    exp_done = sem("exp_done")
    inv_done = sem("inv_done")
    wgt_done = sem("wgt_done")
    probs_ready = sem("probs_ready")
    probt_psum = sem("probt_psum")
    probt_ready = sem("probt_ready")
    pv_done = sem("pv_done")
    head_out = sem("head_out")
    dist_scaled = sem("dist_scaled")
    nz_sig = sem("nz_sig")
    nz_silu = sem("nz_silu")
    n_ready = sem("n_ready")
    nt_psum = sem("nt_psum")
    nt_hi = sem("nt_hi")
    nt_lo = sem("nt_lo")
    gate_out = sem("gate_out")
    uz_copied = sem("uz_copied")
    mix_psum = sem("mix_psum")
    mix_act = sem("mix_act")
    mix_dve = sem("mix_dve")
    zt_psum = sem("zt_psum")
    zt_sig = sem("zt_sig")
    zt_silu = sem("zt_silu")
    pwt_psum = sem("pwt_psum")
    pool_v = sem("pool_v")
    pool_hi_done = sem("pool_hi_done")
    pool_lo_done = sem("pool_lo_done")
    y_sum = sem("y_sum")
    yt_psum = sem("yt_psum")
    yt_hi = sem("yt_hi")
    yt_lo = sem("yt_lo")

    def up(v):
        return v.bitcast(F32)

    block = nc.Block()
    with block:

        @block.sync
        def _(sp):
            def load(first, rows, cols, beside=None):
                for kt in range(rows.shape[0] // P):
                    if kt == 2 * RING and beside:
                        beside()
                    sp.wait_ge(split_done, first + (kt + 1))
                    sp.dma_start(raw[:, kt % RING, :], rows[kt * P:(kt + 1) * P, cols]).then_inc(
                        raw_landed[kt % RING], 16)

            for start, rows in (
                (V_NORM, norm_g[0].rearrange("(a b) -> a b", b=P)),
                (V_SCALE, pool_scale[0].rearrange("(a b) -> a b", b=P)),
                (V_QG, q_norm_g),
                (V_KG, k_norm_g[0]),
                (V_PE, cmp_pe[0].rearrange("a j d -> (a j) d")),
                (V_B1, cmp_b1[0]),
            ):
                sp.dma_start(vec_rows[start:start + rows.shape[0], :], rows).then_inc(vec_landed, 16)
            for i in range(4):
                c = slice(i * WIDTH, (i + 1) * WIDTH)
                sp.dma_start(x_tok[:, :, c], x_pt[:, :, c]).then_inc(x_landed[i], 16)
            with sp.Fori(0, 3) as i:
                load(i * KT, w_in, bass.ds(i * WIDTH + COL_KV, WIDTH))
            sp.dma_start(wg[:], w_in[:, COL_G:COL_G + GATES].rearrange("(k p) n -> p k n", p=P)).then_inc(
                wg_landed, 16)
            sp.wait_ge(sq_act, 1)
            sp.wait_ge(sq_dve, 1)
            sp.wait_ge(xt_lo, 16)
            for kv in range(2):
                sp.dma_start(w1[:, kv], cmp_w1[0, kv].rearrange("(j d) e -> d j e", d=HD)).then_inc(w1_landed, 16)
            sp.dma_start(w2[:], cmp_w2[0].rearrange("a e f -> e a f")).then_inc(w1_landed, 16)
            with sp.Fori(0, 2) as i:
                load(i * KT + 3 * KT, w_in, bass.ds(i * WIDTH + COL_Q, WIDTH))
            with sp.Fori(0, KVH) as i:
                load(i * KT + CH_L2, w_in, bass.ds(i * WIDTH + COL_U, WIDTH))

            def load_pool_w(n):
                sp.wait_ge(head_out, 1 + H)
                sp.wait_ge(pool_lo_done, n * 2 + 2)
                sp.dma_start(pw[:], pool_w[0, bass.ds(n, 1)].rearrange("g (c p) d -> p (g c) d", p=P)).then_inc(
                    pw_landed, 16)

            def load_bias(which, col, left, between=None):
                sp.wait_ge(acc_free[1], left)
                sp.wait_ge(vec_ready, 1)
                if between:
                    between()
                sp.dma_start(bias[:], merge_bias[0, which, bass.ds(col, WIDTH)].to_broadcast([P, WIDTH])).then_inc(
                    bias_landed, 16)

            with sp.Fori(0, 2) as i:
                load(i * 2 * KT + CH_TL, w_in, bass.ds(i * WIDTH + COL_NZ, WIDTH), lambda: load_pool_w(i * 2))

                def beside():
                    load_bias(bass.ds(i, 1), 0, i * 2 + (Q_TL + 1), lambda: load_pool_w(i * 2 + 1))

                load(i * 2 * KT + CH_TL + KT, w_in, bass.ds(i * D + COL_M, WIDTH), beside)
            with sp.Fori(0, N_Y - 1) as i:
                load(i * PER3 + CH_P3, w_pu, bass.ds(i * WIDTH, WIDTH))
                load(i * PER3 + CH_P3 + UT, w_nu, bass.ds(i * WIDTH, WIDTH))
                for which in range(2):
                    load(i * PER3 + CH_P3 + 2 * UT + which * KT, w_in,
                         bass.ds(i * WIDTH + COL_M + which * D + WIDTH, WIDTH),
                         lambda: load_bias(slice(which, which + 1), i * WIDTH + WIDTH,
                                           i * 4 + (Q_P3 + 1 + 3 * which)))
            load(CH_EP, w_pu, slice((N_Y - 1) * WIDTH, N_Y * WIDTH))
            load(CH_EP + UT, w_nu, slice((N_Y - 1) * WIDTH, N_Y * WIDTH))
            sp.wait_ge(weights_free, CH_EP + UT + RING)
            for g in range(N_Y):
                sp.dma_start(x_out[:, g], x_pt[:, :, g * WIDTH:(g + 1) * WIDTH]).then_inc(xo_landed, 16)
            with sp.Fori(0, N_Y) as i:
                load(i * KT + CH_P4, w_o, bass.ds(i * WIDTH, WIDTH))

        @block.gpsimd
        def _(pool):
            g = nc.gpsimd
            g.memset(ident[:], 0.0).then_inc(const_pool, 1)
            g.memset(neg_half[:], -0.5).then_inc(const_pool, 1)
            g.memset(row_mask[:], 1.0).then_inc(const_pool, 1)
            pool.wait_ge(const_pool, 3)
            g.affine_select(out=ident[:], in_=ident[:], compare_op=ALU.not_equal, fill=1.0, base=0,
                            pattern=[[-1, P]], channel_multiplier=1).then_inc(const_ready, 1)
            g.affine_select(out=row_mask[:], in_=row_mask[:], compare_op=ALU.is_ge, fill=0.0,
                            base=1 - CMP_BLOCK, pattern=[[0, 1]], channel_multiplier=1).then_inc(const_ready, 1)
            g.iota(dist[:, 0, 0:P], [[1, P]], base=0, channel_multiplier=-1,
                   allow_small_or_imprecise_dtypes=True).then_inc(const_pool, 1)
            g.iota(dist[:, 0, P:3 * P], [[1, 2 * P]], base=-P, channel_multiplier=-1,
                   allow_small_or_imprecise_dtypes=True).then_inc(const_pool, 1)
            g.iota(dist_c[:, 0], [[-P, TT], [CMP_STRIDE, NC]], base=CMP_BLOCK - 1, channel_multiplier=-1,
                   allow_small_or_imprecise_dtypes=True).then_inc(const_pool, 1)
            pool.wait_ge(const_pool, 6)
            for h in reversed(range(GQ)):
                slope = 2.0 ** (-8.0 * (h + 1) / H)
                if h == 0:
                    pool.wait_ge(const_pool, 6 + 2 * (GQ - 1))
                g.tensor_scalar(dist[:, h], dist[:, 0], slope, None, ALU.mult).then_inc(const_pool, 1)
                g.tensor_scalar(dist_c[:, h], dist_c[:, 0], slope, None, ALU.mult).then_inc(const_pool, 1)
            pool.wait_ge(const_pool, 6 + 2 * GQ)
            g.affine_select(out=dist[:, :, 0:P], in_=dist[:, :, 0:P], compare_op=ALU.is_ge, fill=MASKED,
                            base=0, pattern=[[0, GQ], [-1, P]], channel_multiplier=1).then_inc(const_ready, 1)
            g.affine_select(out=dist[:, :, P:3 * P], in_=dist[:, :, P:3 * P], compare_op=ALU.is_ge, fill=MASKED,
                            base=P, pattern=[[0, GQ], [-1, 2 * P]], channel_multiplier=1).then_inc(const_ready, 1)
            g.affine_select(out=dist_c[:], in_=dist_c[:], compare_op=ALU.is_ge, fill=MASKED,
                            base=1 - CMP_BLOCK, pattern=[[0, GQ], [P, TT], [-CMP_STRIDE, NC]],
                            channel_multiplier=1).then_inc(const_ready, 1)
            pool.wait_ge(row_ms, 1)
            g.tensor_tensor(rstd[:], row_ss[:], neg_half[:, 0:TT], ALU.pow).then_inc(rstd_ready, 1)
            pool.wait_ge(kc_step, 3)
            g.tensor_tensor(kc_rs[:], kc_ss[:], neg_half[0:KVH * NC, 0:1], ALU.pow).then_inc(kc_rstd, 1)
            with pool.Fori(0, KVH) as j:
                pool.wait_ge(qk_ms, j + 1)
                g.tensor_tensor(stat_rs[:], stat_ss[:], neg_half[:], ALU.pow).then_inc(qk_rstd, 1)
            pool.wait_ge(acc_free[0], 1 + Q_TL)
            pool.wait_ge(acc_free[1], 1 + Q_TL)
            for n, w in enumerate(WINDOWS):
                g.memset(band[:, n], 1.0 / w).then_inc(band_built, 1)
            pool.wait_ge(band_built, 4)
            for n, w in enumerate(WINDOWS):
                for t in range(w - 1):
                    g.memset(band[:, n, t:t + 1], 1.0 / (t + 1)).then_inc(band_built, 1)
            done = 4 + sum(w - 1 for w in WINDOWS)
            pool.wait_ge(band_built, done)
            for n, w in enumerate(WINDOWS):
                for part, base in ((slice(0, 2 * P), 0), (slice(2 * P, 3 * P), 0)):
                    b = band[:, n, part]
                    g.affine_select(out=b, in_=b, compare_op=ALU.is_ge, fill=0.0, base=base,
                                    pattern=[[1, part.stop - part.start]], channel_multiplier=-1).then_inc(band_built, 1)
            done += 8
            pool.wait_ge(band_built, done)
            for n, w in enumerate(WINDOWS):
                for part in (slice(0, 2 * P), slice(2 * P, 3 * P)):
                    b = band[:, n, part]
                    g.affine_select(out=b, in_=b, compare_op=ALU.is_ge, fill=0.0, base=w - 1,
                                    pattern=[[-1, part.stop - part.start]], channel_multiplier=1).then_inc(band_built, 1)
            done += 8
            pool.wait_ge(band_built, done)
            for n, w in enumerate(WINDOWS):
                for start in (0, 2 * P):
                    b = band[:, n, start:start + P]
                    g.tensor_tensor(b, b, ident[:], ALU.subtract).then_inc(band_built, 1)
            with pool.Fori(0, 2) as i:
                for half in range(2):
                    pool.wait_ge(pool_lo_done, i * 4 + 2 * half + 2)
                    g.tensor_copy(u_g[:], uz[:, bass.ds(i * 2 + half, 1)])
                    g.tensor_copy(z_g[:], uz[:, bass.ds(i * 2 + half + 4, 1)])
                    g.tensor_copy(scale_g[:], vec_t[:, bass.ds(i * 8 + 4 * half + V_SCALE, 4)]).then_inc(uz_copied, 1)

        @block.scalar
        def _(act):
            a = nc.scalar

            def ahead(first, kt, last=False):
                if last and kt >= KT - LEAD:
                    return
                slot = (kt + LEAD) % RING
                act.wait_ge(weights_free, first + (kt + LEAD + 1))
                act.wait_ge(raw_landed[slot], first * 4 + ((kt + LEAD) // RING * 16 + 16))
                a.activation(w_hi[:, slot, :], raw[:, slot, :], ACT.Copy).then_inc(hi_done, 1)

            act.wait_ge(vec_ready, 1)
            for b in range(KT // 2):
                act.wait_ge(x_psum, b + 1)
                for e in range(2):
                    k = a.activation(act_hi[:, 2 * b + e, :], ps[:, b % 8, e * T:(e + 1) * T], ACT.Copy,
                                     scale=vec_t[:, V_NORM + 2 * b + e:V_NORM + 2 * b + e + 1])
                k.then_inc(xt_hi, 1)
            for c in range(LEAD):
                act.wait_ge(raw_landed[c], 16)
                a.activation(w_hi[:, c, :], raw[:, c, :], ACT.Copy).then_inc(hi_done, 1)
            act.wait_ge(xt_lo, KT // 2)
            a.activation(x_tok[:, 0, :], x_tok[:, 0, :], ACT.Square, accum_out=row_ss[:, 0:1]).then_inc(sq_act, 1)
            act.wait_ge(rstd_ready, 1)

            def leave(q, dst):
                act.wait_ge(acc_done, q + 1)
                a.activation(dst, ps[:, 0:NH, :], ACT.Copy, scale=rstd[:, 0:1]).then_inc(acc_free[0], 1)

            with act.Fori(0, N_A - 1) as i:
                for kt in range(KT):
                    ahead(i * KT, kt)
                leave(i, kvq[:, bass.ds(i * 2, 2), 0, :])

            base = (N_A - 1) * KT
            for kt in range(KT):
                if kt == 0:
                    act.wait_ge(wg_landed, 16)
                    a.activation(wg_hi[:], wg[:], ACT.Copy).then_inc(wg_hi_done, 1)
                ahead(base, kt)
                if kt in (2, 6):
                    n = (kt - 2) // 4
                    kb = (kb_k, kb_v)[n]
                    act.wait_ge(ct_psum, n + 1)
                    act.wait_ge(kb_pos, n + 1)
                    for half in range(2):
                        k = a.activation(
                            kb[:, :, 2 * half:2 * half + 2, :].rearrange("p r h c -> p h c r"),
                            ps[:, 6 + half, :].rearrange("p (h c r) -> p h c r", h=2, r=CMP_STRIDE), ACT.Copy)
                    k.then_inc(ct_sbuf, 1)
                if kt == 22:
                    act.wait_ge(hid_step, 4)
                    a.activation(hid_s[:], hid_x[:], ACT.Sigmoid).then_inc(hid_sig, 1)
                if kt == 24:
                    act.wait_ge(w2_psum, 1)
                    a.activation(vc[:], ps[0:NC, 7, :].rearrange("p (h d) -> p h d", h=KVH), ACT.Copy).then_inc(vc_ready, 1)
            leave(N_A - 1, kvq[:, 2 * (N_A - 1):2 * N_A, 0, :])
            act.wait_ge(gate_psum, 1)
            for t in range(TT):
                lin = ps[:, 4 + t, 0:GATES].rearrange("p (h b) -> p h b", b=NBR)
                a.activation(gate6[:, :, 2 * t:2 * t + 2], lin[:, :, 1:3], ACT.Sigmoid, scale=rstd[:, t:t + 1])
                k = a.activation(gate6[:, :, 4 + t], lin[:, :, 0], ACT.Sigmoid, scale=rstd[:, t:t + 1])
            k.then_inc(gate_sig, 1)
            act.wait_ge(acc_free[1], 1 + N_A)

            with act.Fori(0, KVH) as j:
                for kt in range(KT):
                    ahead(j * KT + CH_L2, kt)
                    if kt == 0:
                        act.wait_ge(head_out, j * GQ + 1)
                        a.activation(qk[:, :, 0:GQ, :], kvq[:, bass.ds(j + 6, 1), :, :], ACT.Square)
                        for m, src in ((4, 2), (5, 4)):
                            k = a.activation(qk[:, :, m, :], kvq[:, src, :, bass.ds(j * HD, HD)], ACT.Square)
                        k.then_inc(qk_sq, 1)
                    if kt == 3:
                        act.wait_ge(qkt_psum, j + 1)
                        a.activation(qk_t[:, 4, :], ps[:, 6, 0:T], ACT.Copy, scale=vec_t[:, V_KG + 1:V_KG + 2])
                        a.activation(qk_t[:, 5, :], ps[:, 6, T:2 * T], ACT.Copy,
                                     scale=vec_t[:, V_KG + 2:V_KG + 3]).then_inc(qkt_act, 1)
                    if kt >= 6 and (kt - 6) % 7 == 0 and (kt - 6) // 7 < GQ:
                        h = (kt - 6) // 7
                        act.wait_ge(head_max, j * GQ + (h + 1))
                        for br in range(2):
                            a.activation(s[:, br, 0:P], s[:, br, 0:P], ACT.Exp, bias=neg_max[:, br:br + 1],
                                         accum_out=sums[:, br:br + 1])
                            a.activation(s[:, br, P:3 * P], s[:, br, P:3 * P], ACT.Exp, bias=neg_max[:, 2 + br:3 + br],
                                         accum_out=sums[:, 2 + br:3 + br])
                        for t in range(TT):
                            k = a.activation(s_cmp[:, t, :], s_cmp[:, t, :], ACT.Exp, bias=neg_max[:, 4 + t:5 + t],
                                             accum_out=sums[:, 4 + t:5 + t])
                        k.then_inc(exp_done, 1)
                    if kt >= 8 and (kt - 8) % 7 == 0 and (kt - 8) // 7 < GQ:
                        h = (kt - 8) // 7
                        act.wait_ge(probt_psum, j * GQ + (h + 1))
                        a.activation(prob_t[:], ps[:, 6:8, 0:3 * P], ACT.Copy)
                        a.activation(prob_ct[:], ps[0:NC, 6:8, 3 * P:4 * P], ACT.Copy).then_inc(probt_ready, 1)
                leave(j + Q_L2, uz[:, bass.ds(j * 2, 2), 0, :])

            def pool_group(kt, n):
                if kt == 9:
                    act.wait_ge(mix_psum, n + 1)
                    a.activation(mix_t[:, 0:2, :], ps[:, 4, :], ACT.Copy).then_inc(mix_act, 1)
                    act.wait_ge(zt_psum, n + 1)
                    for half in range(2):
                        a.activation(silu_zt[:, 2 * half:2 * half + 2, :], ps[:, 6 + half, :],
                                     ACT.Sigmoid).then_inc(zt_sig, 1)
                if kt in (13, 15):
                    b = (kt - 13) // 2
                    act.wait_ge(pool_v, n * 2 + (b + 1))
                    a.activation(pool_hi[:, bass.ds(n * 4 + 2 * b, 2), :], silu_zt[:, 2 * b:2 * b + 2, :],
                                 ACT.Copy).then_inc(pool_hi_done, 1)

            with act.Fori(0, 2) as i:
                for kt in range(KT):
                    ahead(i * 2 * KT + CH_TL, kt)
                    pool_group(kt, i * 2)
                for t in range(TT):
                    if t == 0:
                        act.wait_ge(acc_done, i * 2 + (Q_TL + 1))
                    else:
                        act.wait_ge(weights_free, i * 2 * KT + (CH_TL + KT + RING))
                    a.activation(n_tok[:, t, :], ps[:, NH * t:NH * t + NH, :], ACT.Sigmoid,
                                 scale=rstd[:, t:t + 1]).then_inc(nz_sig, 1)
                for kt in range(KT):
                    ahead(i * 2 * KT + CH_TL + KT, kt)
                    if kt in (1, 3, 5, 7):
                        b = kt // 2
                        act.wait_ge(nt_psum, i * 4 + (b + 1))
                        a.activation(nsa_hi[:, bass.ds(i * 8 + 2 * b, 2), :], ps[:, 6 + b % 2, :],
                                     ACT.Copy).then_inc(nt_hi, 1)
                    pool_group(kt, i * 2 + 1)
                for t in range(TT):
                    act.wait_ge(acc_free[t], i * 2 + (Q_TL + 3))
                    y = ys[:, bass.ds(i * -1 + 1, 1), t, :]
                    a.activation(y, y, ACT.Sigmoid).then_inc(gate_out, 1)

            with act.Fori(0, N_Y - 1) as i:
                for kt in range(2 * UT):
                    ahead(i * PER3 + CH_P3, kt)
                for which in range(2):
                    for kt in range(KT):
                        ahead(i * PER3 + CH_P3 + 2 * UT + which * KT, kt)
                    for t in range(TT):
                        act.wait_ge(acc_free[t], i * 4 + (Q_P3 + 4 + which))
                        y = ys[:, bass.ds(i + 2, 1), t, :] if which == 0 else ys[:, 0, t, :]
                        a.activation(y, y, ACT.Sigmoid).then_inc(gate_out, 1)

            def turn_y(b):
                act.wait_ge(yt_psum, b + 1)
                a.activation(act_hi[:, 2 * b:2 * b + 2, :], ps[:, 4 + b % 4, :], ACT.Copy).then_inc(yt_hi, 1)

            for kt in range(2 * UT):
                ahead(CH_EP, kt)
                if kt % 2 == 1 and kt // 2 < 12:
                    turn_y(kt // 2)
            for b in range(12, 16):
                turn_y(b)

            with act.Fori(0, N_Y - 1) as i:
                for kt in range(KT):
                    ahead(i * KT + CH_P4, kt)
                for t in range(TT):
                    act.wait_ge(acc_free[t], i + (Q_P4 + 2))
                act.dma_start(out_pt[:, :, bass.ds(i * WIDTH, WIDTH)], x_out[:, bass.ds(i, 1), :, :]).then_inc(
                    out_stored, 16)
            for kt in range(KT):
                ahead(CH_P4 + (N_Y - 1) * KT, kt, last=True)
            for t in range(TT):
                act.wait_ge(acc_free[t], Q_P4 + N_Y + 1)
                act.dma_start(out_pt[:, t:t + 1, (N_Y - 1) * WIDTH:], x_out[:, N_Y - 1, t:t + 1, :]).then_inc(
                    out_stored, 16)
            act.wait_ge(out_stored, 16 * (N_Y + 1))

        @block.vector
        def _(dve):
            v = nc.vector
            dve.sem_inc(split_done, RING)
            dve.sem_inc(acc_free[0], 1)
            dve.sem_inc(acc_free[1], 1)
            dve.sem_inc(head_out, 1)
            dve.sem_inc(nt_lo, 2)
            dve.sem_inc(pool_lo_done, 2)

            def split(chunk, slot):
                dve.wait_ge(hi_done, chunk)
                v.tensor_tensor(w_lo[:, slot, :], raw[:, slot, :], up(w_hi[:, slot, :]), ALU.subtract).then_inc(
                    split_done, 1)

            def ahead(first, kt, last=False):
                if last and kt >= KT - LEAD:
                    return
                split(first + (kt + LEAD + 1), (kt + LEAD) % RING)

            dve.wait_ge(vec_psum, 1)
            v.tensor_copy(vec_t[:, 0:V_END], ps[:, 7, 0:V_END]).then_inc(vec_ready, 1)
            dve.wait_ge(vec_ready, 1)
            for b in range(KT // 2):
                dve.wait_ge(xt_hi, b + 1)
                for e in range(2):
                    kt = 2 * b + e
                    k = v.scalar_tensor_tensor(act_lo[:, kt, :], ps[:, b % 8, e * T:(e + 1) * T],
                                               vec_t[:, V_NORM + kt:V_NORM + kt + 1], up(act_hi[:, kt, :]),
                                               ALU.mult, ALU.subtract)
                k.then_inc(xt_lo, 1)
            for c in range(LEAD):
                split(c + 1, c)
            v.tensor_tensor_reduce(out=x_tok[:, 1, :], in0=x_tok[:, 1, :], in1=x_tok[:, 1, :], scale=1.0, scalar=0.0,
                                   op0=ALU.mult, op1=ALU.add, accum_out=row_ss[:, 1:2]).then_inc(sq_dve, 1)
            dve.wait_ge(sq_act, 1)
            dve.wait_ge(sq_dve, 1)
            v.tensor_scalar(row_ss[:], row_ss[:], 1.0 / D, EPS, ALU.mult, ALU.add).then_inc(row_ms, 1)
            dve.wait_ge(rstd_ready, 1)

            def leave(last_chunk, dst):
                dve.wait_ge(weights_free, last_chunk + RING)
                v.tensor_scalar(dst, ps[:, NH:2 * NH, :], rstd[:, 1:2], None, ALU.mult).then_inc(acc_free[1], 1)

            with dve.Fori(0, N_A - 1) as i:
                for kt in range(KT):
                    ahead(i * KT, kt)
                leave(i * KT + KT, kvq[:, bass.ds(i * 2, 2), 1, :])

            base = (N_A - 1) * KT
            for kt in range(KT):
                if kt == 0:
                    dve.wait_ge(wg_hi_done, 1)
                    v.tensor_tensor(wg_lo[:], wg[:], up(wg_hi[:]), ALU.subtract).then_inc(wg_lo_done, 1)
                    dve.wait_ge(wg_lo_done, 1)
                    for n, kb in enumerate((kb_k, kb_v)):
                        v.memset(kb[:, :, KVH, :], 0.0).then_inc(kb_zero, 1)
                        dve.wait_ge(kb_zero, n + 1)
                        v.tensor_copy(kb[:, :, KVH, 0], vec_t[:, V_PE + n * CMP_BLOCK:V_PE + n * CMP_BLOCK + CMP_STRIDE])
                        v.tensor_copy(kb[:, :, KVH, CMP_STRIDE - 1],
                                      vec_t[:, V_PE + n * CMP_BLOCK + CMP_STRIDE:V_PE + (n + 1) * CMP_BLOCK]).then_inc(
                            kb_pos, 1)
                ahead(base, kt)
                if kt == 21:
                    dve.wait_ge(hid_psum, 1)
                    for n in range(2):
                        first, second = KVH * NC, (KVH + 1) * NC - 1
                        v.tensor_tensor(hid_b[:, n:n + 1], vec_t[:, V_B1 + n:V_B1 + n + 1], ps[:, 6 + n, first:first + 1],
                                        ALU.add).then_inc(hid_step, 1)
                        dve.wait_ge(hid_step, 2 * n + 1)
                        v.tensor_scalar(hid_x[:, n, :], ps[:, 6 + n, 0:KVH * NC], hid_b[:, n:n + 1],
                                        ps[:, 6 + n, second:second + 1], ALU.add, ALU.add).then_inc(hid_step, 1)
                if kt == 22:
                    dve.wait_ge(hid_sig, 1)
                    v.tensor_tensor(hid[:], hid_x[:], hid_s[:], ALU.mult).then_inc(hid_step, 1)
                if kt == 24:
                    dve.wait_ge(w2_psum, 1)
                    v.tensor_copy(kc_n[:], ps[0:KVH * NC, 6, 128:256]).then_inc(kc_step, 1)
                    dve.wait_ge(kc_step, 1)
                    v.tensor_tensor_reduce(out=kc_sq[:], in0=kc_n[:], in1=kc_n[:], scale=1.0, scalar=0.0,
                                           op0=ALU.mult, op1=ALU.add, accum_out=kc_ss[:]).then_inc(kc_step, 1)
                    dve.wait_ge(kc_step, 2)
                    v.tensor_scalar(kc_ss[:], kc_ss[:], 1.0 / HD, EPS, ALU.mult, ALU.add).then_inc(kc_step, 1)
                if kt == 25:
                    dve.wait_ge(kc_rstd, 1)
                    v.tensor_scalar(kc_n[:], kc_n[:], kc_rs[:], None, ALU.mult).then_inc(kc_step, 1)
                if kt == 27:
                    dve.wait_ge(kct_psum, 1)
                    v.tensor_scalar(kc_t[:], ps[:, 6, 0:KVH * NC], vec_t[:, V_KG:V_KG + 1], None, ALU.mult).then_inc(
                        kct_ready, 1)
            leave(N_A * KT, kvq[:, 2 * (N_A - 1):2 * N_A, 1, :])
            dve.wait_ge(gate_sig, 1)
            v.tensor_scalar(gate6[:, :, 4], gate6[:, :, 4], row_mask[:], None, ALU.mult).then_inc(gate_ready, 1)
            v.tensor_scalar(vec_t[:, V_QG:V_QG + 1], vec_t[:, V_QG:V_QG + 1], HD ** -0.5, None, ALU.mult).then_inc(
                gate_ready, 1)
            dve.wait_ge(gate_ready, 2)
            dve.wait_ge(acc_free[0], 1 + N_A)
            dve.wait_ge(const_ready, 5)

            with dve.Fori(0, KVH) as j:
                for kt in range(KT):
                    ahead(j * KT + CH_L2, kt)
                    if kt == 0:
                        dve.wait_ge(qk_sq, j + 1)
                        v.reduce_sum(stat_ss[:], qk[:].rearrange("p t m d -> p (t m) d"), AX.X).then_inc(qk_ss, 1)
                        dve.wait_ge(qk_ss, j + 1)
                        v.tensor_scalar(stat_ss[:], stat_ss[:], 1.0 / HD, EPS, ALU.mult, ALU.add).then_inc(qk_ms, 1)
                    if kt == 1:
                        dve.wait_ge(qk_rstd, j + 1)
                        for t in range(TT):
                            v.tensor_tensor(qk[:, t, 0:GQ, :], kvq[:, bass.ds(j + 6, 1), t, :].rearrange(
                                "p a (m d) -> p (a m) d", d=HD),
                                stat_rs[:, 6 * t:6 * t + GQ].unsqueeze(2).to_broadcast([P, GQ, HD]), ALU.mult)
                            for m, src in ((4, 2), (5, 4)):
                                k = v.tensor_scalar(qk[:, t, m, :], kvq[:, src, t, bass.ds(j * HD, HD)],
                                                    stat_rs[:, 6 * t + m:6 * t + m + 1], None, ALU.mult)
                        k.then_inc(qk_normed, 1)
                    if kt == 3:
                        dve.wait_ge(qkt_psum, j + 1)
                        v.tensor_scalar(qk_t[:, 0:4, :], ps[:, 4:6, :], vec_t[:, V_QG:V_QG + 1], None,
                                        ALU.mult).then_inc(qkt_dve, 1)
                    if kt >= 5 and (kt - 5) % 7 == 0 and (kt - 5) // 7 < GQ:
                        h = (kt - 5) // 7
                        dve.wait_ge(scores_done, j * GQ + (h + 1))
                        v.tensor_tensor(s[:], ps[:, 4:6, 0:3 * P],
                                        dist[:, h, :].unsqueeze(1).to_broadcast([P, 2, 3 * P]), ALU.add).then_inc(biased, 1)
                        v.tensor_tensor(s_cmp[:], ps[:, 4:6, 3 * P:3 * P + NC], dist_c[:, h], ALU.add).then_inc(biased, 1)
                        dve.wait_ge(biased, j * (2 * GQ) + (2 * h + 2))
                        v.tensor_reduce(neg_max[:, 0:2], s[:, :, 0:P], AX.X, ALU.max, negate=True)
                        v.tensor_reduce(neg_max[:, 2:4], s[:, :, P:3 * P], AX.X, ALU.max, negate=True)
                        v.tensor_reduce(neg_max[:, 4:6], s_cmp[:], AX.X, ALU.max, negate=True).then_inc(head_max, 1)
                    if kt >= 7 and (kt - 7) % 7 == 0 and (kt - 7) // 7 < GQ:
                        h = (kt - 7) // 7
                        dve.wait_ge(exp_done, j * GQ + (h + 1))
                        v.reciprocal(inv[:], sums[:]).then_inc(inv_done, 1)
                        dve.wait_ge(inv_done, j * GQ + (h + 1))
                        v.tensor_tensor(wgt[:], inv[:], gate6[:, bass.ds(j * GQ + h, 1), :], ALU.mult).then_inc(
                            wgt_done, 1)
                        dve.wait_ge(wgt_done, j * GQ + (h + 1))
                        for br in range(2):
                            v.tensor_scalar(s[:, br, 0:P], s[:, br, 0:P], wgt[:, br:br + 1], None, ALU.mult)
                            v.tensor_scalar(s[:, br, P:3 * P], s[:, br, P:3 * P], wgt[:, 2 + br:3 + br], None, ALU.mult)
                        for t in range(TT):
                            k = v.tensor_scalar(s_cmp[:, t, :], s_cmp[:, t, :], wgt[:, 4 + t:5 + t], None, ALU.mult)
                        k.then_inc(probs_ready, 1)
                    if kt >= 10 and (kt - 10) % 7 == 0 and (kt - 10) // 7 < GQ:
                        h = (kt - 10) // 7
                        dve.wait_ge(pv_done, j * GQ + (h + 1))
                        v.tensor_scalar(kvq[:, bass.ds(j + 6, 1), :, h * HD:(h + 1) * HD],
                                        ps[:, 4:6, 3 * P:4 * P], 1.0, None, ALU.mult).then_inc(head_out, 1)
                v.tensor_scalar(dist[:], dist[:], 0.25, None, ALU.mult)
                v.tensor_scalar(dist_c[:], dist_c[:], 0.25, None, ALU.mult).then_inc(dist_scaled, 1)
                leave(j * KT + (CH_L2 + KT), uz[:, bass.ds(j * 2, 2), 1, :])

            def pool_group(kt, n):
                if kt == 9:
                    dve.wait_ge(mix_psum, n + 1)
                    v.tensor_copy(mix_t[:, 2:4, :], ps[:, 5, :]).then_inc(mix_dve, 1)
                if kt == 10:
                    for half in range(2):
                        dve.wait_ge(zt_sig, n * 2 + (half + 1))
                        c = silu_zt[:, 2 * half:2 * half + 2, :]
                        v.tensor_tensor(c, c, ps[:, 6 + half, :], ALU.mult).then_inc(zt_silu, 1)
                if kt in (13, 15):
                    b = (kt - 13) // 2
                    dve.wait_ge(pwt_psum, n * 2 + (b + 1))
                    dve.wait_ge(zt_silu, n * 2 + 2)
                    for e in range(2):
                        dt = 2 * b + e
                        k = v.scalar_tensor_tensor(silu_zt[:, dt, :], ps[:, 4 + b, e * T:(e + 1) * T],
                                                   scale_g[:, dt:dt + 1], silu_zt[:, dt, :], ALU.mult, ALU.mult)
                    k.then_inc(pool_v, 1)
                    dve.wait_ge(pool_hi_done, n * 2 + (b + 1))
                    at_ = bass.ds(n * 4 + 2 * b, 2)
                    v.tensor_tensor(pool_lo[:, at_, :], silu_zt[:, 2 * b:2 * b + 2, :], up(pool_hi[:, at_, :]),
                                    ALU.subtract).then_inc(pool_lo_done, 1)

            def gate_leave(n, chunk_done, q, dst):
                dve.wait_ge(bias_landed, n * 16 + 16)
                for t in range(TT):
                    if t == 0:
                        dve.wait_ge(acc_done, q + 1)
                    else:
                        dve.wait_ge(weights_free, chunk_done + RING)
                    v.scalar_tensor_tensor(dst(t), ps[:, NH * t:NH * t + NH, :].rearrange("p a b -> p (a b)"),
                                           rstd[:, t:t + 1], bias[:], ALU.mult, ALU.add).then_inc(acc_free[t], 1)

            with dve.Fori(0, 2) as i:
                for kt in range(KT):
                    ahead(i * 2 * KT + CH_TL, kt)
                    pool_group(kt, i * 2)
                for t in range(TT):
                    dve.wait_ge(nz_sig, i * 2 + (t + 1))
                    v.scalar_tensor_tensor(n_tok[:, t, :], ps[:, NH * t:NH * t + NH, :].rearrange("p a b -> p (a b)"),
                                           rstd[:, t:t + 1], n_tok[:, t, :], ALU.mult, ALU.mult).then_inc(acc_free[t], 1)
                for t in range(TT):
                    dve.wait_ge(acc_free[t], i * 2 + (Q_TL + 2))
                    k = v.tensor_tensor(n_tok[:, t, :].rearrange("p (a b) -> p a b", a=2),
                                        n_tok[:, t, :].rearrange("p (a b) -> p a b", a=2),
                                        kvq[:, bass.ds(i * 2 + 6, 2), t, :], ALU.mult)
                k.then_inc(n_ready, 1)
                for kt in range(KT):
                    ahead(i * 2 * KT + CH_TL + KT, kt)
                    if kt in (1, 3, 5, 7):
                        b = kt // 2
                        dve.wait_ge(nt_hi, i * 4 + (b + 1))
                        at_ = bass.ds(i * 8 + 2 * b, 2)
                        v.tensor_tensor(nsa_lo[:, at_, :], ps[:, 6 + b % 2, :].rearrange("p (a b) -> p a b", a=2),
                                        up(nsa_hi[:, at_, :]), ALU.subtract).then_inc(nt_lo, 1)
                    pool_group(kt, i * 2 + 1)
                gate_leave(i, i * 2 * KT + (CH_TL + 2 * KT), i * 2 + (Q_TL + 1), lambda t: ys[:, bass.ds(i * -1 + 1, 1), t, :])

            def times(y, t):
                return v.tensor_tensor(y, y, ps[:, NH * t:NH * t + NH, :].rearrange("p a b -> p (a b)"), ALU.mult)

            def pool_leave(chunk_done, q, n, y):
                dve.wait_ge(gate_out, n * 4 + 4)
                dve.wait_ge(acc_done, q + 1)
                times(y(0), 0).then_inc(acc_free[0], 1)
                dve.wait_ge(weights_free, chunk_done + RING)
                times(y(1), 1).then_inc(acc_free[1], 1)

            def nsa_leave(chunk_done, q, y):
                dve.wait_ge(acc_done, q + 1)
                times(ys[:, 0, 0, :], 0).then_inc(acc_free[0], 1)
                dve.wait_ge(weights_free, chunk_done + RING)
                times(ys[:, 0, 1, :], 1).then_inc(acc_free[1], 1)
                for t in range(TT):
                    dve.wait_ge(acc_free[t], q + 2)
                    k = v.tensor_tensor(y(t), y(t), ys[:, 0, t, :], ALU.add)
                k.then_inc(y_sum, 1)

            with dve.Fori(0, N_Y - 1) as i:
                for kt in range(UT):
                    ahead(i * PER3 + CH_P3, kt)
                y = lambda t: ys[:, bass.ds(i + 1, 1), t, :]
                pool_leave(i * PER3 + (CH_P3 + UT), i * 4 + Q_P3, i, y)
                for kt in range(UT):
                    ahead(i * PER3 + CH_P3 + UT, kt)
                nsa_leave(i * PER3 + (CH_P3 + 2 * UT), i * 4 + (Q_P3 + 1), y)
                for which in range(2):
                    for kt in range(KT):
                        ahead(i * PER3 + CH_P3 + 2 * UT + which * KT, kt)
                    gate_leave(i * 2 + (2 + which), i * PER3 + (CH_P3 + 2 * UT + (which + 1) * KT),
                               i * 4 + (Q_P3 + 2 + which),
                               (lambda t: ys[:, bass.ds(i + 2, 1), t, :]) if which == 0 else (lambda t: ys[:, 0, t, :]))

            def turn_y(b):
                dve.wait_ge(yt_hi, b + 1)
                v.tensor_tensor(act_lo[:, 2 * b:2 * b + 2, :], ps[:, 4 + b % 4, :].rearrange("p (a b) -> p a b", a=2),
                                up(act_hi[:, 2 * b:2 * b + 2, :]), ALU.subtract).then_inc(yt_lo, 1)

            y_last = lambda t: ys[:, N_Y, t, :]
            for kt in range(2 * UT):
                ahead(CH_EP, kt)
                if kt % 2 == 1 and kt // 2 < 12:
                    turn_y(kt // 2)
                if kt == UT - 1:
                    pool_leave(CH_EP + UT, Q_EP, N_Y - 1, y_last)
            nsa_leave(CH_EP + 2 * UT, Q_EP + 1, y_last)
            for b in range(12, 16):
                turn_y(b)

            dve.wait_ge(xo_landed, 16 * N_Y)

            def out_leave(q, chunk_done, xo):
                for t in range(TT):
                    if t == 0:
                        dve.wait_ge(acc_done, q + 1)
                    else:
                        dve.wait_ge(weights_free, chunk_done + RING)
                    v.tensor_tensor(xo(t), xo(t), ps[:, NH * t:NH * t + NH, :].rearrange("p a b -> p (a b)"),
                                    ALU.add).then_inc(acc_free[t], 1)

            with dve.Fori(0, N_Y - 1) as i:
                for kt in range(KT):
                    ahead(i * KT + CH_P4, kt)
                out_leave(i + Q_P4, i * KT + (CH_P4 + KT), lambda t: x_out[:, bass.ds(i, 1), t, :])
            for kt in range(KT):
                ahead(CH_P4 + (N_Y - 1) * KT, kt, last=True)
            out_leave(Q_P4 + N_Y - 1, CHUNKS, lambda t: x_out[:, N_Y - 1, t, :])

        @block.tensor
        def _(pe):
            pe.sem_inc(weights_free, RING)
            mm, tr = nc.tensor.matmul, nc.tensor.transpose

            def product(first, q, hi, lo, side=None, tiles=None):
                tiles = tiles or hi.shape[1]
                for kt in range(tiles):
                    slot = kt % RING
                    pe.wait_ge(split_done, first + (kt + 1 + RING))
                    for t in range(TT):
                        if kt == 0:
                            pe.wait_ge(acc_free[t], q + 1)
                        for part, (a_, w_) in enumerate(((hi, w_hi), (hi, w_lo), (lo, w_hi))):
                            for n in range(NH):
                                m = mm(ps[:, NH * t + n, :], a_[:, kt, t * P:(t + 1) * P],
                                       w_[:, slot, n * BANK:(n + 1) * BANK],
                                       start=(kt == 0 and part == 0), stop=(kt == tiles - 1 and part == 2))
                        if kt == tiles - 1 and t == 0:
                            m.then_inc(acc_done, 1)
                    m.then_inc(weights_free, 1)
                    if side:
                        side(kt)

            pe.wait_ge(const_ready, 1)
            pe.wait_ge(vec_landed, 16 * 6)
            tr(ps[:, 7, 0:V_END], vec_rows[0:V_END, :], ident[0:V_END, 0:V_END]).then_inc(vec_psum, 1)
            pe.wait_ge(vec_ready, 1)
            for b in range(KT // 2):
                if b % 4 == 0:
                    pe.wait_ge(x_landed[b // 4], 16)
                if b >= 8:
                    pe.wait_ge(xt_lo, b - 7)
                for e in range(2):
                    for t in range(TT):
                        k = tr(ps[:, b % 8, (2 * e + t) * P:(2 * e + t + 1) * P],
                               x_tok[:, t, (2 * b + e) * P:(2 * b + e + 1) * P], ident[:])
                k.then_inc(x_psum, 1)
            pe.wait_ge(xt_lo, KT // 2)
            with pe.Fori(0, N_A - 1) as i:
                product(i * KT, i, act_hi, act_lo)

            def gates_and_compression(kt):
                if kt == 0:
                    pe.wait_ge(wg_lo_done, 1)
                for t in range(TT):
                    for part, (a_, w_) in enumerate(((act_hi, wg_hi), (act_hi, wg_lo), (act_lo, wg_hi))):
                        k = mm(ps[:, 4 + t, 0:GATES], a_[:, kt, t * P:(t + 1) * P], w_[:, kt, :],
                               start=(kt == 0 and part == 0), stop=(kt == KT - 1 and part == 2))
                if kt == KT - 1:
                    k.then_inc(gate_psum, 1)
                if kt in (2, 6):
                    n = (kt - 2) // 4
                    if n == 0:
                        pe.wait_ge(acc_free[0], 1 + 1)
                        pe.wait_ge(acc_free[1], 1 + 1)
                    else:
                        pe.wait_ge(ct_sbuf, 1)
                    for h in range(KVH):
                        for t in range(TT):
                            k = tr(ps[:, 6 + h // 2, ((h % 2) * TT + t) * P:((h % 2) * TT + t + 1) * P],
                                   kvq[:, n, t, h * HD:(h + 1) * HD], ident[:])
                    k.then_inc(ct_psum, 1)
                if 10 <= kt < 20:
                    if kt == 10:
                        pe.wait_ge(ct_sbuf, 2)
                        pe.wait_ge(w1_landed, 48)
                    js = range((kt - 10) * 16 // 5, (kt - 9) * 16 // 5)
                    for j in js:
                        late = j // CMP_STRIDE
                        for n, kb in enumerate((kb_k, kb_v)):
                            k = mm(ps[:, 6 + n, 0:(KVH + 1) * NC], w1[:, n, j, :],
                                   kb[:, j % CMP_STRIDE, :, late:late + NC],
                                   start=(j == 0), stop=(j == CMP_BLOCK - 1))
                    if kt == 19:
                        k.then_inc(hid_psum, 1)
                if kt == 24:
                    pe.wait_ge(hid_step, 5)
                    mm(ps[0:KVH * NC, 6, 128:256], hid[:, 0, :], w2[:, 0, :], start=True, stop=True)
                    for h in range(KVH):
                        k = mm(ps[0:NC, 7, h * HD:(h + 1) * HD], hid[:, 1, h * NC:(h + 1) * NC], w2[:, 1, :],
                               start=True, stop=True)
                    k.then_inc(w2_psum, 1)
                if kt == 27:
                    pe.wait_ge(kc_step, 4)
                    tr(ps[:, 6, 0:KVH * NC], kc_n[:], ident[0:KVH * NC, 0:KVH * NC]).then_inc(kct_psum, 1)

            product((N_A - 1) * KT, N_A - 1, act_hi, act_lo, gates_and_compression)
            pe.wait_ge(kct_ready, 1)
            pe.wait_ge(vc_ready, 1)
            pe.wait_ge(gate_ready, 2)

            with pe.Fori(0, KVH) as j:
                def attention(kt):
                    if kt == 3:
                        pe.wait_ge(qk_normed, j + 1)
                        pe.wait_ge(head_out, j * GQ + 1)
                        for m in range(6):
                            for t in range(TT):
                                k = tr(ps[:, 4 + m // 2, ((m % 2) * TT + t) * P:((m % 2) * TT + t + 1) * P],
                                       qk[:, t, m, :], ident[:])
                        k.then_inc(qkt_psum, 1)
                    if kt >= 5 and (kt - 5) % 7 == 0 and (kt - 5) // 7 < GQ:
                        h = (kt - 5) // 7
                        if h == 0:
                            pe.wait_ge(qkt_act, j + 1)
                            pe.wait_ge(qkt_dve, j + 1)
                        pe.wait_ge(head_out, j * GQ + (h + 1))
                        for br in range(2):
                            mm(ps[:, 4 + br, 0:P], qk_t[:, h, 0:P], qk_t[:, 4 + br, 0:P], start=True, stop=True)
                            mm(ps[:, 4 + br, P:3 * P], qk_t[:, h, P:2 * P], qk_t[:, 4 + br, :], start=True, stop=True)
                        for t in range(TT):
                            k = mm(ps[:, 4 + t, 3 * P:3 * P + NC], qk_t[:, h, t * P:(t + 1) * P],
                                   kc_t[:, bass.ds(j * NC, NC)], start=True, stop=True)
                        k.then_inc(scores_done, 1)
                    if kt >= 8 and (kt - 8) % 7 == 0 and (kt - 8) // 7 < GQ:
                        h = (kt - 8) // 7
                        pe.wait_ge(probs_ready, j * GQ + (h + 1))
                        for br in range(2):
                            for b in range(3):
                                tr(ps[:, 6 + br, b * P:(b + 1) * P], s[:, br, b * P:(b + 1) * P], ident[:])
                        for t in range(TT):
                            k = tr(ps[0:NC, 6 + t, 3 * P:4 * P], s_cmp[:, t, :], ident[:])
                        k.then_inc(probt_psum, 1)
                    if kt >= 10 and (kt - 10) % 7 == 0 and (kt - 10) // 7 < GQ:
                        h = (kt - 10) // 7
                        pe.wait_ge(probt_ready, j * GQ + (h + 1))
                        vals = lambda half, t: kvq[:, half, t, bass.ds(j * HD, HD)]
                        for t in range(TT):
                            o = ps[:, 4 + t, 3 * P:4 * P]
                            first = True
                            for br, half in ((0, 3), (1, 5)):
                                for kb in range(t + 1):
                                    mm(o, prob_t[:, br, (t + kb) * P:(t + kb + 1) * P], vals(half, kb),
                                       start=first, stop=False)
                                    first = False
                            k = mm(o, prob_ct[:, t, :], vc[:, bass.ds(j, 1), :], start=False, stop=True)
                        k.then_inc(pv_done, 1)

                product(j * KT + CH_L2, j + Q_L2, act_hi, act_lo, attention)

            def pool_group(kt, n):
                if kt == 9:
                    pe.wait_ge(uz_copied, n + 1)
                    for c in range(PG // P):
                        o = ps[:, 4 + c // 2, (c % 2) * T:(c % 2 + 1) * T]
                        mm(o[:, 0:P], u_g[:, 0, c * P:(c + 1) * P], band[:, bass.ds(n, 1), 0:P], start=True, stop=True)
                        mm(o[:, P:2 * P], u_g[:, 0, c * P:(c + 1) * P], band[:, bass.ds(n, 1), P:2 * P],
                           start=True, stop=False)
                        k = mm(o[:, P:2 * P], u_g[:, 1, c * P:(c + 1) * P], band[:, bass.ds(n, 1), 2 * P:3 * P],
                               start=False, stop=True)
                    k.then_inc(mix_psum, 1)
                    for c in range(PG // P):
                        for t in range(TT):
                            k = tr(ps[:, 6 + c // 2, ((c % 2) * TT + t) * P:((c % 2) * TT + t + 1) * P],
                                   z_g[:, t, c * P:(c + 1) * P], ident[:])
                    k.then_inc(zt_psum, 1)
                if 12 <= kt < 16:
                    d = kt - 12
                    if d == 0:
                        pe.wait_ge(mix_act, n + 1)
                        pe.wait_ge(mix_dve, n + 1)
                        pe.wait_ge(pw_landed, n * 16 + 16)
                    for c in range(PG // P):
                        k = mm(ps[:, 4 + d // 2, (d % 2) * T:(d % 2 + 1) * T], pw[:, c, d * P:(d + 1) * P],
                               mix_t[:, c, :], start=(c == 0), stop=(c == PG // P - 1))
                    if d % 2:
                        k.then_inc(pwt_psum, 1)

            pe.wait_ge(band_built, 4 + sum(w - 1 for w in WINDOWS) + 24)
            with pe.Fori(0, 2) as i:
                product(i * 2 * KT + CH_TL, i * 2 + Q_TL, act_hi, act_lo, lambda kt: pool_group(kt, i * 2))

                def turn_and_pool(kt):
                    if kt in (1, 3, 5, 7):
                        b = kt // 2
                        if b == 0:
                            pe.wait_ge(n_ready, i + 1)
                            pe.wait_ge(pool_lo_done, i * 4 + 4)
                        pe.wait_ge(nt_lo, i * 4 + (b + 1))
                        for e in range(2):
                            for t in range(TT):
                                k = tr(ps[:, 6 + b % 2, (2 * e + t) * P:(2 * e + t + 1) * P],
                                       n_tok[:, t, (2 * b + e) * P:(2 * b + e + 1) * P], ident[:])
                        k.then_inc(nt_psum, 1)
                    if kt == 9:
                        pe.wait_ge(nt_lo, i * 4 + 6)
                    pool_group(kt, i * 2 + 1)

                product(i * 2 * KT + CH_TL + KT, i * 2 + (Q_TL + 1), act_hi, act_lo, turn_and_pool)

            pe.wait_ge(pool_lo_done, 2 + 8)
            pe.wait_ge(nt_lo, 2 + 8)
            with pe.Fori(0, N_Y - 1) as i:
                product(i * PER3 + CH_P3, i * 4 + Q_P3, pool_hi, pool_lo)
                product(i * PER3 + (CH_P3 + UT), i * 4 + (Q_P3 + 1), nsa_hi, nsa_lo)
                for which in range(2):
                    product(i * PER3 + (CH_P3 + 2 * UT + which * KT), i * 4 + (Q_P3 + 2 + which), act_hi, act_lo)

            def turn_y(b):
                g, e0 = b // 4, 2 * (b % 4)
                if b >= 4:
                    pe.wait_ge(yt_lo, b - 3)
                for e in range(2):
                    for t in range(TT):
                        k = tr(ps[:, 4 + b % 4, (2 * e + t) * P:(2 * e + t + 1) * P],
                               ys[:, 1 + g, t, (e0 + e) * P:(e0 + e + 1) * P], ident[:])
                k.then_inc(yt_psum, 1)

            def turn_from(start):
                def side(kt):
                    if (kt + start) % 2 == 1 and (kt + start) // 2 < 12:
                        if kt + start == 1:
                            pe.wait_ge(y_sum, N_Y - 1)
                        turn_y((kt + start) // 2)
                return side

            product(CH_EP, Q_EP, pool_hi, pool_lo, turn_from(0))
            product(CH_EP + UT, Q_EP + 1, nsa_hi, nsa_lo, turn_from(UT))
            pe.wait_ge(y_sum, N_Y)
            for b in range(12, 16):
                turn_y(b)
            pe.wait_ge(yt_lo, 16)
            with pe.Fori(0, N_Y) as i:
                product(i * KT + CH_P4, i + Q_P4, act_hi, act_lo)


_INS = ["x", "norm_g", "w_in", "merge_bias", "pool_w", "pool_scale", "q_norm_g", "k_norm_g", "cmp_pe", "cmp_w1",
        "cmp_b1", "cmp_w2", "w_pool_up", "w_nsa_up", "w_out"]


def kernel(**inputs):
    import numpy as np
    from concourse import bacc
    from concourse.bass_utils import run_bass_kernel_spmd

    nc = bacc.Bacc("TRN2", target_bir_lowering=False, num_devices=1, dynamic_dma_scratch_size=1024)
    arrays, args = {}, []
    for name in _INS:
        a = np.ascontiguousarray(inputs[name])
        arrays[f"in_{name}"] = a
        args.append(nc.dram_tensor(f"in_{name}", a.shape, mybir.dt.from_np(a.dtype), kind="ExternalInput").ap())
    out = nc.dram_tensor("out_y", inputs["x"].shape, F32, kind="ExternalOutput").ap()
    trunk(nc, *args, out)
    r = run_bass_kernel_spmd(nc, [arrays], core_ids=[0])
    return r.results[0]["out_y"]
```

```python
import math

import concourse.bass as bass
from concourse import mybir
from concourse.alu_op_type import AluOpType as ALU

ACT = mybir.ActivationFunctionType
AX = mybir.AxisListType
F32 = mybir.dt.float32
F32R = mybir.dt.float32r

P = 128
BANK = 512
WIDTH = 1024
RING = 4
LEAD = 2
EPS = 1e-6
MASKED = -1e36
WINDOWS = (2, 4, 8, 16)
CMP_BLOCK, CMP_STRIDE = 32, 16


def trunk(nc, x, norm_g, w_in, merge_bias, pool_w, pool_scale, q_norm_g, k_norm_g, cmp_pe, cmp_w1,
          cmp_b1, cmp_w2, w_pool_up, w_nsa_up, w_out, out):
    _, T, D = x.shape
    HD = q_norm_g.shape[1]
    TT = T // P
    KT = D // P
    POOL = pool_scale.shape[1]
    PG = POOL // len(WINDOWS)
    QW = w_nsa_up.shape[1]
    H = QW // HD
    KVH = H // 4
    GQ = H // KVH
    KVW = KVH * HD
    NBR = 3
    NC = (T - CMP_BLOCK) // CMP_STRIDE + 1
    UT = POOL // P
    NH = WIDTH // BANK
    GATES = NBR * H
    assert (T, D, HD, KVH, PG, QW, KVW) == (256, 4096, 128, 4, 512, 2048, 512)

    COL_U, COL_Z = 0, POOL
    COL_Q = 2 * POOL
    COL_NZ = COL_Q + QW
    COL_KV = COL_NZ + QW
    COL_G = COL_KV + 6 * KVW
    COL_M = COL_G + GATES
    assert COL_Z == 2 * WIDTH

    N_A = 5
    CH_L2 = N_A * KT
    CH_TL = CH_L2 + KVH * KT
    CH_P3 = CH_TL + 4 * KT
    PER3 = 2 * UT + 2 * KT
    N_Y = D // WIDTH
    CH_EP = CH_P3 + (N_Y - 1) * PER3
    CH_P4 = CH_EP + 2 * UT
    CHUNKS = CH_P4 + N_Y * KT
    Q_L2, Q_TL, Q_P3 = N_A, N_A + KVH, N_A + KVH + 4
    Q_EP = Q_P3 + 4 * (N_Y - 1)
    Q_P4 = Q_EP + 2

    w_in, w_pu, w_nu, w_o = w_in[0], w_pool_up[0], w_nsa_up[0], w_out[0]
    x_pt = x[0].rearrange("(t p) c -> p t c", p=P)
    out_pt = out[0].rearrange("(t p) c -> p t c", p=P)

    at = [(nc.sbuf_base + 63) // 64 * 64]

    def region(size):
        start = at[0]
        at[0] += (size + 31) // 32 * 32
        return start

    def view(name, start, shape, dt=F32):
        return nc.alloc_sbuf_tensor_at(name, shape, dt, offset=start)

    def sized(name, shape, dt=F32):
        return view(name, region(4 * math.prod(shape[1:])), shape, dt)

    act_hi = sized("act_hi", [P, KT, T], F32R)
    act_lo = sized("act_lo", [P, KT, T], F32R)
    raw = sized("raw", [P, RING, WIDTH])
    w_hi = sized("w_hi", [P, RING, WIDTH], F32R)
    w_lo = sized("w_lo", [P, RING, WIDTH], F32R)
    ident = sized("ident", [P, P])
    vec_t = sized("vec_t", [P, P])
    rstd = sized("rstd", [P, TT])
    row_parts = sized("row_parts", [P, TT, N_Y])
    row_ss = sized("row_ss", [P, TT])
    neg_half = sized("neg_half", [P, 6 * TT * KVH])
    scale_g = sized("scale_g", [P, 4])
    bias_at = region(4 * WIDTH)
    bias = view("bias", bias_at, [P, WIDTH])
    vec_rows = view("vec_rows", bias_at, [P, P])
    sq_a = view("sq_a", bias_at, [P, TT * KVH, HD])
    reg_a = region(32768)
    reg_t = region(16384)
    reg_k = region(24576)
    reg_q = region(16384)
    reg_n = region(16384)
    assert at[0] <= nc.sbuf_usable_end, (at[0], nc.sbuf_usable_end)

    x_tok = view("x_tok", reg_a, [P, TT, D])
    w1 = view("w1", reg_a, [P, 2, CMP_BLOCK, HD])
    uz = view("uz", reg_a, [P, 8, TT, PG])
    pool_hi = view("pool_hi", reg_a, [P, UT, T], F32R)
    pool_lo = view("pool_lo", reg_a + 16384, [P, UT, T], F32R)
    x_out = view("x_out", reg_a, [P, N_Y, TT, WIDTH])
    ys = view("ys", reg_t, [P, 1 + N_Y, TT, WIDTH])
    kvq = view("kvq", reg_k, [P, 6 + KVH, TT, KVW])
    nsa_hi = view("nsa_hi", reg_q, [P, UT, T], F32R)
    nsa_lo = view("nsa_lo", reg_n, [P, UT, T], F32R)
    u_g = view("u_g", reg_k, [P, TT, PG])
    mix_t = view("mix_t", reg_k, [P, PG // P, T])
    z_g = view("z_g", reg_k + 4096, [P, TT, PG])
    silu_zt = view("silu_zt", reg_k + 4096, [P, PG // P, T])
    pw = view("pw", reg_k + 8192, [P, PG // P, PG])
    n_tok = view("n_tok", reg_k + 16384, [P, TT, WIDTH])
    band = view("band", reg_t, [P, 4, 3 * P])
    t_at = [reg_t]

    def in_t(name, shape, dt=F32):
        start = t_at[0]
        t_at[0] += (4 * math.prod(shape[1:]) + 31) // 32 * 32
        assert t_at[0] <= reg_t + 16384, name
        return view(name, start, shape, dt)

    n_at = [reg_n]

    def in_n(name, shape, dt=F32):
        start = n_at[0]
        n_at[0] += (4 * math.prod(shape[1:]) + 31) // 32 * 32
        assert n_at[0] <= reg_n + 16384, name
        return view(name, start, shape, dt)

    dist = in_t("dist", [P, GQ, 3 * P])
    dist_c = in_t("dist_c", [P, GQ, TT, NC])
    kc_t = in_t("kc_t", [P, KVH * NC])
    vc = in_t("vc", [NC, KVH, HD])
    gate6 = in_t("gate6", [P, H, 6])
    row_mask = in_t("row_mask", [P, 1])
    stat_ss = in_t("stat_ss", [P, 6, TT, KVH])
    stat_rs = in_t("stat_rs", [P, 6, TT, KVH])
    t_mark = t_at[0]
    neg_max = in_t("neg_max", [P, 6])
    sums = in_t("sums", [P, 6])
    inv = in_t("inv", [P, 6])
    wgt = in_t("wgt", [P, 6])
    s_cmp = in_t("s_cmp", [P, TT, NC])
    prob_ct = in_t("prob_ct", [NC, TT, P])
    prob_t = in_t("prob_t", [P, 2, 3 * P])
    qk = in_n("qk", [P, TT, 6, HD])
    qk_t = in_n("qk_t", [P, 6, T])
    s = in_n("s", [P, 2, 3 * P])
    WG = KT * GATES
    PAD = P - GATES
    wg = view("wg", reg_n, [P, WG])
    kb_v = view("kb_v", reg_n, [P, CMP_STRIDE, KVH + 1, CMP_STRIDE])
    sq_b = view("sq_b", reg_n, [P, TT * KVH, HD])
    wg_hi = view("wg_hi", reg_n + 6144, [P, WG + PAD], F32R)
    kb_k = view("kb_k", reg_q + 8192, [P, CMP_STRIDE, KVH + 1, CMP_STRIDE])
    wg_lo = view("wg_lo", reg_t + 16384 - 6464, [P, WG + PAD], F32R)
    assert t_mark <= reg_t + 16384 - 6464
    gate_t = view("gate_t", reg_n + 6144, [GATES, T])
    after = [reg_n + 6144 + 6464]

    def behind(name, shape):
        start = after[0]
        after[0] += (4 * math.prod(shape[1:]) + 31) // 32 * 32
        assert after[0] <= reg_n + 16384, name
        return view(name, start, shape)

    w2 = behind("w2", [P, 2, HD])
    hid_b = behind("hid_b", [P, 2])
    hid_x = behind("hid_x", [P, 2, KVH * NC])
    hid_s = behind("hid_s", [P, 2, KVH * NC])
    hid = behind("hid", [P, 2, KVH * NC])
    kc_n = behind("kc_n", [KVH * NC, HD])
    kc_sq = behind("kc_sq", [KVH * NC, HD])
    kc_ss = behind("kc_ss", [KVH * NC, 1])
    kc_rs = behind("kc_rs", [KVH * NC, 1])

    V_NORM = 0
    V_SCALE = V_NORM + KT
    V_QG = V_SCALE + UT
    V_KG = V_QG + 1
    V_PE = V_KG + NBR
    V_B1 = V_PE + 2 * CMP_BLOCK
    V_END = V_B1 + 2

    ps = nc.alloc_psum_tensor("ps", [P, 8, BANK], F32)

    sems = {}

    def sem(name):
        sems[name] = nc.alloc_semaphore(name)
        return sems[name]

    vec_landed = sem("vec_landed")
    x_landed = [sem(f"x_landed{i}") for i in range(4)]
    raw_landed = [sem(f"raw_landed{i}") for i in range(RING)]
    wg_landed = sem("wg_landed")
    w1_landed = sem("w1_landed")
    bias_landed = sem("bias_landed")
    pw_landed = sem("pw_landed")
    xo_landed = sem("xo_landed")
    out_stored = sem("out_stored")
    hi_done = sem("hi_done")
    split_done = sem("split_done")
    weights_free = sem("weights_free")
    acc_done = sem("acc_done")
    acc_free = [sem("acc_free0"), sem("acc_free1")]
    const_pool = sem("const_pool")
    const_ready = sem("const_ready")
    band_built = sem("band_built")
    vec_psum = sem("vec_psum")
    vec_ready = sem("vec_ready")
    x_psum = sem("x_psum")
    xt_hi = sem("xt_hi")
    xt_lo = sem("xt_lo")
    sq_act = sem("sq_act")
    sq_dve = sem("sq_dve")
    row_sum = sem("row_sum")
    row_ms = sem("row_ms")
    rstd_ready = sem("rstd_ready")
    wg_hi_done = sem("wg_hi_done")
    wg_lo_done = sem("wg_lo_done")
    ct_psum = sem("ct_psum")
    ct_sbuf = sem("ct_sbuf")
    kb_zero = sem("kb_zero")
    kb_pos = sem("kb_pos")
    hid_psum = sem("hid_psum")
    hid_step = sem("hid_step")
    hid_sig = sem("hid_sig")
    w2_psum = sem("w2_psum")
    kc_step = sem("kc_step")
    kc_rstd = sem("kc_rstd")
    kct_psum = sem("kct_psum")
    kct_ready = sem("kct_ready")
    vc_ready = sem("vc_ready")
    gate_psum = sem("gate_psum")
    gate_sig = sem("gate_sig")
    gate_ready = sem("gate_ready")
    qk_sq = sem("qk_sq")
    qk_ss = sem("qk_ss")
    gate_lin = sem("gate_lin")
    gate_turned = sem("gate_turned")
    wg_padded = sem("wg_padded")
    qk_ms = sem("qk_ms")
    qk_rstd = sem("qk_rstd")
    qk_normed = sem("qk_normed")
    qkt_psum = sem("qkt_psum")
    qkt_act = sem("qkt_act")
    qkt_dve = sem("qkt_dve")
    scores_done = sem("scores_done")
    biased = sem("biased")
    head_max = sem("head_max")
    exp_done = sem("exp_done")
    inv_done = sem("inv_done")
    wgt_done = sem("wgt_done")
    probs_ready = sem("probs_ready")
    probt_psum = sem("probt_psum")
    probt_ready = sem("probt_ready")
    pv_done = sem("pv_done")
    head_out = sem("head_out")
    dist_scaled = sem("dist_scaled")
    nz_sig = sem("nz_sig")
    nz_silu = sem("nz_silu")
    n_ready = sem("n_ready")
    nt_psum = sem("nt_psum")
    nt_hi = sem("nt_hi")
    nt_lo = sem("nt_lo")
    gate_out = sem("gate_out")
    uz_copied = sem("uz_copied")
    mix_psum = sem("mix_psum")
    mix_act = sem("mix_act")
    mix_dve = sem("mix_dve")
    zt_psum = sem("zt_psum")
    zt_sig = sem("zt_sig")
    zt_silu = sem("zt_silu")
    pwt_psum = sem("pwt_psum")
    pool_v = sem("pool_v")
    pool_hi_done = sem("pool_hi_done")
    pool_lo_done = sem("pool_lo_done")
    y_sum = sem("y_sum")
    yt_psum = sem("yt_psum")
    yt_hi = sem("yt_hi")
    yt_lo = sem("yt_lo")

    SCORES = [4 + 7 * h for h in range(GQ)]
    EXPS = [5 + 7 * h for h in range(GQ)]
    SCALES = [6 + 7 * h for h in range(GQ)]
    TURNS = [8 + 7 * h for h in range(GQ)]
    VALUES = [10 + 7 * h for h in range(GQ)]
    LAST_Y = [3, 5, 7, 9]

    def up(v):
        return v.bitcast(F32)

    block = nc.Block()
    with block:

        @block.sync
        def _(sp):
            def load(first, rows, cols, beside={}):
                for kt in range(rows.shape[0] // P):
                    if kt in beside:
                        beside[kt]()
                    sp.wait_ge(split_done, first + (kt + 1))
                    sp.dma_start(raw[:, kt % RING, :], rows[kt * P:(kt + 1) * P, cols]).then_inc(
                        raw_landed[kt % RING], 16)

            for start, rows in (
                (V_NORM, norm_g[0].rearrange("(a b) -> a b", b=P)),
                (V_SCALE, pool_scale[0].rearrange("(a b) -> a b", b=P)),
                (V_QG, q_norm_g),
                (V_KG, k_norm_g[0]),
                (V_PE, cmp_pe[0].rearrange("a j d -> (a j) d")),
                (V_B1, cmp_b1[0]),
            ):
                sp.dma_start(vec_rows[start:start + rows.shape[0], :], rows).then_inc(vec_landed, 16)
            def load_x(i):
                c = slice(i * WIDTH, (i + 1) * WIDTH)
                sp.dma_start(x_tok[:, :, c], x_pt[:, :, c]).then_inc(x_landed[i], 16)

            load_x(0)
            load(0, w_in, slice(COL_KV, COL_KV + WIDTH), {2: lambda: load_x(1), 6: lambda: load_x(2), 12: lambda: load_x(3)})

            wg_cols = w_in[:, COL_G:COL_G + GATES].rearrange("(k p) n -> p k n", p=P)

            def load_wg(k):
                n = KT // 8
                sp.dma_start(wg[:, k * n * GATES:(k + 1) * n * GATES].rearrange("p (k n) -> p k n", n=GATES),
                             wg_cols[:, k * n:(k + 1) * n, :]).then_inc(wg_landed, 16)

            def load_w1(n):
                if n == 0:
                    sp.wait_ge(sq_act, N_Y)
                    sp.wait_ge(sq_dve, N_Y)
                    sp.wait_ge(xt_lo, KT // 2)
                kv, j = n // 4, n % 4 * 8
                sp.dma_start(w1[:, kv, j:j + 8, :], cmp_w1[0, kv, j * HD:(j + 8) * HD, :].rearrange(
                    "(j d) e -> d j e", d=HD)).then_inc(w1_landed, 16)

            def load_w2():
                sp.dma_start(w2[:], cmp_w2[0].rearrange("a e f -> e a f")).then_inc(w1_landed, 16)

            load(KT, w_in, slice(COL_KV + WIDTH, COL_KV + 2 * WIDTH),
                 {8 + 3 * k: (lambda k=k: load_wg(k)) for k in range(8)})
            load(2 * KT, w_in, slice(COL_KV + 2 * WIDTH, COL_KV + 3 * WIDTH),
                 {4 + 3 * n: (lambda n=n: load_w1(n)) for n in range(8)} | {28: load_w2})
            with sp.Fori(0, 2) as i:
                load(i * KT + 3 * KT, w_in, bass.ds(i * WIDTH + COL_Q, WIDTH))
            with sp.Fori(0, KVH) as i:
                load(i * KT + CH_L2, w_in, bass.ds(i * WIDTH + COL_U, WIDTH))

            def load_pool_w(n):
                sp.wait_ge(head_out, 1 + H)
                sp.wait_ge(pool_lo_done, n * 2 + 2)
                sp.dma_start(pw[:], pool_w[0, bass.ds(n, 1)].rearrange("g (c p) d -> p (g c) d", p=P)).then_inc(
                    pw_landed, 16)

            def load_bias(which, col, left, between=None):
                sp.wait_ge(acc_free[1], left)
                sp.wait_ge(vec_ready, 1)
                if between:
                    between()
                sp.dma_start(bias[:], merge_bias[0, which, bass.ds(col, WIDTH)].to_broadcast([P, WIDTH])).then_inc(
                    bias_landed, 16)

            with sp.Fori(0, 2) as i:
                load(i * 2 * KT + CH_TL, w_in, bass.ds(i * WIDTH + COL_NZ, WIDTH), {8: lambda: load_pool_w(i * 2)})

                def beside():
                    load_bias(bass.ds(i, 1), 0, i * 2 + (Q_TL + 1), lambda: load_pool_w(i * 2 + 1))

                load(i * 2 * KT + CH_TL + KT, w_in, bass.ds(i * D + COL_M, WIDTH), {8: beside})
            with sp.Fori(0, N_Y - 1) as i:
                load(i * PER3 + CH_P3, w_pu, bass.ds(i * WIDTH, WIDTH))
                load(i * PER3 + CH_P3 + UT, w_nu, bass.ds(i * WIDTH, WIDTH))
                for which in range(2):
                    load(i * PER3 + CH_P3 + 2 * UT + which * KT, w_in,
                         bass.ds(i * WIDTH + COL_M + which * D + WIDTH, WIDTH),
                         {8: lambda: load_bias(slice(which, which + 1), i * WIDTH + WIDTH,
                                               i * 4 + (Q_P3 + 1 + 3 * which))})
            load(CH_EP, w_pu, slice((N_Y - 1) * WIDTH, N_Y * WIDTH))
            load(CH_EP + UT, w_nu, slice((N_Y - 1) * WIDTH, N_Y * WIDTH))
            sp.wait_ge(weights_free, CH_EP + UT + RING)
            for g in range(N_Y):
                sp.dma_start(x_out[:, g], x_pt[:, :, g * WIDTH:(g + 1) * WIDTH]).then_inc(xo_landed, 16)
            with sp.Fori(0, N_Y) as i:
                load(i * KT + CH_P4, w_o, bass.ds(i * WIDTH, WIDTH))

        @block.gpsimd
        def _(pool):
            g = nc.gpsimd
            g.memset(ident[:], 0.0).then_inc(const_pool, 1)
            g.memset(neg_half[:], -0.5).then_inc(const_pool, 1)
            g.memset(row_mask[:], 1.0).then_inc(const_pool, 1)
            pool.wait_ge(const_pool, 3)
            g.affine_select(out=ident[:], in_=ident[:], compare_op=ALU.not_equal, fill=1.0, base=0,
                            pattern=[[-1, P]], channel_multiplier=1).then_inc(const_ready, 1)
            g.affine_select(out=row_mask[:], in_=row_mask[:], compare_op=ALU.is_ge, fill=0.0,
                            base=1 - CMP_BLOCK, pattern=[[0, 1]], channel_multiplier=1).then_inc(const_ready, 1)
            g.iota(dist[:, 0, 0:P], [[1, P]], base=0, channel_multiplier=-1,
                   allow_small_or_imprecise_dtypes=True).then_inc(const_pool, 1)
            g.iota(dist[:, 0, P:3 * P], [[1, 2 * P]], base=-P, channel_multiplier=-1,
                   allow_small_or_imprecise_dtypes=True).then_inc(const_pool, 1)
            g.iota(dist_c[:, 0], [[-P, TT], [CMP_STRIDE, NC]], base=CMP_BLOCK - 1, channel_multiplier=-1,
                   allow_small_or_imprecise_dtypes=True).then_inc(const_pool, 1)
            pool.wait_ge(const_pool, 6)
            for h in reversed(range(GQ)):
                slope = 2.0 ** (-8.0 * (h + 1) / H)
                if h == 0:
                    pool.wait_ge(const_pool, 6 + 2 * (GQ - 1))
                g.tensor_scalar(dist[:, h], dist[:, 0], slope, None, ALU.mult).then_inc(const_pool, 1)
                g.tensor_scalar(dist_c[:, h], dist_c[:, 0], slope, None, ALU.mult).then_inc(const_pool, 1)
            pool.wait_ge(const_pool, 6 + 2 * GQ)
            g.affine_select(out=dist[:, :, 0:P], in_=dist[:, :, 0:P], compare_op=ALU.is_ge, fill=MASKED,
                            base=0, pattern=[[0, GQ], [-1, P]], channel_multiplier=1).then_inc(const_ready, 1)
            g.affine_select(out=dist[:, :, P:3 * P], in_=dist[:, :, P:3 * P], compare_op=ALU.is_ge, fill=MASKED,
                            base=P, pattern=[[0, GQ], [-1, 2 * P]], channel_multiplier=1).then_inc(const_ready, 1)
            g.affine_select(out=dist_c[:], in_=dist_c[:], compare_op=ALU.is_ge, fill=MASKED,
                            base=1 - CMP_BLOCK, pattern=[[0, GQ], [P, TT], [-CMP_STRIDE, NC]],
                            channel_multiplier=1).then_inc(const_ready, 1)
            pool.wait_ge(row_ms, 1)
            g.tensor_tensor(rstd[:], row_ss[:], neg_half[:, 0:TT], ALU.pow).then_inc(rstd_ready, 1)
            pool.wait_ge(kc_step, 3)
            g.tensor_tensor(kc_rs[:], kc_ss[:], neg_half[0:KVH * NC, 0:1], ALU.pow).then_inc(kc_rstd, 1)
            pool.wait_ge(qk_ms, 1)
            flat = "p a t h -> p (a t h)"
            g.tensor_tensor(stat_rs[:].rearrange(flat), stat_ss[:].rearrange(flat), neg_half[:], ALU.pow).then_inc(
                qk_rstd, 1)
            pool.wait_ge(acc_free[0], 1 + Q_TL)
            pool.wait_ge(acc_free[1], 1 + Q_TL)
            for n, w in enumerate(WINDOWS):
                g.memset(band[:, n], 1.0 / w).then_inc(band_built, 1)
            pool.wait_ge(band_built, 4)
            for n, w in enumerate(WINDOWS):
                for t in range(w - 1):
                    g.memset(band[:, n, t:t + 1], 1.0 / (t + 1)).then_inc(band_built, 1)
            done = 4 + sum(w - 1 for w in WINDOWS)
            pool.wait_ge(band_built, done)
            for n, w in enumerate(WINDOWS):
                for part, base in ((slice(0, 2 * P), 0), (slice(2 * P, 3 * P), 0)):
                    b = band[:, n, part]
                    g.affine_select(out=b, in_=b, compare_op=ALU.is_ge, fill=0.0, base=base,
                                    pattern=[[1, part.stop - part.start]], channel_multiplier=-1).then_inc(band_built, 1)
            done += 8
            pool.wait_ge(band_built, done)
            for n, w in enumerate(WINDOWS):
                for part in (slice(0, 2 * P), slice(2 * P, 3 * P)):
                    b = band[:, n, part]
                    g.affine_select(out=b, in_=b, compare_op=ALU.is_ge, fill=0.0, base=w - 1,
                                    pattern=[[-1, part.stop - part.start]], channel_multiplier=1).then_inc(band_built, 1)
            done += 8
            pool.wait_ge(band_built, done)
            for n, w in enumerate(WINDOWS):
                for start in (0, 2 * P):
                    b = band[:, n, start:start + P]
                    g.tensor_tensor(b, b, ident[:], ALU.subtract).then_inc(band_built, 1)
            with pool.Fori(0, 2) as i:
                for half in range(2):
                    pool.wait_ge(pool_lo_done, i * 4 + 2 * half + 2)
                    g.tensor_copy(u_g[:], uz[:, bass.ds(i * 2 + half, 1)])
                    g.tensor_copy(z_g[:], uz[:, bass.ds(i * 2 + half + 4, 1)])
                    g.tensor_copy(scale_g[:], vec_t[:, bass.ds(i * 8 + 4 * half + V_SCALE, 4)]).then_inc(uz_copied, 1)

        @block.scalar
        def _(act):
            a = nc.scalar

            def ahead(first, kt, last=False):
                if last and kt >= KT - LEAD:
                    return
                slot = (kt + LEAD) % RING
                act.wait_ge(weights_free, first + (kt + LEAD + 1))
                act.wait_ge(raw_landed[slot], first * 4 + ((kt + LEAD) // RING * 16 + 16))
                a.activation(w_hi[:, slot, :], raw[:, slot, :], ACT.Copy).then_inc(hi_done, 1)

            def turn_x(b):
                act.wait_ge(x_psum, b + 1)
                for e in range(2):
                    k = a.activation(act_hi[:, 2 * b + e, :], ps[:, 4 + b % 4, e * T:(e + 1) * T], ACT.Copy,
                                     scale=vec_t[:, V_NORM + 2 * b + e:V_NORM + 2 * b + e + 1])
                k.then_inc(xt_hi, 1)

            act.wait_ge(vec_ready, 1)
            turn_x(0)
            for c in range(LEAD):
                act.wait_ge(raw_landed[c], 16)
                a.activation(w_hi[:, c, :], raw[:, c, :], ACT.Copy).then_inc(hi_done, 1)
            turn_x(1)

            def leave(q, dst):
                act.wait_ge(acc_done, q + 1)
                a.activation(dst, ps[:, 0:NH, :], ACT.Copy, scale=rstd[:, 0:1]).then_inc(acc_free[0], 1)

            for kt in range(KT):
                ahead(0, kt)
                if kt % 2 == 0 and kt // 2 + 2 < KT // 2:
                    turn_x(kt // 2 + 2)
                if kt % 8 == 5:
                    c = kt // 8
                    act.wait_ge(xt_lo, 4 * c + 4)
                    piece = x_tok[:, 0, c * WIDTH:(c + 1) * WIDTH]
                    a.activation(piece, piece, ACT.Square, accum_out=row_parts[:, 0, c:c + 1]).then_inc(sq_act, 1)
            act.wait_ge(rstd_ready, 1)
            leave(0, kvq[:, 0:2, 0, :])

            with act.Fori(1, N_A - 1) as i:
                for kt in range(KT):
                    ahead(i * KT, kt)
                leave(i, kvq[:, bass.ds(i * 2, 2), 0, :])

            def square(n, out_):
                half = (2, 4, 6, 7, 8, 9)[n]
                a.activation(out_[:], kvq[:, half].rearrange("p t (h d) -> p (t h) d", d=HD), ACT.Square).then_inc(
                    qk_sq, 1)

            base = (N_A - 1) * KT
            for kt in range(KT):
                if kt == 0:
                    act.wait_ge(wg_landed, 16 * 8)
                    a.activation(wg_hi[:, 0:WG], wg[:], ACT.Copy).then_inc(wg_hi_done, 1)
                ahead(base, kt)
                if kt in (2, 6):
                    n = (kt - 2) // 4
                    kb = (kb_k, kb_v)[n]
                    act.wait_ge(ct_psum, n + 1)
                    act.wait_ge(kb_pos, n + 1)
                    for half in range(2):
                        k = a.activation(
                            kb[:, :, 2 * half:2 * half + 2, :].rearrange("p r h c -> p h c r"),
                            ps[:, 6 + half, :].rearrange("p (h c r) -> p h c r", h=2, r=CMP_STRIDE), ACT.Copy)
                    k.then_inc(ct_sbuf, 1)
                if kt in (8, 11, 14, 17):
                    n = (kt - 8) // 3
                    act.wait_ge(acc_free[0], N_A)
                    act.wait_ge(acc_free[1], N_A)
                    if n:
                        act.wait_ge(qk_ss, n)
                    square(n, sq_a)
                if kt == 16:
                    act.wait_ge(gate_psum, 1)
                    a.activation(gate_t[:], ps[0:GATES, 4, 0:T], ACT.Copy).then_inc(gate_lin, 1)
                if kt == 19:
                    act.wait_ge(gate_turned, 1)
                    lin = ps[:, 5, 0:TT * GATES].rearrange("p (t h b) -> p t h b", t=TT, b=NBR)
                    for t in range(TT):
                        a.activation(gate6[:, :, 2 * t:2 * t + 2], lin[:, t, :, 1:3], ACT.Sigmoid, scale=rstd[:, t:t + 1])
                        k = a.activation(gate6[:, :, 4 + t], lin[:, t, :, 0], ACT.Sigmoid, scale=rstd[:, t:t + 1])
                    k.then_inc(gate_sig, 1)
                if kt == 22:
                    act.wait_ge(hid_step, 4)
                    a.activation(hid_s[:], hid_x[:], ACT.Sigmoid).then_inc(hid_sig, 1)
                if kt == 24:
                    act.wait_ge(w2_psum, 1)
                    a.activation(vc[:], ps[0:NC, 7, :].rearrange("p (h d) -> p h d", h=KVH), ACT.Copy).then_inc(vc_ready, 1)
            leave(N_A - 1, kvq[:, 2 * (N_A - 1):2 * N_A, 0, :])
            act.wait_ge(acc_free[0], 1 + N_A)
            act.wait_ge(acc_free[1], 1 + N_A)
            act.wait_ge(qk_ss, 4)
            square(4, sq_a)
            square(5, sq_b)

            with act.Fori(0, KVH) as j:
                for kt in range(KT):
                    ahead(j * KT + CH_L2, kt)
                    if kt == 2:
                        act.wait_ge(qkt_psum, j + 1)
                        a.activation(qk_t[:, 4, :], ps[:, 6, 0:T], ACT.Copy, scale=vec_t[:, V_KG + 1:V_KG + 2])
                        a.activation(qk_t[:, 5, :], ps[:, 6, T:2 * T], ACT.Copy,
                                     scale=vec_t[:, V_KG + 2:V_KG + 3]).then_inc(qkt_act, 1)
                    if kt in EXPS:
                        h = EXPS.index(kt)
                        act.wait_ge(head_max, j * GQ + (h + 1))
                        for br in range(2):
                            a.activation(s[:, br, 0:P], s[:, br, 0:P], ACT.Exp, bias=neg_max[:, br:br + 1],
                                         accum_out=sums[:, br:br + 1])
                            a.activation(s[:, br, P:3 * P], s[:, br, P:3 * P], ACT.Exp, bias=neg_max[:, 2 + br:3 + br],
                                         accum_out=sums[:, 2 + br:3 + br])
                        for t in range(TT):
                            k = a.activation(s_cmp[:, t, :], s_cmp[:, t, :], ACT.Exp, bias=neg_max[:, 4 + t:5 + t],
                                             accum_out=sums[:, 4 + t:5 + t])
                        k.then_inc(exp_done, 1)
                    if kt in TURNS:
                        h = TURNS.index(kt)
                        act.wait_ge(probt_psum, j * GQ + (h + 1))
                        a.activation(prob_t[:], ps[:, 6:8, 0:3 * P], ACT.Copy)
                        a.activation(prob_ct[:], ps[0:NC, 6:8, 3 * P:4 * P], ACT.Copy).then_inc(probt_ready, 1)
                leave(j + Q_L2, uz[:, bass.ds(j * 2, 2), 0, :])

            def pool_group(kt, n):
                if kt == 9:
                    act.wait_ge(mix_psum, n + 1)
                    a.activation(mix_t[:, 0:2, :], ps[:, 4, :], ACT.Copy).then_inc(mix_act, 1)
                    act.wait_ge(zt_psum, n + 1)
                    for half in range(2):
                        a.activation(silu_zt[:, 2 * half:2 * half + 2, :], ps[:, 6 + half, :],
                                     ACT.Sigmoid).then_inc(zt_sig, 1)
                if kt in (13, 15):
                    b = (kt - 13) // 2
                    act.wait_ge(pool_v, n * 2 + (b + 1))
                    a.activation(pool_hi[:, bass.ds(n * 4 + 2 * b, 2), :], silu_zt[:, 2 * b:2 * b + 2, :],
                                 ACT.Copy).then_inc(pool_hi_done, 1)

            with act.Fori(0, 2) as i:
                for kt in range(KT):
                    ahead(i * 2 * KT + CH_TL, kt)
                    pool_group(kt, i * 2)
                for t in range(TT):
                    if t == 0:
                        act.wait_ge(acc_done, i * 2 + (Q_TL + 1))
                    else:
                        act.wait_ge(weights_free, i * 2 * KT + (CH_TL + KT + RING))
                    a.activation(n_tok[:, t, :], ps[:, NH * t:NH * t + NH, :], ACT.Sigmoid,
                                 scale=rstd[:, t:t + 1]).then_inc(nz_sig, 1)
                for kt in range(KT):
                    ahead(i * 2 * KT + CH_TL + KT, kt)
                    if kt in (1, 3, 5, 7):
                        b = kt // 2
                        act.wait_ge(nt_psum, i * 4 + (b + 1))
                        a.activation(nsa_hi[:, bass.ds(i * 8 + 2 * b, 2), :], ps[:, 6 + b % 2, :],
                                     ACT.Copy).then_inc(nt_hi, 1)
                    pool_group(kt, i * 2 + 1)
                for t in range(TT):
                    act.wait_ge(acc_free[t], i * 2 + (Q_TL + 3))
                    y = ys[:, bass.ds(i * -1 + 1, 1), t, :]
                    a.activation(y, y, ACT.Sigmoid).then_inc(gate_out, 1)

            with act.Fori(0, N_Y - 1) as i:
                for kt in range(2 * UT):
                    ahead(i * PER3 + CH_P3, kt)
                for which in range(2):
                    for kt in range(KT):
                        ahead(i * PER3 + CH_P3 + 2 * UT + which * KT, kt)
                    for t in range(TT):
                        act.wait_ge(acc_free[t], i * 4 + (Q_P3 + 4 + which))
                        y = ys[:, bass.ds(i + 2, 1), t, :] if which == 0 else ys[:, 0, t, :]
                        a.activation(y, y, ACT.Sigmoid).then_inc(gate_out, 1)

            def turn_y(b):
                act.wait_ge(yt_psum, b + 1)
                a.activation(act_hi[:, 2 * b:2 * b + 2, :], ps[:, 4 + b % 4, :], ACT.Copy).then_inc(yt_hi, 1)

            for kt in range(2 * UT):
                ahead(CH_EP, kt)
                if kt % 2 == 1 and kt // 2 < 12:
                    turn_y(kt // 2)

            def store(i):
                for t in range(TT):
                    act.wait_ge(acc_free[t], i + (Q_P4 + 2))
                act.dma_start(out_pt[:, :, bass.ds(i * WIDTH, WIDTH)], x_out[:, bass.ds(i, 1), :, :]).then_inc(
                    out_stored, 16)

            for kt in range(KT):
                ahead(CH_P4, kt)
                if kt in LAST_Y:
                    turn_y(12 + LAST_Y.index(kt))
            store(0)
            with act.Fori(1, N_Y - 1) as i:
                for kt in range(KT):
                    ahead(i * KT + CH_P4, kt)
                store(i)
            for kt in range(KT):
                ahead(CH_P4 + (N_Y - 1) * KT, kt, last=True)
            for t in range(TT):
                act.wait_ge(acc_free[t], Q_P4 + N_Y + 1)
                act.dma_start(out_pt[:, t:t + 1, (N_Y - 1) * WIDTH:], x_out[:, N_Y - 1, t:t + 1, :]).then_inc(
                    out_stored, 16)
            act.wait_ge(out_stored, 16 * (N_Y + 1))

        @block.vector
        def _(dve):
            v = nc.vector
            dve.sem_inc(split_done, RING)
            dve.sem_inc(acc_free[0], 1)
            dve.sem_inc(acc_free[1], 1)
            dve.sem_inc(head_out, 1)
            dve.sem_inc(nt_lo, 2)
            dve.sem_inc(pool_lo_done, 2)

            def split(chunk, slot):
                dve.wait_ge(hi_done, chunk)
                v.tensor_tensor(w_lo[:, slot, :], raw[:, slot, :], up(w_hi[:, slot, :]), ALU.subtract).then_inc(
                    split_done, 1)

            def ahead(first, kt, last=False):
                if last and kt >= KT - LEAD:
                    return
                split(first + (kt + LEAD + 1), (kt + LEAD) % RING)

            dve.wait_ge(vec_psum, 1)
            v.tensor_copy(vec_t[:, 0:V_END], ps[:, 7, 0:V_END]).then_inc(vec_ready, 1)
            dve.wait_ge(vec_ready, 1)
            for w_ in (wg_hi, wg_lo):
                v.memset(up(w_[:, WG:]), 0.0).then_inc(wg_padded, 1)

            def turn_x(b):
                dve.wait_ge(xt_hi, b + 1)
                for e in range(2):
                    kt = 2 * b + e
                    k = v.scalar_tensor_tensor(act_lo[:, kt, :], ps[:, 4 + b % 4, e * T:(e + 1) * T],
                                               vec_t[:, V_NORM + kt:V_NORM + kt + 1], up(act_hi[:, kt, :]),
                                               ALU.mult, ALU.subtract)
                k.then_inc(xt_lo, 1)

            turn_x(0)
            for c in range(LEAD):
                split(c + 1, c)
            turn_x(1)

            def leave(last_chunk, dst):
                dve.wait_ge(weights_free, last_chunk + RING)
                v.tensor_scalar(dst, ps[:, NH:2 * NH, :], rstd[:, 1:2], None, ALU.mult).then_inc(acc_free[1], 1)

            for kt in range(KT):
                ahead(0, kt)
                if kt % 2 == 0 and kt // 2 + 2 < KT // 2:
                    turn_x(kt // 2 + 2)
                if kt % 8 == 5:
                    c = kt // 8
                    piece = x_tok[:, 1, c * WIDTH:(c + 1) * WIDTH]
                    dve.wait_ge(x_psum, 4 * c + 4)
                    v.tensor_tensor_reduce(out=piece, in0=piece, in1=piece, scale=1.0, scalar=0.0, op0=ALU.mult,
                                           op1=ALU.add, accum_out=row_parts[:, 1, c:c + 1]).then_inc(sq_dve, 1)
            dve.wait_ge(sq_act, N_Y)
            dve.wait_ge(sq_dve, N_Y)
            v.reduce_sum(row_ss[:], row_parts[:], AX.X).then_inc(row_sum, 1)
            dve.wait_ge(row_sum, 1)
            v.tensor_scalar(row_ss[:], row_ss[:], 1.0 / D, EPS, ALU.mult, ALU.add).then_inc(row_ms, 1)
            dve.wait_ge(rstd_ready, 1)
            leave(KT, kvq[:, 0:2, 1, :])

            def sum_squares(n, from_):
                dve.wait_ge(qk_sq, n + 1)
                v.reduce_sum(stat_ss[:, n].rearrange("p t h -> p (t h)"), from_[:], AX.X).then_inc(qk_ss, 1)

            with dve.Fori(1, N_A - 1) as i:
                for kt in range(KT):
                    ahead(i * KT, kt)
                leave(i * KT + KT, kvq[:, bass.ds(i * 2, 2), 1, :])

            base = (N_A - 1) * KT
            for kt in range(KT):
                if kt == 0:
                    dve.wait_ge(wg_hi_done, 1)
                    v.tensor_tensor(wg_lo[:, 0:WG], wg[:], up(wg_hi[:, 0:WG]), ALU.subtract).then_inc(wg_lo_done, 1)
                    dve.wait_ge(wg_lo_done, 1)
                    for n, kb in enumerate((kb_k, kb_v)):
                        v.memset(kb[:, :, KVH, :], 0.0).then_inc(kb_zero, 1)
                        dve.wait_ge(kb_zero, n + 1)
                        v.tensor_copy(kb[:, :, KVH, 0], vec_t[:, V_PE + n * CMP_BLOCK:V_PE + n * CMP_BLOCK + CMP_STRIDE])
                        v.tensor_copy(kb[:, :, KVH, CMP_STRIDE - 1],
                                      vec_t[:, V_PE + n * CMP_BLOCK + CMP_STRIDE:V_PE + (n + 1) * CMP_BLOCK]).then_inc(
                            kb_pos, 1)
                ahead(base, kt)
                if kt in (8, 11, 14, 17):
                    sum_squares((kt - 8) // 3, sq_a)
                if kt == 20:
                    dve.wait_ge(gate_sig, 1)
                    dve.wait_ge(const_ready, 5)
                    v.tensor_scalar(gate6[:, :, 4], gate6[:, :, 4], row_mask[:], None, ALU.mult).then_inc(gate_ready, 1)
                    v.tensor_scalar(vec_t[:, V_QG:V_QG + 1], vec_t[:, V_QG:V_QG + 1], HD ** -0.5, None,
                                    ALU.mult).then_inc(gate_ready, 1)
                if kt == 21:
                    dve.wait_ge(hid_psum, 1)
                    for n in range(2):
                        first, second = KVH * NC, (KVH + 1) * NC - 1
                        v.tensor_tensor(hid_b[:, n:n + 1], vec_t[:, V_B1 + n:V_B1 + n + 1], ps[:, 6 + n, first:first + 1],
                                        ALU.add).then_inc(hid_step, 1)
                        dve.wait_ge(hid_step, 2 * n + 1)
                        v.tensor_scalar(hid_x[:, n, :], ps[:, 6 + n, 0:KVH * NC], hid_b[:, n:n + 1],
                                        ps[:, 6 + n, second:second + 1], ALU.add, ALU.add).then_inc(hid_step, 1)
                if kt == 22:
                    dve.wait_ge(hid_sig, 1)
                    v.tensor_tensor(hid[:], hid_x[:], hid_s[:], ALU.mult).then_inc(hid_step, 1)
                if kt == 24:
                    dve.wait_ge(w2_psum, 1)
                    v.tensor_copy(kc_n[:], ps[0:KVH * NC, 6, 128:256]).then_inc(kc_step, 1)
                    dve.wait_ge(kc_step, 1)
                    v.tensor_tensor_reduce(out=kc_sq[:], in0=kc_n[:], in1=kc_n[:], scale=1.0, scalar=0.0,
                                           op0=ALU.mult, op1=ALU.add, accum_out=kc_ss[:]).then_inc(kc_step, 1)
                    dve.wait_ge(kc_step, 2)
                    v.tensor_scalar(kc_ss[:], kc_ss[:], 1.0 / HD, EPS, ALU.mult, ALU.add).then_inc(kc_step, 1)
                if kt == 25:
                    dve.wait_ge(kc_rstd, 1)
                    v.tensor_scalar(kc_n[:], kc_n[:], kc_rs[:], None, ALU.mult).then_inc(kc_step, 1)
                if kt == 27:
                    dve.wait_ge(kct_psum, 1)
                    v.tensor_scalar(kc_t[:], ps[:, 6, 0:KVH * NC], vec_t[:, V_KG:V_KG + 1], None, ALU.mult).then_inc(
                        kct_ready, 1)
            leave(N_A * KT, kvq[:, 2 * (N_A - 1):2 * N_A, 1, :])
            dve.wait_ge(gate_ready, 2)
            dve.wait_ge(acc_free[0], 1 + N_A)
            sum_squares(4, sq_a)
            sum_squares(5, sq_b)
            dve.wait_ge(qk_ss, 6)
            v.tensor_scalar(stat_ss[:], stat_ss[:], 1.0 / HD, EPS, ALU.mult, ALU.add).then_inc(qk_ms, 1)
            dve.wait_ge(qk_rstd, 1)

            with dve.Fori(0, KVH) as j:
                for kt in range(KT):
                    ahead(j * KT + CH_L2, kt)
                    if kt == 0:
                        for t in range(TT):
                            v.tensor_tensor(qk[:, t, 0:GQ, :], kvq[:, bass.ds(j + 6, 1), t, :].rearrange(
                                "p a (m d) -> p (a m) d", d=HD),
                                stat_rs[:, bass.ds(j + 2, 1), t, :].rearrange("p a h -> p (a h)").unsqueeze(
                                    2).to_broadcast([P, GQ, HD]), ALU.mult)
                            k = v.tensor_tensor(qk[:, t, GQ:GQ + 2, :], kvq[:, 2:6:2, t, bass.ds(j * HD, HD)],
                                                stat_rs[:, 0:2, t, bass.ds(j, 1)].to_broadcast([P, 2, HD]), ALU.mult)
                        k.then_inc(qk_normed, 1)
                    if kt == 2:
                        dve.wait_ge(qkt_psum, j + 1)
                        v.tensor_scalar(qk_t[:, 0:4, :], ps[:, 4:6, :], vec_t[:, V_QG:V_QG + 1], None,
                                        ALU.mult).then_inc(qkt_dve, 1)
                    if kt in SCORES:
                        h = SCORES.index(kt)
                        dve.wait_ge(scores_done, j * GQ + (h + 1))
                        v.tensor_tensor(s[:], ps[:, 4:6, 0:3 * P],
                                        dist[:, h, :].unsqueeze(1).to_broadcast([P, 2, 3 * P]), ALU.add).then_inc(biased, 1)
                        v.tensor_tensor(s_cmp[:], ps[:, 4:6, 3 * P:3 * P + NC], dist_c[:, h], ALU.add).then_inc(biased, 1)
                        dve.wait_ge(biased, j * (2 * GQ) + (2 * h + 2))
                        v.tensor_reduce(neg_max[:, 0:2], s[:, :, 0:P], AX.X, ALU.max, negate=True)
                        v.tensor_reduce(neg_max[:, 2:4], s[:, :, P:3 * P], AX.X, ALU.max, negate=True)
                        v.tensor_reduce(neg_max[:, 4:6], s_cmp[:], AX.X, ALU.max, negate=True).then_inc(head_max, 1)
                    if kt in SCALES:
                        h = SCALES.index(kt)
                        dve.wait_ge(exp_done, j * GQ + (h + 1))
                        v.reciprocal(inv[:], sums[:]).then_inc(inv_done, 1)
                        dve.wait_ge(inv_done, j * GQ + (h + 1))
                        v.tensor_tensor(wgt[:], inv[:], gate6[:, bass.ds(j * GQ + h, 1), :], ALU.mult).then_inc(
                            wgt_done, 1)
                        dve.wait_ge(wgt_done, j * GQ + (h + 1))
                        for br in range(2):
                            v.tensor_scalar(s[:, br, 0:P], s[:, br, 0:P], wgt[:, br:br + 1], None, ALU.mult)
                            v.tensor_scalar(s[:, br, P:3 * P], s[:, br, P:3 * P], wgt[:, 2 + br:3 + br], None, ALU.mult)
                        for t in range(TT):
                            k = v.tensor_scalar(s_cmp[:, t, :], s_cmp[:, t, :], wgt[:, 4 + t:5 + t], None, ALU.mult)
                        k.then_inc(probs_ready, 1)
                    if kt in VALUES:
                        h = VALUES.index(kt)
                        dve.wait_ge(pv_done, j * GQ + (h + 1))
                        v.tensor_scalar(kvq[:, bass.ds(j + 6, 1), :, h * HD:(h + 1) * HD],
                                        ps[:, 4:6, 3 * P:4 * P], 1.0, None, ALU.mult).then_inc(head_out, 1)
                    if kt == 28:
                        v.tensor_scalar(dist[:], dist[:], 0.25, None, ALU.mult)
                        v.tensor_scalar(dist_c[:], dist_c[:], 0.25, None, ALU.mult).then_inc(dist_scaled, 1)
                leave(j * KT + (CH_L2 + KT), uz[:, bass.ds(j * 2, 2), 1, :])

            def pool_group(kt, n):
                if kt == 9:
                    dve.wait_ge(mix_psum, n + 1)
                    v.tensor_copy(mix_t[:, 2:4, :], ps[:, 5, :]).then_inc(mix_dve, 1)
                if kt == 10:
                    for half in range(2):
                        dve.wait_ge(zt_sig, n * 2 + (half + 1))
                        c = silu_zt[:, 2 * half:2 * half + 2, :]
                        v.tensor_tensor(c, c, ps[:, 6 + half, :], ALU.mult).then_inc(zt_silu, 1)
                if kt in (13, 15):
                    b = (kt - 13) // 2
                    dve.wait_ge(pwt_psum, n * 2 + (b + 1))
                    dve.wait_ge(zt_silu, n * 2 + 2)
                    for e in range(2):
                        dt = 2 * b + e
                        k = v.scalar_tensor_tensor(silu_zt[:, dt, :], ps[:, 4 + b, e * T:(e + 1) * T],
                                                   scale_g[:, dt:dt + 1], silu_zt[:, dt, :], ALU.mult, ALU.mult)
                    k.then_inc(pool_v, 1)
                    dve.wait_ge(pool_hi_done, n * 2 + (b + 1))
                    at_ = bass.ds(n * 4 + 2 * b, 2)
                    v.tensor_tensor(pool_lo[:, at_, :], silu_zt[:, 2 * b:2 * b + 2, :], up(pool_hi[:, at_, :]),
                                    ALU.subtract).then_inc(pool_lo_done, 1)

            def gate_leave(n, chunk_done, q, dst):
                dve.wait_ge(bias_landed, n * 16 + 16)
                for t in range(TT):
                    if t == 0:
                        dve.wait_ge(acc_done, q + 1)
                    else:
                        dve.wait_ge(weights_free, chunk_done + RING)
                    v.scalar_tensor_tensor(dst(t), ps[:, NH * t:NH * t + NH, :].rearrange("p a b -> p (a b)"),
                                           rstd[:, t:t + 1], bias[:], ALU.mult, ALU.add).then_inc(acc_free[t], 1)

            with dve.Fori(0, 2) as i:
                for kt in range(KT):
                    ahead(i * 2 * KT + CH_TL, kt)
                    pool_group(kt, i * 2)
                for t in range(TT):
                    dve.wait_ge(nz_sig, i * 2 + (t + 1))
                    v.scalar_tensor_tensor(n_tok[:, t, :], ps[:, NH * t:NH * t + NH, :].rearrange("p a b -> p (a b)"),
                                           rstd[:, t:t + 1], n_tok[:, t, :], ALU.mult, ALU.mult).then_inc(acc_free[t], 1)
                for t in range(TT):
                    dve.wait_ge(acc_free[t], i * 2 + (Q_TL + 2))
                    k = v.tensor_tensor(n_tok[:, t, :].rearrange("p (a b) -> p a b", a=2),
                                        n_tok[:, t, :].rearrange("p (a b) -> p a b", a=2),
                                        kvq[:, bass.ds(i * 2 + 6, 2), t, :], ALU.mult)
                k.then_inc(n_ready, 1)
                for kt in range(KT):
                    ahead(i * 2 * KT + CH_TL + KT, kt)
                    if kt in (1, 3, 5, 7):
                        b = kt // 2
                        dve.wait_ge(nt_hi, i * 4 + (b + 1))
                        at_ = bass.ds(i * 8 + 2 * b, 2)
                        v.tensor_tensor(nsa_lo[:, at_, :], ps[:, 6 + b % 2, :].rearrange("p (a b) -> p a b", a=2),
                                        up(nsa_hi[:, at_, :]), ALU.subtract).then_inc(nt_lo, 1)
                    pool_group(kt, i * 2 + 1)
                gate_leave(i, i * 2 * KT + (CH_TL + 2 * KT), i * 2 + (Q_TL + 1), lambda t: ys[:, bass.ds(i * -1 + 1, 1), t, :])

            def times(y, t):
                return v.tensor_tensor(y, y, ps[:, NH * t:NH * t + NH, :].rearrange("p a b -> p (a b)"), ALU.mult)

            def pool_leave(chunk_done, q, n, y):
                dve.wait_ge(gate_out, n * 4 + 4)
                dve.wait_ge(acc_done, q + 1)
                times(y(0), 0).then_inc(acc_free[0], 1)
                dve.wait_ge(weights_free, chunk_done + RING)
                times(y(1), 1).then_inc(acc_free[1], 1)

            def nsa_leave(chunk_done, q, y):
                dve.wait_ge(acc_done, q + 1)
                times(ys[:, 0, 0, :], 0).then_inc(acc_free[0], 1)
                dve.wait_ge(weights_free, chunk_done + RING)
                times(ys[:, 0, 1, :], 1).then_inc(acc_free[1], 1)
                for t in range(TT):
                    dve.wait_ge(acc_free[t], q + 2)
                    k = v.tensor_tensor(y(t), y(t), ys[:, 0, t, :], ALU.add)
                k.then_inc(y_sum, 1)

            with dve.Fori(0, N_Y - 1) as i:
                for kt in range(UT):
                    ahead(i * PER3 + CH_P3, kt)
                y = lambda t: ys[:, bass.ds(i + 1, 1), t, :]
                pool_leave(i * PER3 + (CH_P3 + UT), i * 4 + Q_P3, i, y)
                for kt in range(UT):
                    ahead(i * PER3 + CH_P3 + UT, kt)
                nsa_leave(i * PER3 + (CH_P3 + 2 * UT), i * 4 + (Q_P3 + 1), y)
                for which in range(2):
                    for kt in range(KT):
                        ahead(i * PER3 + CH_P3 + 2 * UT + which * KT, kt)
                    gate_leave(i * 2 + (2 + which), i * PER3 + (CH_P3 + 2 * UT + (which + 1) * KT),
                               i * 4 + (Q_P3 + 2 + which),
                               (lambda t: ys[:, bass.ds(i + 2, 1), t, :]) if which == 0 else (lambda t: ys[:, 0, t, :]))

            def turn_y(b):
                dve.wait_ge(yt_hi, b + 1)
                v.tensor_tensor(act_lo[:, 2 * b:2 * b + 2, :], ps[:, 4 + b % 4, :].rearrange("p (a b) -> p a b", a=2),
                                up(act_hi[:, 2 * b:2 * b + 2, :]), ALU.subtract).then_inc(yt_lo, 1)

            y_last = lambda t: ys[:, N_Y, t, :]
            for kt in range(2 * UT):
                ahead(CH_EP, kt)
                if kt % 2 == 1 and kt // 2 < 12:
                    turn_y(kt // 2)
                if kt == UT - 1:
                    pool_leave(CH_EP + UT, Q_EP, N_Y - 1, y_last)
            nsa_leave(CH_EP + 2 * UT, Q_EP + 1, y_last)

            def out_leave(q, chunk_done, xo):
                for t in range(TT):
                    if t == 0:
                        dve.wait_ge(acc_done, q + 1)
                    else:
                        dve.wait_ge(weights_free, chunk_done + RING)
                    v.tensor_tensor(xo(t), xo(t), ps[:, NH * t:NH * t + NH, :].rearrange("p a b -> p (a b)"),
                                    ALU.add).then_inc(acc_free[t], 1)

            for kt in range(KT):
                ahead(CH_P4, kt)
                if kt in LAST_Y:
                    turn_y(12 + LAST_Y.index(kt))
            dve.wait_ge(xo_landed, 16 * N_Y)
            out_leave(Q_P4, CH_P4 + KT, lambda t: x_out[:, 0, t, :])
            with dve.Fori(1, N_Y - 1) as i:
                for kt in range(KT):
                    ahead(i * KT + CH_P4, kt)
                out_leave(i + Q_P4, i * KT + (CH_P4 + KT), lambda t: x_out[:, bass.ds(i, 1), t, :])
            for kt in range(KT):
                ahead(CH_P4 + (N_Y - 1) * KT, kt, last=True)
            out_leave(Q_P4 + N_Y - 1, CHUNKS, lambda t: x_out[:, N_Y - 1, t, :])

        @block.tensor
        def _(pe):
            pe.sem_inc(weights_free, RING)
            mm, tr = nc.tensor.matmul, nc.tensor.transpose

            def product(first, q, hi, lo, side=None, tiles=None, before=None):
                tiles = tiles or hi.shape[1]
                for kt in range(tiles):
                    slot = kt % RING
                    if before:
                        before(kt)
                    pe.wait_ge(split_done, first + (kt + 1 + RING))
                    for t in range(TT):
                        if kt == 0:
                            pe.wait_ge(acc_free[t], q + 1)
                        for part, (a_, w_) in enumerate(((hi, w_hi), (hi, w_lo), (lo, w_hi))):
                            for n in range(NH):
                                m = mm(ps[:, NH * t + n, :], a_[:, kt, t * P:(t + 1) * P],
                                       w_[:, slot, n * BANK:(n + 1) * BANK],
                                       start=(kt == 0 and part == 0), stop=(kt == tiles - 1 and part == 2))
                        if kt == tiles - 1 and t == 0:
                            m.then_inc(acc_done, 1)
                    m.then_inc(weights_free, 1)
                    if side:
                        side(kt)

            pe.wait_ge(const_ready, 1)
            pe.wait_ge(vec_landed, 16 * 6)
            tr(ps[:, 7, 0:V_END], vec_rows[0:V_END, :], ident[0:V_END, 0:V_END]).then_inc(vec_psum, 1)
            pe.wait_ge(vec_ready, 1)

            def turn_x(b):
                if b % 4 == 0:
                    pe.wait_ge(x_landed[b // 4], 16)
                if b >= 4:
                    pe.wait_ge(xt_lo, b - 3)
                for e in range(2):
                    for t in range(TT):
                        k = tr(ps[:, 4 + b % 4, (2 * e + t) * P:(2 * e + t + 1) * P],
                               x_tok[:, t, (2 * b + e) * P:(2 * b + e + 1) * P], ident[:])
                k.then_inc(x_psum, 1)

            def turn_beside(kt):
                if kt % 2 == 0 and kt // 2 + 2 < KT // 2:
                    turn_x(kt // 2 + 2)

            turn_x(0)
            turn_x(1)
            product(0, 0, act_hi, act_lo, turn_beside,
                    before=lambda kt: kt % 2 == 0 and pe.wait_ge(xt_lo, kt // 2 + 1))
            with pe.Fori(1, N_A - 1) as i:
                product(i * KT, i, act_hi, act_lo)

            def gates_and_compression(kt):
                if kt == 0:
                    pe.wait_ge(wg_lo_done, 1)
                    pe.wait_ge(wg_padded, 2)
                if kt < KT // 2:
                    for g in (2 * kt, 2 * kt + 1):
                        for part, (w_, a_) in enumerate(((wg_hi, act_hi), (wg_lo, act_hi), (wg_hi, act_lo))):
                            k = mm(ps[:, 4, 0:T], w_[:, g * GATES:g * GATES + P], a_[:, g, :],
                                   start=(g == 0 and part == 0), stop=(g == KT - 1 and part == 2))
                if kt == KT // 2 - 1:
                    k.then_inc(gate_psum, 1)
                if kt == 18:
                    pe.wait_ge(gate_lin, 1)
                    for t in range(TT):
                        k = tr(ps[:, 5, t * GATES:(t + 1) * GATES], gate_t[:, t * P:(t + 1) * P],
                               ident[0:GATES, 0:GATES])
                    k.then_inc(gate_turned, 1)
                if kt in (2, 6):
                    n = (kt - 2) // 4
                    if n == 0:
                        pe.wait_ge(acc_free[0], 1 + 1)
                        pe.wait_ge(acc_free[1], 1 + 1)
                    else:
                        pe.wait_ge(ct_sbuf, 1)
                    for h in range(KVH):
                        for t in range(TT):
                            k = tr(ps[:, 6 + h // 2, ((h % 2) * TT + t) * P:((h % 2) * TT + t + 1) * P],
                                   kvq[:, n, t, h * HD:(h + 1) * HD], ident[:])
                    k.then_inc(ct_psum, 1)
                if 10 <= kt < 20:
                    if kt == 10:
                        pe.wait_ge(ct_sbuf, 2)
                        pe.wait_ge(w1_landed, 16 * 9)
                    js = range((kt - 10) * 16 // 5, (kt - 9) * 16 // 5)
                    for j in js:
                        late = j // CMP_STRIDE
                        for n, kb in enumerate((kb_k, kb_v)):
                            k = mm(ps[:, 6 + n, 0:(KVH + 1) * NC], w1[:, n, j, :],
                                   kb[:, j % CMP_STRIDE, :, late:late + NC],
                                   start=(j == 0), stop=(j == CMP_BLOCK - 1))
                    if kt == 19:
                        k.then_inc(hid_psum, 1)
                if kt == 24:
                    pe.wait_ge(hid_step, 5)
                    mm(ps[0:KVH * NC, 6, 128:256], hid[:, 0, :], w2[:, 0, :], start=True, stop=True)
                    for h in range(KVH):
                        k = mm(ps[0:NC, 7, h * HD:(h + 1) * HD], hid[:, 1, h * NC:(h + 1) * NC], w2[:, 1, :],
                               start=True, stop=True)
                    k.then_inc(w2_psum, 1)
                if kt == 27:
                    pe.wait_ge(kc_step, 4)
                    tr(ps[:, 6, 0:KVH * NC], kc_n[:], ident[0:KVH * NC, 0:KVH * NC]).then_inc(kct_psum, 1)

            product((N_A - 1) * KT, N_A - 1, act_hi, act_lo, gates_and_compression)
            pe.wait_ge(kct_ready, 1)
            pe.wait_ge(vc_ready, 1)
            pe.wait_ge(gate_ready, 2)

            with pe.Fori(0, KVH) as j:
                def attention(kt):
                    if kt == 2:
                        pe.wait_ge(qk_normed, j + 1)
                        pe.wait_ge(head_out, j * GQ + 1)
                        for m in range(6):
                            for t in range(TT):
                                k = tr(ps[:, 4 + m // 2, ((m % 2) * TT + t) * P:((m % 2) * TT + t + 1) * P],
                                       qk[:, t, m, :], ident[:])
                        k.then_inc(qkt_psum, 1)
                    if kt in SCORES:
                        h = SCORES.index(kt)
                        if h == 0:
                            pe.wait_ge(qkt_act, j + 1)
                            pe.wait_ge(qkt_dve, j + 1)
                        pe.wait_ge(head_out, j * GQ + (h + 1))
                        for br in range(2):
                            mm(ps[:, 4 + br, 0:P], qk_t[:, h, 0:P], qk_t[:, 4 + br, 0:P], start=True, stop=True)
                            mm(ps[:, 4 + br, P:3 * P], qk_t[:, h, P:2 * P], qk_t[:, 4 + br, :], start=True, stop=True)
                        for t in range(TT):
                            k = mm(ps[:, 4 + t, 3 * P:3 * P + NC], qk_t[:, h, t * P:(t + 1) * P],
                                   kc_t[:, bass.ds(j * NC, NC)], start=True, stop=True)
                        k.then_inc(scores_done, 1)
                    if kt in TURNS:
                        h = TURNS.index(kt)
                        pe.wait_ge(probs_ready, j * GQ + (h + 1))
                        for br in range(2):
                            for b in range(3):
                                tr(ps[:, 6 + br, b * P:(b + 1) * P], s[:, br, b * P:(b + 1) * P], ident[:])
                        for t in range(TT):
                            k = tr(ps[0:NC, 6 + t, 3 * P:4 * P], s_cmp[:, t, :], ident[:])
                        k.then_inc(probt_psum, 1)
                    if kt in VALUES:
                        h = VALUES.index(kt)
                        pe.wait_ge(probt_ready, j * GQ + (h + 1))
                        vals = lambda half, t: kvq[:, half, t, bass.ds(j * HD, HD)]
                        for t in range(TT):
                            o = ps[:, 4 + t, 3 * P:4 * P]
                            first = True
                            for br, half in ((0, 3), (1, 5)):
                                for kb in range(t + 1):
                                    mm(o, prob_t[:, br, (t + kb) * P:(t + kb + 1) * P], vals(half, kb),
                                       start=first, stop=False)
                                    first = False
                            k = mm(o, prob_ct[:, t, :], vc[:, bass.ds(j, 1), :], start=False, stop=True)
                        k.then_inc(pv_done, 1)

                product(j * KT + CH_L2, j + Q_L2, act_hi, act_lo, attention)

            def pool_group(kt, n):
                if kt == 9:
                    pe.wait_ge(band_built, 4 + sum(w - 1 for w in WINDOWS) + 24)
                    pe.wait_ge(uz_copied, n + 1)
                    for c in range(PG // P):
                        o = ps[:, 4 + c // 2, (c % 2) * T:(c % 2 + 1) * T]
                        mm(o[:, 0:P], u_g[:, 0, c * P:(c + 1) * P], band[:, bass.ds(n, 1), 0:P], start=True, stop=True)
                        mm(o[:, P:2 * P], u_g[:, 0, c * P:(c + 1) * P], band[:, bass.ds(n, 1), P:2 * P],
                           start=True, stop=False)
                        k = mm(o[:, P:2 * P], u_g[:, 1, c * P:(c + 1) * P], band[:, bass.ds(n, 1), 2 * P:3 * P],
                               start=False, stop=True)
                    k.then_inc(mix_psum, 1)
                    for c in range(PG // P):
                        for t in range(TT):
                            k = tr(ps[:, 6 + c // 2, ((c % 2) * TT + t) * P:((c % 2) * TT + t + 1) * P],
                                   z_g[:, t, c * P:(c + 1) * P], ident[:])
                    k.then_inc(zt_psum, 1)
                if 12 <= kt < 16:
                    d = kt - 12
                    if d == 0:
                        pe.wait_ge(mix_act, n + 1)
                        pe.wait_ge(mix_dve, n + 1)
                        pe.wait_ge(pw_landed, n * 16 + 16)
                    for c in range(PG // P):
                        k = mm(ps[:, 4 + d // 2, (d % 2) * T:(d % 2 + 1) * T], pw[:, c, d * P:(d + 1) * P],
                               mix_t[:, c, :], start=(c == 0), stop=(c == PG // P - 1))
                    if d % 2:
                        k.then_inc(pwt_psum, 1)

            with pe.Fori(0, 2) as i:
                product(i * 2 * KT + CH_TL, i * 2 + Q_TL, act_hi, act_lo, lambda kt: pool_group(kt, i * 2))

                def turn_and_pool(kt):
                    if kt in (1, 3, 5, 7):
                        b = kt // 2
                        if b == 0:
                            pe.wait_ge(n_ready, i + 1)
                            pe.wait_ge(pool_lo_done, i * 4 + 4)
                        pe.wait_ge(nt_lo, i * 4 + (b + 1))
                        for e in range(2):
                            for t in range(TT):
                                k = tr(ps[:, 6 + b % 2, (2 * e + t) * P:(2 * e + t + 1) * P],
                                       n_tok[:, t, (2 * b + e) * P:(2 * b + e + 1) * P], ident[:])
                        k.then_inc(nt_psum, 1)
                    if kt == 9:
                        pe.wait_ge(nt_lo, i * 4 + 6)
                    pool_group(kt, i * 2 + 1)

                product(i * 2 * KT + CH_TL + KT, i * 2 + (Q_TL + 1), act_hi, act_lo, turn_and_pool)

            pe.wait_ge(pool_lo_done, 2 + 8)
            pe.wait_ge(nt_lo, 2 + 8)
            with pe.Fori(0, N_Y - 1) as i:
                product(i * PER3 + CH_P3, i * 4 + Q_P3, pool_hi, pool_lo)
                product(i * PER3 + (CH_P3 + UT), i * 4 + (Q_P3 + 1), nsa_hi, nsa_lo)
                for which in range(2):
                    product(i * PER3 + (CH_P3 + 2 * UT + which * KT), i * 4 + (Q_P3 + 2 + which), act_hi, act_lo)

            def turn_y(b):
                g, e0 = b // 4, 2 * (b % 4)
                if b >= 4:
                    pe.wait_ge(yt_lo, b - 3)
                for e in range(2):
                    for t in range(TT):
                        k = tr(ps[:, 4 + b % 4, (2 * e + t) * P:(2 * e + t + 1) * P],
                               ys[:, 1 + g, t, (e0 + e) * P:(e0 + e + 1) * P], ident[:])
                k.then_inc(yt_psum, 1)

            def turn_from(start):
                def side(kt):
                    if (kt + start) % 2 == 1 and (kt + start) // 2 < 12:
                        if kt + start == 1:
                            pe.wait_ge(y_sum, N_Y - 1)
                        turn_y((kt + start) // 2)
                return side

            product(CH_EP, Q_EP, pool_hi, pool_lo, turn_from(0))
            product(CH_EP + UT, Q_EP + 1, nsa_hi, nsa_lo, turn_from(UT))

            def turn_last(kt):
                if kt in LAST_Y:
                    if kt == LAST_Y[0]:
                        pe.wait_ge(y_sum, N_Y)
                    turn_y(12 + LAST_Y.index(kt))

            product(CH_P4, Q_P4, act_hi, act_lo, turn_last,
                    before=lambda kt: kt in (0, 24) and pe.wait_ge(yt_lo, 12 if kt == 0 else 16))
            with pe.Fori(1, N_Y) as i:
                product(i * KT + CH_P4, i + Q_P4, act_hi, act_lo)


_INS = ["x", "norm_g", "w_in", "merge_bias", "pool_w", "pool_scale", "q_norm_g", "k_norm_g", "cmp_pe", "cmp_w1",
        "cmp_b1", "cmp_w2", "w_pool_up", "w_nsa_up", "w_out"]


def kernel(**inputs):
    import numpy as np
    from concourse import bacc
    from concourse.bass_utils import run_bass_kernel_spmd

    nc = bacc.Bacc("TRN2", target_bir_lowering=False, num_devices=1, dynamic_dma_scratch_size=1024)
    arrays, args = {}, []
    for name in _INS:
        a = np.ascontiguousarray(inputs[name])
        arrays[f"in_{name}"] = a
        args.append(nc.dram_tensor(f"in_{name}", a.shape, mybir.dt.from_np(a.dtype), kind="ExternalInput").ap())
    out = nc.dram_tensor("out_y", inputs["x"].shape, F32, kind="ExternalOutput").ap()
    trunk(nc, *args, out)
    r = run_bass_kernel_spmd(nc, [arrays], core_ids=[0])
    return r.results[0]["out_y"]
```

```python
import math

import concourse.bass as bass
from concourse import mybir
from concourse.alu_op_type import AluOpType as ALU

ACT = mybir.ActivationFunctionType
AX = mybir.AxisListType
F32 = mybir.dt.float32
F32R = mybir.dt.float32r

P = 128
BANK = 512
WIDTH = 1024
RING = 4
LEAD = 2
EPS = 1e-6
MASKED = -1e36
WINDOWS = (2, 4, 8, 16)
CMP_BLOCK, CMP_STRIDE = 32, 16


def trunk(nc, x, norm_g, w_in, merge_bias, pool_w, pool_scale, q_norm_g, k_norm_g, cmp_pe, cmp_w1,
          cmp_b1, cmp_w2, w_pool_up, w_nsa_up, w_out, out):
    _, T, D = x.shape
    HD = q_norm_g.shape[1]
    TT = T // P
    KT = D // P
    POOL = pool_scale.shape[1]
    PG = POOL // len(WINDOWS)
    QW = w_nsa_up.shape[1]
    H = QW // HD
    KVH = H // 4
    GQ = H // KVH
    KVW = KVH * HD
    NBR = 3
    NC = (T - CMP_BLOCK) // CMP_STRIDE + 1
    UT = POOL // P
    NH = WIDTH // BANK
    GATES = NBR * H
    assert (T, D, HD, KVH, PG, QW, KVW) == (256, 4096, 128, 4, 512, 2048, 512)

    COL_U, COL_Z = 0, POOL
    COL_Q = 2 * POOL
    COL_NZ = COL_Q + QW
    COL_KV = COL_NZ + QW
    COL_G = COL_KV + 6 * KVW
    COL_M = COL_G + GATES
    assert COL_Z == 2 * WIDTH

    N_PROJ = (6 * KVW + QW) // WIDTH
    CH_L2 = N_PROJ * KT
    CH_TL = CH_L2 + KVH * KT
    CH_P3 = CH_TL + 4 * KT
    PER3 = 2 * UT + 2 * KT
    N_Y = D // WIDTH
    CH_EP = CH_P3 + (N_Y - 1) * PER3
    CH_P4 = CH_EP + 2 * UT
    CHUNKS = CH_P4 + N_Y * KT
    Q_L2, Q_TL, Q_P3 = N_PROJ, N_PROJ + KVH, N_PROJ + KVH + 4
    Q_EP = Q_P3 + 4 * (N_Y - 1)
    Q_P4 = Q_EP + 2

    w_in, w_pu, w_nu, w_o = w_in[0], w_pool_up[0], w_nsa_up[0], w_out[0]
    x_pt = x[0].rearrange("(t p) c -> p t c", p=P)
    out_pt = out[0].rearrange("(t p) c -> p t c", p=P)

    at = [(nc.sbuf_base + 63) // 64 * 64]

    def region(size):
        start = at[0]
        at[0] += (size + 31) // 32 * 32
        return start

    def view(name, start, shape, dt=F32):
        return nc.alloc_sbuf_tensor_at(name, shape, dt, offset=start)

    def sized(name, shape, dt=F32):
        return view(name, region(4 * math.prod(shape[1:])), shape, dt)

    act_hi = sized("act_hi", [P, KT, T], F32R)
    act_lo = sized("act_lo", [P, KT, T], F32R)
    raw = sized("raw", [P, RING, WIDTH])
    w_hi = sized("w_hi", [P, RING, WIDTH], F32R)
    w_lo = sized("w_lo", [P, RING, WIDTH], F32R)
    ident = sized("ident", [P, P])
    vec_t = sized("vec_t", [P, P])
    rstd = sized("rstd", [P, TT])
    row_parts = sized("row_parts", [P, TT, N_Y])
    row_ss = sized("row_ss", [P, TT])
    neg_half = sized("neg_half", [P, 2 * TT * KVH])
    scale_g = sized("scale_g", [P, 4])
    band_x = sized("band_x", [P, 4, max(WINDOWS)])
    bias_at = region(4 * WIDTH)
    bias = view("bias", bias_at, [P, WIDTH])
    vec_rows = view("vec_rows", bias_at, [P, P])
    sq_a = view("sq_a", bias_at, [P, TT * KVH, HD])
    reg_a = region(32768)
    reg_t = region(16384)
    reg_k = region(24576)
    reg_q = region(16384)
    reg_n = region(16384)
    assert at[0] <= nc.sbuf_usable_end, (at[0], nc.sbuf_usable_end)

    x_tok = view("x_tok", reg_a, [P, TT, D])
    w1 = view("w1", reg_a, [P, 2, CMP_BLOCK, HD])
    uz = view("uz", reg_a, [P, 8, TT, PG])
    pool_hi = view("pool_hi", reg_a, [P, UT, T], F32R)
    pool_lo = view("pool_lo", reg_a + 16384, [P, UT, T], F32R)
    x_out = view("x_out", reg_a, [P, N_Y, TT, WIDTH])
    ys = view("ys", reg_t, [P, 1 + N_Y, TT, WIDTH])
    kvq = view("kvq", reg_k, [P, 6 + KVH, TT, KVW])
    nsa_hi = view("nsa_hi", reg_q, [P, UT, T], F32R)
    nsa_lo = view("nsa_lo", reg_n, [P, UT, T], F32R)
    u_g = view("u_g", reg_k, [P, TT, PG])
    mix_hi = view("mix_hi", reg_k, [P, PG // P, T], F32R)
    z_g = view("z_g", reg_k + 4096, [P, TT, PG])
    silu_zt = view("silu_zt", reg_k + 4096, [P, PG // P, T])
    pw = view("pw", reg_k + 8192, [P, PG // P, PG])
    pw_lo = view("pw_lo", reg_k + 8192, [P, PG // P, PG], F32R)
    pw_hi = view("pw_hi", reg_k + 16384, [P, PG // P, PG], F32R)
    n_tok = view("n_tok", reg_k + 16384, [P, TT, WIDTH])
    band = view("band", reg_t, [P, 4, TT, P])
    mix_lo = view("mix_lo", reg_t + 4096, [P, PG // P, T], F32R)
    t_at = [reg_t]

    def in_t(name, shape, dt=F32):
        start = t_at[0]
        t_at[0] += (4 * math.prod(shape[1:]) + 31) // 32 * 32
        assert t_at[0] <= reg_t + 16384, name
        return view(name, start, shape, dt)

    n_at = [reg_n]

    def in_n(name, shape, dt=F32):
        start = n_at[0]
        n_at[0] += (4 * math.prod(shape[1:]) + 31) // 32 * 32
        assert n_at[0] <= reg_n + 16384, name
        return view(name, start, shape, dt)

    dist = in_t("dist", [P, GQ, 3 * P])
    dist_c = in_t("dist_c", [P, GQ, TT, NC])
    kc_t = in_t("kc_t", [P, KVH * NC])
    vc = in_t("vc", [NC, KVH, HD])
    gate6 = in_t("gate6", [P, H, 6])
    row_mask = in_t("row_mask", [P, 1])
    k_ss = in_t("k_ss", [P, 2, TT, KVH])
    k_rs = in_t("k_rs", [P, 2, TT, KVH])
    q_ss = in_t("q_ss", [P, TT, GQ])
    q_rs = in_t("q_rs", [P, TT, GQ])
    t_mark = t_at[0]
    neg_max = in_t("neg_max", [P, 6])
    sums = in_t("sums", [P, 6])
    inv = in_t("inv", [P, 6])
    wgt = in_t("wgt", [P, 6])
    s_cmp = in_t("s_cmp", [P, TT, NC])
    prob_ct = in_t("prob_ct", [NC, TT, P])
    prob_t = in_t("prob_t", [P, 2, 3 * P])
    qk = in_n("qk", [P, TT, 6, HD])
    qk_t = in_n("qk_t", [P, 6, T])
    s = in_n("s", [P, 2, 3 * P])
    WG = KT * GATES
    PAD = P - GATES
    wg = view("wg", reg_n, [P, WG])
    kb_v = view("kb_v", reg_n, [P, CMP_STRIDE, KVH + 1, CMP_STRIDE])
    wg_hi = view("wg_hi", reg_n + 6144, [P, WG + PAD], F32R)
    kb_k = view("kb_k", reg_q + 8192, [P, CMP_STRIDE, KVH + 1, CMP_STRIDE])
    wg_lo = view("wg_lo", reg_t + 16384 - 6464, [P, WG + PAD], F32R)
    assert t_mark <= reg_t + 16384 - 6464
    gate_t = view("gate_t", reg_n + 6144, [GATES, T])
    after = [reg_n + 6144 + 6464]

    def behind(name, shape):
        start = after[0]
        after[0] += (4 * math.prod(shape[1:]) + 31) // 32 * 32
        assert after[0] <= reg_n + 16384, name
        return view(name, start, shape)

    w2 = behind("w2", [P, 2, HD])
    hid_b = behind("hid_b", [P, 2])
    hid_x = behind("hid_x", [P, 2, KVH * NC])
    hid_s = behind("hid_s", [P, 2, KVH * NC])
    hid = behind("hid", [P, 2, KVH * NC])
    kc_n = behind("kc_n", [KVH * NC, HD])
    kc_sq = behind("kc_sq", [KVH * NC, HD])
    kc_ss = behind("kc_ss", [KVH * NC, 1])
    kc_rs = behind("kc_rs", [KVH * NC, 1])

    V_NORM = 0
    V_SCALE = V_NORM + KT
    V_QG = V_SCALE + UT
    V_KG = V_QG + 1
    V_PE = V_KG + NBR
    V_B1 = V_PE + 2 * CMP_BLOCK
    V_END = V_B1 + 2

    ps = nc.alloc_psum_tensor("ps", [P, 8, BANK], F32)

    BAND_STEPS = sum(WINDOWS) + (4 + TT) * len(WINDOWS)

    def sem(name):
        return nc.alloc_semaphore(name)

    norm_landed = sem("norm_landed")
    vec_landed = sem("vec_landed")
    X_CUTS = [0, 2 * P, 4 * P, WIDTH, 2 * WIDTH, 3 * WIDTH, D]
    x_landed = [sem(f"x_landed{i}") for i in range(len(X_CUTS) - 1)]
    raw_landed = [sem(f"raw_landed{i}") for i in range(RING)]
    wg_landed = sem("wg_landed")
    w1_landed = sem("w1_landed")
    bias_landed = sem("bias_landed")
    pw_landed = sem("pw_landed")
    xo_landed = sem("xo_landed")
    out_stored = sem("out_stored")
    hi_done = sem("hi_done")
    split_done = sem("split_done")
    weights_free = sem("weights_free")
    acc_done = sem("acc_done")
    acc_free = [sem("acc_free0"), sem("acc_free1")]
    const_pool = sem("const_pool")
    const_ready = sem("const_ready")
    band_built = sem("band_built")
    vec_psum = sem("vec_psum")
    vec_ready = sem("vec_ready")
    x_psum = sem("x_psum")
    xt_hi = sem("xt_hi")
    xt_lo = sem("xt_lo")
    sq_act = sem("sq_act")
    sq_dve = sem("sq_dve")
    row_sum = sem("row_sum")
    row_ms = sem("row_ms")
    rstd_ready = sem("rstd_ready")
    wg_hi_done = sem("wg_hi_done")
    wg_lo_done = sem("wg_lo_done")
    ct_psum = sem("ct_psum")
    ct_sbuf = sem("ct_sbuf")
    kb_zero = sem("kb_zero")
    kb_pos = sem("kb_pos")
    hid_psum = sem("hid_psum")
    hid_step = sem("hid_step")
    hid_sig = sem("hid_sig")
    w2_psum = sem("w2_psum")
    kc_step = sem("kc_step")
    kc_rstd = sem("kc_rstd")
    kct_psum = sem("kct_psum")
    kct_ready = sem("kct_ready")
    vc_ready = sem("vc_ready")
    gate_psum = sem("gate_psum")
    gate_sig = sem("gate_sig")
    gate_ready = sem("gate_ready")
    qk_sq = sem("qk_sq")
    qk_ss = sem("qk_ss")
    gate_lin = sem("gate_lin")
    gate_turned = sem("gate_turned")
    wg_padded = sem("wg_padded")
    k_ms = sem("k_ms")
    k_rstd = sem("k_rstd")
    q_ms = sem("q_ms")
    q_rstd = sem("q_rstd")
    qk_normed = sem("qk_normed")
    qkt_psum = sem("qkt_psum")
    qkt_act = sem("qkt_act")
    qkt_dve = sem("qkt_dve")
    scores_done = sem("scores_done")
    biased = sem("biased")
    head_max = sem("head_max")
    exp_done = sem("exp_done")
    inv_done = sem("inv_done")
    wgt_done = sem("wgt_done")
    probs_ready = sem("probs_ready")
    probt_psum = sem("probt_psum")
    probt_ready = sem("probt_ready")
    pv_done = sem("pv_done")
    head_out = sem("head_out")
    nz_sig = sem("nz_sig")
    n_ready = sem("n_ready")
    nt_psum = sem("nt_psum")
    nt_hi = sem("nt_hi")
    nt_lo = sem("nt_lo")
    gate_out = sem("gate_out")
    uz_copied = sem("uz_copied")
    mix_psum = sem("mix_psum")
    mix_hi_done = sem("mix_hi_done")
    mix_lo_done = sem("mix_lo_done")
    pw_hi_done = sem("pw_hi_done")
    pw_lo_done = sem("pw_lo_done")
    zt_psum = sem("zt_psum")
    zt_sig = sem("zt_sig")
    zt_silu = sem("zt_silu")
    pwt_psum = sem("pwt_psum")
    pool_v = sem("pool_v")
    pool_hi_done = sem("pool_hi_done")
    pool_lo_done = sem("pool_lo_done")
    y_sum = sem("y_sum")
    yt_psum = sem("yt_psum")
    yt_hi = sem("yt_hi")
    yt_lo = sem("yt_lo")

    SCORES = [4 + 7 * h for h in range(GQ)]
    EXPS = [5 + 7 * h for h in range(GQ)]
    SCALES = [6 + 7 * h for h in range(GQ)]
    TURNS = [8 + 7 * h for h in range(GQ)]
    VALUES = [10 + 7 * h for h in range(GQ)]
    PW_SPLITS = [8, 10]
    POOL_MIX = 9
    POOL_PRODUCTS = [13, 14, 15, 16]
    POOL_ENDS = POOL_PRODUCTS[1::2]
    LAST_Y = [1, 3, 5, 7, 9]
    EARLY_Y = [kt for kt in range(1, 2 * UT, 2) if kt != UT - 1][:KT // 2 - len(LAST_Y)]
    SMALL_AT = KT - 3

    def up(v):
        return v.bitcast(F32)

    block = nc.Block()
    with block:

        @block.sync
        def _(sp):
            def load(first, rows, cols, beside=()):
                for kt in range(rows.shape[0] // P):
                    if kt in beside:
                        beside[kt]()
                    sp.wait_ge(split_done, first + (kt + 1))
                    sp.dma_start(raw[:, kt % RING, :], rows[kt * P:(kt + 1) * P, cols]).then_inc(
                        raw_landed[kt % RING], 16)

            def load_x(i):
                c = slice(X_CUTS[i], X_CUTS[i + 1])
                sp.dma_start(x_tok[:, :, c], x_pt[:, :, c]).then_inc(x_landed[i], 16)

            small = (
                (V_SCALE, pool_scale[0].rearrange("(a b) -> a b", b=P)),
                (V_QG, q_norm_g),
                (V_KG, k_norm_g[0]),
                (V_PE, cmp_pe[0].rearrange("a j d -> (a j) d")),
                (V_B1, cmp_b1[0]),
            )

            def load_small():
                for start, rows in small:
                    sp.dma_start(vec_rows[start:start + rows.shape[0], :], rows).then_inc(vec_landed, 16)

            load_x(0)
            sp.dma_start(vec_rows[V_NORM:V_NORM + KT, :], norm_g[0].rearrange("(a b) -> a b", b=P)).then_inc(
                norm_landed, 16)
            load(0, w_in, slice(COL_KV, COL_KV + WIDTH),
                 {1: lambda: load_x(1), 2: lambda: load_x(2), 3: lambda: load_x(3), 6: lambda: load_x(4),
                  12: lambda: load_x(5), 16: load_small})

            wg_cols = w_in[:, COL_G:COL_G + GATES].rearrange("(k p) n -> p k n", p=P)

            def load_wg(k):
                n = KT // 8
                sp.dma_start(wg[:, k * n * GATES:(k + 1) * n * GATES].rearrange("p (k n) -> p k n", n=GATES),
                             wg_cols[:, k * n:(k + 1) * n, :]).then_inc(wg_landed, 16)

            def load_w1(n):
                if n == 0:
                    sp.wait_ge(sq_act, N_Y)
                    sp.wait_ge(sq_dve, N_Y)
                    sp.wait_ge(xt_lo, KT // 2)
                kv, j = n // 4, n % 4 * 8
                sp.dma_start(w1[:, kv, j:j + 8, :], cmp_w1[0, kv, j * HD:(j + 8) * HD, :].rearrange(
                    "(j d) e -> d j e", d=HD)).then_inc(w1_landed, 16)

            def load_w2():
                sp.dma_start(w2[:], cmp_w2[0].rearrange("a e f -> e a f")).then_inc(w1_landed, 16)

            load(KT, w_in, slice(COL_KV + WIDTH, COL_KV + 2 * WIDTH),
                 {8 + 3 * k: (lambda k=k: load_wg(k)) for k in range(8)})
            load(2 * KT, w_in, slice(COL_KV + 2 * WIDTH, COL_KV + 3 * WIDTH),
                 {4 + 3 * n: (lambda n=n: load_w1(n)) for n in range(8)} | {28: load_w2})
            with sp.Fori(0, 2) as i:
                load(i * KT + 3 * KT, w_in, bass.ds(i * WIDTH + COL_Q, WIDTH))
            with sp.Fori(0, KVH) as i:
                load(i * KT + CH_L2, w_in, bass.ds(i * WIDTH + COL_U, WIDTH))

            def load_pool_w(n):
                sp.wait_ge(head_out, 1 + H)
                sp.wait_ge(pool_lo_done, n * 2 + 2)
                sp.dma_start(pw[:], pool_w[0, bass.ds(n, 1)].rearrange("g (c p) d -> p (g c) d", p=P)).then_inc(
                    pw_landed, 16)

            def load_bias(which, col, left, between=None):
                sp.wait_ge(acc_free[1], left)
                sp.wait_ge(vec_ready, 2)
                if between:
                    between()
                sp.dma_start(bias[:], merge_bias[0, which, bass.ds(col, WIDTH)].to_broadcast([P, WIDTH])).then_inc(
                    bias_landed, 16)

            with sp.Fori(0, 2) as i:
                load(i * 2 * KT + CH_TL, w_in, bass.ds(i * WIDTH + COL_NZ, WIDTH), {8: lambda: load_pool_w(i * 2)})

                def beside():
                    load_bias(bass.ds(i, 1), 0, i * 2 + (Q_TL + 1), lambda: load_pool_w(i * 2 + 1))

                load(i * 2 * KT + CH_TL + KT, w_in, bass.ds(i * D + COL_M, WIDTH), {8: beside})
            with sp.Fori(0, N_Y - 1) as i:
                load(i * PER3 + CH_P3, w_pu, bass.ds(i * WIDTH, WIDTH))
                load(i * PER3 + CH_P3 + UT, w_nu, bass.ds(i * WIDTH, WIDTH))
                for which in range(2):
                    load(i * PER3 + CH_P3 + 2 * UT + which * KT, w_in,
                         bass.ds(i * WIDTH + COL_M + which * D + WIDTH, WIDTH),
                         {8: lambda: load_bias(slice(which, which + 1), i * WIDTH + WIDTH,
                                               i * 4 + (Q_P3 + 1 + 3 * which))})
            load(CH_EP, w_pu, slice((N_Y - 1) * WIDTH, N_Y * WIDTH))
            load(CH_EP + UT, w_nu, slice((N_Y - 1) * WIDTH, N_Y * WIDTH))

            def load_residual(g):
                sp.wait_ge(weights_free, CH_EP + UT + RING)
                sp.dma_start(x_out[:, g], x_pt[:, :, g * WIDTH:(g + 1) * WIDTH]).then_inc(xo_landed, 16)

            load(CH_P4, w_o, slice(0, WIDTH), {5 + 6 * g: (lambda g=g: load_residual(g)) for g in range(N_Y)})
            with sp.Fori(1, N_Y) as i:
                load(i * KT + CH_P4, w_o, bass.ds(i * WIDTH, WIDTH))

        @block.gpsimd
        def _(pool):
            g = nc.gpsimd
            g.memset(ident[:], 0.0).then_inc(const_pool, 1)
            g.memset(neg_half[:], -0.5).then_inc(const_pool, 1)
            g.memset(row_mask[:], 1.0).then_inc(const_pool, 1)
            pool.wait_ge(const_pool, 3)
            g.affine_select(out=ident[:], in_=ident[:], compare_op=ALU.not_equal, fill=1.0, base=0,
                            pattern=[[-1, P]], channel_multiplier=1).then_inc(const_ready, 1)
            g.affine_select(out=row_mask[:], in_=row_mask[:], compare_op=ALU.is_ge, fill=0.0,
                            base=1 - CMP_BLOCK, pattern=[[0, 1]], channel_multiplier=1).then_inc(const_ready, 1)
            g.iota(dist[:, 0, 0:P], [[1, P]], base=0, channel_multiplier=-1,
                   allow_small_or_imprecise_dtypes=True).then_inc(const_pool, 1)
            g.iota(dist[:, 0, P:3 * P], [[1, 2 * P]], base=-P, channel_multiplier=-1,
                   allow_small_or_imprecise_dtypes=True).then_inc(const_pool, 1)
            g.iota(dist_c[:, 0], [[-P, TT], [CMP_STRIDE, NC]], base=CMP_BLOCK - 1, channel_multiplier=-1,
                   allow_small_or_imprecise_dtypes=True).then_inc(const_pool, 1)
            pool.wait_ge(const_pool, 6)
            for h in reversed(range(GQ)):
                slope = 2.0 ** (-8.0 * (h + 1) / H)
                if h == 0:
                    pool.wait_ge(const_pool, 6 + 2 * (GQ - 1))
                g.tensor_scalar(dist[:, h], dist[:, 0], slope, None, ALU.mult).then_inc(const_pool, 1)
                g.tensor_scalar(dist_c[:, h], dist_c[:, 0], slope, None, ALU.mult).then_inc(const_pool, 1)
            pool.wait_ge(const_pool, 6 + 2 * GQ)
            g.affine_select(out=dist[:, :, 0:P], in_=dist[:, :, 0:P], compare_op=ALU.is_ge, fill=MASKED,
                            base=0, pattern=[[0, GQ], [-1, P]], channel_multiplier=1).then_inc(const_ready, 1)
            g.affine_select(out=dist[:, :, P:3 * P], in_=dist[:, :, P:3 * P], compare_op=ALU.is_ge, fill=MASKED,
                            base=P, pattern=[[0, GQ], [-1, 2 * P]], channel_multiplier=1).then_inc(const_ready, 1)
            g.affine_select(out=dist_c[:], in_=dist_c[:], compare_op=ALU.is_ge, fill=MASKED,
                            base=1 - CMP_BLOCK, pattern=[[0, GQ], [P, TT], [-CMP_STRIDE, NC]],
                            channel_multiplier=1).then_inc(const_ready, 1)
            pool.wait_ge(row_ms, 1)
            g.tensor_tensor(rstd[:], row_ss[:], neg_half[:, 0:TT], ALU.pow).then_inc(rstd_ready, 1)
            pool.wait_ge(kc_step, 3)
            g.tensor_tensor(kc_rs[:], kc_ss[:], neg_half[0:KVH * NC, 0:1], ALU.pow).then_inc(kc_rstd, 1)
            pool.wait_ge(k_ms, 1)
            flat = "p a t h -> p (a t h)"
            g.tensor_tensor(k_rs[:].rearrange(flat), k_ss[:].rearrange(flat), neg_half[:], ALU.pow).then_inc(k_rstd, 1)
            flat = "p t h -> p (t h)"
            pool.wait_ge(q_ms, 1)
            g.tensor_tensor(q_rs[:].rearrange(flat), q_ss[:].rearrange(flat), neg_half[:, 0:TT * GQ],
                            ALU.pow).then_inc(q_rstd, 1)
            with pool.Fori(0, KVH) as j:
                pool.wait_ge(q_ms, j + 2)
                g.tensor_tensor(q_rs[:].rearrange(flat), q_ss[:].rearrange(flat), neg_half[:, 0:TT * GQ],
                                ALU.pow).then_inc(q_rstd, 1)
            pool.wait_ge(acc_free[0], 1 + Q_TL)
            pool.wait_ge(acc_free[1], 1 + Q_TL)
            for n, w in enumerate(WINDOWS):
                g.memset(band[:, n], 1.0 / w).then_inc(band_built, 1)
                g.memset(band_x[:, n], 1.0 / w).then_inc(band_built, 1)
            done = 2 * len(WINDOWS)
            pool.wait_ge(band_built, done)
            for n, w in enumerate(WINDOWS):
                for t in range(w - 1):
                    g.memset(band[:, n, 0, t:t + 1], 1.0 / (t + 1)).then_inc(band_built, 1)
                g.affine_select(out=band_x[:, n], in_=band_x[:, n], compare_op=ALU.is_ge, fill=0.0, base=w - 1 - P,
                                pattern=[[-1, max(WINDOWS)]], channel_multiplier=1).then_inc(band_built, 1)
            done += sum(WINDOWS)
            pool.wait_ge(band_built, done)
            for n, w in enumerate(WINDOWS):
                g.affine_select(out=band[:, n], in_=band[:, n], compare_op=ALU.is_ge, fill=0.0, base=0,
                                pattern=[[0, TT], [1, P]], channel_multiplier=-1).then_inc(band_built, 1)
            done += len(WINDOWS)
            pool.wait_ge(band_built, done)
            for n, w in enumerate(WINDOWS):
                g.affine_select(out=band[:, n], in_=band[:, n], compare_op=ALU.is_ge, fill=0.0, base=w - 1,
                                pattern=[[0, TT], [-1, P]], channel_multiplier=1).then_inc(band_built, 1)
            done += len(WINDOWS)
            pool.wait_ge(band_built, done)
            for n in range(len(WINDOWS)):
                for t in range(TT):
                    g.tensor_tensor(band[:, n, t], band[:, n, t], ident[:], ALU.subtract).then_inc(band_built, 1)
            assert done + len(WINDOWS) * TT == BAND_STEPS
            with pool.Fori(0, 2) as i:
                for half in range(2):
                    pool.wait_ge(pool_lo_done, i * 4 + 2 * half + 2)
                    g.tensor_copy(u_g[:], uz[:, bass.ds(i * 2 + half, 1)])
                    g.tensor_copy(z_g[:], uz[:, bass.ds(i * 2 + half + 4, 1)])
                    g.tensor_copy(scale_g[:], vec_t[:, bass.ds(i * 8 + 4 * half + V_SCALE, 4)]).then_inc(uz_copied, 1)

        @block.scalar
        def _(act):
            a = nc.scalar

            def ahead(first, kt, last=False):
                if last and kt >= KT - LEAD:
                    return
                slot = (kt + LEAD) % RING
                act.wait_ge(weights_free, first + (kt + LEAD + 1))
                act.wait_ge(raw_landed[slot], first * 4 + ((kt + LEAD) // RING * 16 + 16))
                a.activation(w_hi[:, slot, :], raw[:, slot, :], ACT.Copy).then_inc(hi_done, 1)

            def turn_x(b):
                act.wait_ge(x_psum, b + 1)
                for e in range(2):
                    k = a.activation(act_hi[:, 2 * b + e, :], ps[:, 4 + b % 4, e * T:(e + 1) * T], ACT.Copy,
                                     scale=vec_t[:, V_NORM + 2 * b + e:V_NORM + 2 * b + e + 1])
                k.then_inc(xt_hi, 1)

            act.wait_ge(const_pool, 2)
            a.activation(row_parts[:, 0, 0:1], neg_half[:, 0:1], ACT.Copy)
            act.wait_ge(vec_ready, 1)
            turn_x(0)
            for c in range(LEAD):
                act.wait_ge(raw_landed[c], 16)
                a.activation(w_hi[:, c, :], raw[:, c, :], ACT.Copy).then_inc(hi_done, 1)
            turn_x(1)

            def leave(q, dst):
                act.wait_ge(acc_done, q + 1)
                a.activation(dst, ps[:, 0:NH, :], ACT.Copy, scale=rstd[:, 0:1]).then_inc(acc_free[0], 1)

            for kt in range(KT):
                ahead(0, kt)
                if kt % 2 == 0 and kt // 2 + 2 < KT // 2:
                    turn_x(kt // 2 + 2)
                if kt % 8 == 5:
                    c = kt // 8
                    act.wait_ge(xt_lo, 4 * c + 4)
                    piece = x_tok[:, 0, c * WIDTH:(c + 1) * WIDTH]
                    a.activation(piece, piece, ACT.Square, accum_out=row_parts[:, 0, c:c + 1]).then_inc(sq_act, 1)
            act.wait_ge(rstd_ready, 1)
            leave(0, kvq[:, 0:2, 0, :])

            with act.Fori(1, N_PROJ - 1) as i:
                for kt in range(KT):
                    ahead(i * KT, kt)
                leave(i, kvq[:, bass.ds(i * 2, 2), 0, :])

            def square(src):
                a.activation(sq_a[:], src.rearrange("p t (h d) -> p (t h) d", d=HD), ACT.Square).then_inc(qk_sq, 1)

            base = (N_PROJ - 1) * KT
            for kt in range(KT):
                if kt == 0:
                    act.wait_ge(wg_landed, 16 * 8)
                    a.activation(wg_hi[:, 0:WG], wg[:], ACT.Copy).then_inc(wg_hi_done, 1)
                ahead(base, kt)
                if kt in (2, 6):
                    n = (kt - 2) // 4
                    kb = (kb_k, kb_v)[n]
                    act.wait_ge(ct_psum, n + 1)
                    act.wait_ge(kb_pos, n + 1)
                    for half in range(2):
                        k = a.activation(
                            kb[:, :, 2 * half:2 * half + 2, :].rearrange("p r h c -> p h c r"),
                            ps[:, 6 + half, :].rearrange("p (h c r) -> p h c r", h=2, r=CMP_STRIDE), ACT.Copy)
                    k.then_inc(ct_sbuf, 1)
                if kt in (8, 10, 12):
                    n = (kt - 8) // 2
                    act.wait_ge(acc_free[0], N_PROJ)
                    act.wait_ge(acc_free[1], N_PROJ)
                    if n:
                        act.wait_ge(qk_ss, n)
                    square(kvq[:, 2 + 2 * n])
                if kt == 16:
                    act.wait_ge(gate_psum, 1)
                    a.activation(gate_t[:], ps[0:GATES, 4, 0:T], ACT.Copy).then_inc(gate_lin, 1)
                if kt == 19:
                    act.wait_ge(gate_turned, 1)
                    lin = ps[:, 5, 0:TT * GATES].rearrange("p (t h b) -> p t h b", t=TT, b=NBR)
                    for t in range(TT):
                        a.activation(gate6[:, :, 2 * t:2 * t + 2], lin[:, t, :, 1:3], ACT.Sigmoid, scale=rstd[:, t:t + 1])
                        k = a.activation(gate6[:, :, 4 + t], lin[:, t, :, 0], ACT.Sigmoid, scale=rstd[:, t:t + 1])
                    k.then_inc(gate_sig, 1)
                if kt == 22:
                    act.wait_ge(hid_step, 4)
                    a.activation(hid_s[:], hid_x[:], ACT.Sigmoid).then_inc(hid_sig, 1)
                if kt == 24:
                    act.wait_ge(w2_psum, 1)
                    a.activation(vc[:], ps[0:NC, 7, :].rearrange("p (h d) -> p h d", h=KVH), ACT.Copy).then_inc(vc_ready, 1)
            leave(N_PROJ - 1, kvq[:, 2 * (N_PROJ - 1):2 * N_PROJ, 0, :])
            act.wait_ge(acc_free[0], 1 + N_PROJ)
            act.wait_ge(acc_free[1], 1 + N_PROJ)

            with act.Fori(0, KVH) as j:
                for kt in range(KT):
                    ahead(j * KT + CH_L2, kt)
                    if kt == 2:
                        act.wait_ge(qkt_psum, j + 1)
                        a.activation(qk_t[:, 4, :], ps[:, 6, 0:T], ACT.Copy, scale=vec_t[:, V_KG + 1:V_KG + 2])
                        a.activation(qk_t[:, 5, :], ps[:, 6, T:2 * T], ACT.Copy,
                                     scale=vec_t[:, V_KG + 2:V_KG + 3]).then_inc(qkt_act, 1)
                    if kt == 13:
                        act.wait_ge(head_out, j * GQ + 2)
                        act.wait_ge(qk_ss, j + 3)
                        square(kvq[:, bass.ds((j + 1) % KVH + 6, 1)].rearrange("p a t c -> p (a t) c"))
                    if kt in EXPS:
                        h = EXPS.index(kt)
                        act.wait_ge(head_max, j * GQ + (h + 1))
                        for br in range(2):
                            a.activation(s[:, br, 0:P], s[:, br, 0:P], ACT.Exp, bias=neg_max[:, br:br + 1],
                                         accum_out=sums[:, br:br + 1])
                            a.activation(s[:, br, P:3 * P], s[:, br, P:3 * P], ACT.Exp, bias=neg_max[:, 2 + br:3 + br],
                                         accum_out=sums[:, 2 + br:3 + br])
                        for t in range(TT):
                            k = a.activation(s_cmp[:, t, :], s_cmp[:, t, :], ACT.Exp, bias=neg_max[:, 4 + t:5 + t],
                                             accum_out=sums[:, 4 + t:5 + t])
                        k.then_inc(exp_done, 1)
                    if kt in TURNS:
                        h = TURNS.index(kt)
                        act.wait_ge(probt_psum, j * GQ + (h + 1))
                        a.activation(prob_t[:], ps[:, 6:8, 0:3 * P], ACT.Copy)
                        a.activation(prob_ct[:], ps[0:NC, 6:8, 3 * P:4 * P], ACT.Copy).then_inc(probt_ready, 1)
                leave(j + Q_L2, uz[:, bass.ds(j * 2, 2), 0, :])

            def pool_group(kt, n):
                if kt == POOL_MIX:
                    act.wait_ge(mix_psum, n + 1)
                    for half in range(2):
                        a.activation(mix_hi[:, 2 * half:2 * half + 2, :], ps[:, 4 + half, :], ACT.Copy).then_inc(
                            mix_hi_done, 1)
                    act.wait_ge(zt_psum, n + 1)
                    for half in range(2):
                        a.activation(silu_zt[:, 2 * half:2 * half + 2, :], ps[:, 6 + half, :],
                                     ACT.Sigmoid).then_inc(zt_sig, 1)
                if kt in PW_SPLITS:
                    c = slice(2 * PW_SPLITS.index(kt), 2 * PW_SPLITS.index(kt) + 2)
                    act.wait_ge(pw_landed, n * 16 + 16)
                    a.activation(pw_hi[:, c, :], pw[:, c, :], ACT.Copy).then_inc(pw_hi_done, 1)
                if kt in POOL_ENDS:
                    b = POOL_ENDS.index(kt)
                    act.wait_ge(pool_v, n * 2 + (b + 1))
                    a.activation(pool_hi[:, bass.ds(n * 4 + 2 * b, 2), :], silu_zt[:, 2 * b:2 * b + 2, :],
                                 ACT.Copy).then_inc(pool_hi_done, 1)

            with act.Fori(0, 2) as i:
                for kt in range(KT):
                    ahead(i * 2 * KT + CH_TL, kt)
                    pool_group(kt, i * 2)
                for t in range(TT):
                    if t == 0:
                        act.wait_ge(acc_done, i * 2 + (Q_TL + 1))
                    else:
                        act.wait_ge(weights_free, i * 2 * KT + (CH_TL + KT + RING))
                    a.activation(n_tok[:, t, :], ps[:, NH * t:NH * t + NH, :], ACT.Sigmoid,
                                 scale=rstd[:, t:t + 1]).then_inc(nz_sig, 1)
                for kt in range(KT):
                    ahead(i * 2 * KT + CH_TL + KT, kt)
                    if kt in (1, 3, 5, 7):
                        b = kt // 2
                        act.wait_ge(nt_psum, i * 4 + (b + 1))
                        a.activation(nsa_hi[:, bass.ds(i * 8 + 2 * b, 2), :], ps[:, 6 + b % 2, :],
                                     ACT.Copy).then_inc(nt_hi, 1)
                    pool_group(kt, i * 2 + 1)
                for t in range(TT):
                    act.wait_ge(acc_free[t], i * 2 + (Q_TL + 3))
                    y = ys[:, bass.ds(i * -1 + 1, 1), t, :]
                    a.activation(y, y, ACT.Sigmoid).then_inc(gate_out, 1)

            with act.Fori(0, N_Y - 1) as i:
                for kt in range(2 * UT):
                    ahead(i * PER3 + CH_P3, kt)
                for which in range(2):
                    for kt in range(KT):
                        ahead(i * PER3 + CH_P3 + 2 * UT + which * KT, kt)
                    for t in range(TT):
                        act.wait_ge(acc_free[t], i * 4 + (Q_P3 + 4 + which))
                        y = ys[:, bass.ds(i + 2, 1), t, :] if which == 0 else ys[:, 0, t, :]
                        a.activation(y, y, ACT.Sigmoid).then_inc(gate_out, 1)

            def turn_y(b):
                act.wait_ge(yt_psum, b + 1)
                a.activation(act_hi[:, 2 * b:2 * b + 2, :], ps[:, 4 + b % 4, :], ACT.Copy).then_inc(yt_hi, 1)

            for kt in range(2 * UT):
                ahead(CH_EP, kt)
                if kt in EARLY_Y:
                    turn_y(EARLY_Y.index(kt))

            def store(i):
                for t in range(TT):
                    act.wait_ge(acc_free[t], i + (Q_P4 + 2))
                act.dma_start(out_pt[:, :, bass.ds(i * WIDTH, WIDTH)], x_out[:, bass.ds(i, 1), :, :]).then_inc(
                    out_stored, 16)

            for kt in range(KT):
                ahead(CH_P4, kt)
                if kt in LAST_Y:
                    turn_y(len(EARLY_Y) + LAST_Y.index(kt))
            store(0)
            with act.Fori(1, N_Y - 1) as i:
                for kt in range(KT):
                    ahead(i * KT + CH_P4, kt)
                store(i)
            for kt in range(KT):
                ahead(CH_P4 + (N_Y - 1) * KT, kt, last=True)
            for t in range(TT):
                act.wait_ge(acc_free[t], Q_P4 + N_Y + 1)
                act.dma_start(out_pt[:, t:t + 1, (N_Y - 1) * WIDTH:], x_out[:, N_Y - 1, t:t + 1, :]).then_inc(
                    out_stored, 16)
            act.wait_ge(out_stored, 16 * (N_Y + 1))

        @block.vector
        def _(dve):
            v = nc.vector
            dve.sem_inc(split_done, RING)
            dve.sem_inc(acc_free[0], 1)
            dve.sem_inc(acc_free[1], 1)
            dve.sem_inc(head_out, 1)
            dve.sem_inc(nt_lo, 2)
            dve.sem_inc(pool_lo_done, 2)

            def split(chunk, slot):
                dve.wait_ge(hi_done, chunk)
                v.tensor_tensor(w_lo[:, slot, :], raw[:, slot, :], up(w_hi[:, slot, :]), ALU.subtract).then_inc(
                    split_done, 1)

            def ahead(first, kt, last=False):
                if last and kt >= KT - LEAD:
                    return
                split(first + (kt + LEAD + 1), (kt + LEAD) % RING)

            dve.wait_ge(vec_psum, 1)
            v.tensor_copy(vec_t[:, V_NORM:V_NORM + KT], ps[:, 7, 0:KT]).then_inc(vec_ready, 1)
            dve.wait_ge(vec_ready, 1)
            for w_ in (wg_hi, wg_lo):
                v.memset(up(w_[:, WG:]), 0.0).then_inc(wg_padded, 1)

            def turn_x(b):
                dve.wait_ge(xt_hi, b + 1)
                for e in range(2):
                    kt = 2 * b + e
                    k = v.scalar_tensor_tensor(act_lo[:, kt, :], ps[:, 4 + b % 4, e * T:(e + 1) * T],
                                               vec_t[:, V_NORM + kt:V_NORM + kt + 1], up(act_hi[:, kt, :]),
                                               ALU.mult, ALU.subtract)
                k.then_inc(xt_lo, 1)

            turn_x(0)
            for c in range(LEAD):
                split(c + 1, c)
            turn_x(1)

            def leave(last_chunk, dst):
                dve.wait_ge(weights_free, last_chunk + RING)
                v.tensor_scalar(dst, ps[:, NH:2 * NH, :], rstd[:, 1:2], None, ALU.mult).then_inc(acc_free[1], 1)

            for kt in range(KT):
                ahead(0, kt)
                if kt % 2 == 0 and kt // 2 + 2 < KT // 2:
                    turn_x(kt // 2 + 2)
                if kt % 8 == 5:
                    c = kt // 8
                    piece = x_tok[:, 1, c * WIDTH:(c + 1) * WIDTH]
                    dve.wait_ge(x_psum, 4 * c + 4)
                    v.tensor_tensor_reduce(out=piece, in0=piece, in1=piece, scale=1.0, scalar=0.0, op0=ALU.mult,
                                           op1=ALU.add, accum_out=row_parts[:, 1, c:c + 1]).then_inc(sq_dve, 1)
                if kt == SMALL_AT:
                    dve.wait_ge(vec_psum, 2)
                    v.tensor_copy(vec_t[:, V_NORM + KT:V_END], ps[:, 7, V_NORM + KT:V_END]).then_inc(vec_ready, 1)
            dve.wait_ge(sq_act, N_Y)
            dve.wait_ge(sq_dve, N_Y)
            v.reduce_sum(row_ss[:], row_parts[:], AX.X).then_inc(row_sum, 1)
            dve.wait_ge(row_sum, 1)
            v.tensor_scalar(row_ss[:], row_ss[:], 1.0 / D, EPS, ALU.mult, ALU.add).then_inc(row_ms, 1)
            dve.wait_ge(rstd_ready, 1)
            leave(KT, kvq[:, 0:2, 1, :])

            def sum_squares(n, ss):
                dve.wait_ge(qk_sq, n + 1)
                v.reduce_sum(ss.rearrange("p t h -> p (t h)"), sq_a[:], AX.X).then_inc(qk_ss, 1)
                dve.wait_ge(qk_ss, n + 1)

            def mean_plus_eps(ss):
                return v.tensor_scalar(ss[:], ss[:], 1.0 / HD, EPS, ALU.mult, ALU.add)

            with dve.Fori(1, N_PROJ - 1) as i:
                for kt in range(KT):
                    ahead(i * KT, kt)
                leave(i * KT + KT, kvq[:, bass.ds(i * 2, 2), 1, :])

            base = (N_PROJ - 1) * KT
            for kt in range(KT):
                if kt == 0:
                    dve.wait_ge(wg_hi_done, 1)
                    v.tensor_tensor(wg_lo[:, 0:WG], wg[:], up(wg_hi[:, 0:WG]), ALU.subtract).then_inc(wg_lo_done, 1)
                    dve.wait_ge(wg_lo_done, 1)
                    for n, kb in enumerate((kb_k, kb_v)):
                        v.memset(kb[:, :, KVH, :], 0.0).then_inc(kb_zero, 1)
                        dve.wait_ge(kb_zero, n + 1)
                        v.tensor_copy(kb[:, :, KVH, 0], vec_t[:, V_PE + n * CMP_BLOCK:V_PE + n * CMP_BLOCK + CMP_STRIDE])
                        v.tensor_copy(kb[:, :, KVH, CMP_STRIDE - 1],
                                      vec_t[:, V_PE + n * CMP_BLOCK + CMP_STRIDE:V_PE + (n + 1) * CMP_BLOCK]).then_inc(
                            kb_pos, 1)
                ahead(base, kt)
                if kt in (8, 10):
                    sum_squares((kt - 8) // 2, k_ss[:, (kt - 8) // 2])
                    if kt == 10:
                        mean_plus_eps(k_ss).then_inc(k_ms, 1)
                if kt == 12:
                    sum_squares(2, q_ss[:])
                    mean_plus_eps(q_ss).then_inc(q_ms, 1)
                if kt == 20:
                    dve.wait_ge(gate_sig, 1)
                    dve.wait_ge(const_ready, 5)
                    v.tensor_scalar(gate6[:, :, 4], gate6[:, :, 4], row_mask[:], None, ALU.mult).then_inc(gate_ready, 1)
                    v.tensor_scalar(vec_t[:, V_QG:V_QG + 1], vec_t[:, V_QG:V_QG + 1], HD ** -0.5, None,
                                    ALU.mult).then_inc(gate_ready, 1)
                if kt == 21:
                    dve.wait_ge(hid_psum, 1)
                    for n in range(2):
                        first, second = KVH * NC, (KVH + 1) * NC - 1
                        v.tensor_tensor(hid_b[:, n:n + 1], vec_t[:, V_B1 + n:V_B1 + n + 1], ps[:, 6 + n, first:first + 1],
                                        ALU.add).then_inc(hid_step, 1)
                        dve.wait_ge(hid_step, 2 * n + 1)
                        v.tensor_scalar(hid_x[:, n, :], ps[:, 6 + n, 0:KVH * NC], hid_b[:, n:n + 1],
                                        ps[:, 6 + n, second:second + 1], ALU.add, ALU.add).then_inc(hid_step, 1)
                if kt == 22:
                    dve.wait_ge(hid_sig, 1)
                    v.tensor_tensor(hid[:], hid_x[:], hid_s[:], ALU.mult).then_inc(hid_step, 1)
                if kt == 24:
                    dve.wait_ge(w2_psum, 1)
                    v.tensor_copy(kc_n[:], ps[0:KVH * NC, 6, 128:256]).then_inc(kc_step, 1)
                    dve.wait_ge(kc_step, 1)
                    v.tensor_tensor_reduce(out=kc_sq[:], in0=kc_n[:], in1=kc_n[:], scale=1.0, scalar=0.0,
                                           op0=ALU.mult, op1=ALU.add, accum_out=kc_ss[:]).then_inc(kc_step, 1)
                    dve.wait_ge(kc_step, 2)
                    v.tensor_scalar(kc_ss[:], kc_ss[:], 1.0 / HD, EPS, ALU.mult, ALU.add).then_inc(kc_step, 1)
                if kt == 25:
                    dve.wait_ge(kc_rstd, 1)
                    v.tensor_scalar(kc_n[:], kc_n[:], kc_rs[:], None, ALU.mult).then_inc(kc_step, 1)
                if kt == 27:
                    dve.wait_ge(kct_psum, 1)
                    v.tensor_scalar(kc_t[:], ps[:, 6, 0:KVH * NC], vec_t[:, V_KG:V_KG + 1], None, ALU.mult).then_inc(
                        kct_ready, 1)
            leave(N_PROJ * KT, kvq[:, 2 * (N_PROJ - 1):2 * N_PROJ, 1, :])
            dve.wait_ge(gate_ready, 2)
            dve.wait_ge(acc_free[0], 1 + N_PROJ)
            dve.wait_ge(k_rstd, 1)

            with dve.Fori(0, KVH) as j:
                for kt in range(KT):
                    ahead(j * KT + CH_L2, kt)
                    if kt == 0:
                        dve.wait_ge(q_rstd, j + 1)
                        for t in range(TT):
                            v.tensor_tensor(qk[:, t, 0:GQ, :], kvq[:, bass.ds(j + 6, 1), t, :].rearrange(
                                "p a (m d) -> p (a m) d", d=HD),
                                q_rs[:, t, :].unsqueeze(2).to_broadcast([P, GQ, HD]), ALU.mult)
                            k = v.tensor_tensor(qk[:, t, GQ:GQ + 2, :], kvq[:, 2:6:2, t, bass.ds(j * HD, HD)],
                                                k_rs[:, 0:2, t, bass.ds(j, 1)].to_broadcast([P, 2, HD]), ALU.mult)
                        k.then_inc(qk_normed, 1)
                    if kt == 2:
                        dve.wait_ge(qkt_psum, j + 1)
                        v.tensor_scalar(qk_t[:, 0:4, :], ps[:, 4:6, :], vec_t[:, V_QG:V_QG + 1], None,
                                        ALU.mult).then_inc(qkt_dve, 1)
                    if kt in SCORES:
                        h = SCORES.index(kt)
                        dve.wait_ge(scores_done, j * GQ + (h + 1))
                        v.tensor_tensor(s[:], ps[:, 4:6, 0:3 * P],
                                        dist[:, h, :].unsqueeze(1).to_broadcast([P, 2, 3 * P]), ALU.add).then_inc(biased, 1)
                        v.tensor_tensor(s_cmp[:], ps[:, 4:6, 3 * P:3 * P + NC], dist_c[:, h], ALU.add).then_inc(biased, 1)
                        dve.wait_ge(biased, j * (2 * GQ) + (2 * h + 2))
                        v.tensor_reduce(neg_max[:, 0:2], s[:, :, 0:P], AX.X, ALU.max, negate=True)
                        v.tensor_reduce(neg_max[:, 2:4], s[:, :, P:3 * P], AX.X, ALU.max, negate=True)
                        v.tensor_reduce(neg_max[:, 4:6], s_cmp[:], AX.X, ALU.max, negate=True).then_inc(head_max, 1)
                    if kt == 13:
                        dve.wait_ge(qk_normed, j + 1)
                        sum_squares(j + 3, q_ss[:])
                        mean_plus_eps(q_ss).then_inc(q_ms, 1)
                    if kt in SCALES:
                        h = SCALES.index(kt)
                        dve.wait_ge(exp_done, j * GQ + (h + 1))
                        v.reciprocal(inv[:], sums[:]).then_inc(inv_done, 1)
                        dve.wait_ge(inv_done, j * GQ + (h + 1))
                        v.tensor_tensor(wgt[:], inv[:], gate6[:, bass.ds(j * GQ + h, 1), :], ALU.mult).then_inc(
                            wgt_done, 1)
                        dve.wait_ge(wgt_done, j * GQ + (h + 1))
                        for br in range(2):
                            v.tensor_scalar(s[:, br, 0:P], s[:, br, 0:P], wgt[:, br:br + 1], None, ALU.mult)
                            v.tensor_scalar(s[:, br, P:3 * P], s[:, br, P:3 * P], wgt[:, 2 + br:3 + br], None, ALU.mult)
                        for t in range(TT):
                            k = v.tensor_scalar(s_cmp[:, t, :], s_cmp[:, t, :], wgt[:, 4 + t:5 + t], None, ALU.mult)
                        k.then_inc(probs_ready, 1)
                    if kt in VALUES:
                        h = VALUES.index(kt)
                        dve.wait_ge(pv_done, j * GQ + (h + 1))
                        v.tensor_scalar(kvq[:, bass.ds(j + 6, 1), :, h * HD:(h + 1) * HD],
                                        ps[:, 4:6, 3 * P:4 * P], 1.0, None, ALU.mult).then_inc(head_out, 1)
                    if kt == 28:
                        v.tensor_scalar(dist[:], dist[:], 0.25, None, ALU.mult)
                        v.tensor_scalar(dist_c[:], dist_c[:], 0.25, None, ALU.mult)
                leave(j * KT + (CH_L2 + KT), uz[:, bass.ds(j * 2, 2), 1, :])

            def pool_group(kt, n):
                if kt == POOL_MIX:
                    for half in range(2):
                        c = slice(2 * half, 2 * half + 2)
                        dve.wait_ge(mix_hi_done, n * 2 + (half + 1))
                        v.tensor_tensor(mix_lo[:, c, :], ps[:, 4 + half, :].rearrange("p (a b) -> p a b", a=2),
                                        up(mix_hi[:, c, :]), ALU.subtract).then_inc(mix_lo_done, 1)
                if kt in PW_SPLITS:
                    half = PW_SPLITS.index(kt)
                    c = slice(2 * half, 2 * half + 2)
                    dve.wait_ge(pw_hi_done, n * 2 + (half + 1))
                    v.tensor_tensor(pw_lo[:, c, :], pw[:, c, :], up(pw_hi[:, c, :]), ALU.subtract).then_inc(
                        pw_lo_done, 1)
                if kt == POOL_MIX + 1:
                    for half in range(2):
                        dve.wait_ge(zt_sig, n * 2 + (half + 1))
                        c = silu_zt[:, 2 * half:2 * half + 2, :]
                        v.tensor_tensor(c, c, ps[:, 6 + half, :], ALU.mult).then_inc(zt_silu, 1)
                if kt in POOL_ENDS:
                    b = POOL_ENDS.index(kt)
                    dve.wait_ge(pwt_psum, n * 2 + (b + 1))
                    dve.wait_ge(zt_silu, n * 2 + 2)
                    for e in range(2):
                        dt = 2 * b + e
                        k = v.scalar_tensor_tensor(silu_zt[:, dt, :], ps[:, 4 + b, e * T:(e + 1) * T],
                                                   scale_g[:, dt:dt + 1], silu_zt[:, dt, :], ALU.mult, ALU.mult)
                    k.then_inc(pool_v, 1)
                    dve.wait_ge(pool_hi_done, n * 2 + (b + 1))
                    at_ = bass.ds(n * 4 + 2 * b, 2)
                    v.tensor_tensor(pool_lo[:, at_, :], silu_zt[:, 2 * b:2 * b + 2, :], up(pool_hi[:, at_, :]),
                                    ALU.subtract).then_inc(pool_lo_done, 1)

            def gate_leave(n, chunk_done, q, dst):
                dve.wait_ge(bias_landed, n * 16 + 16)
                for t in range(TT):
                    if t == 0:
                        dve.wait_ge(acc_done, q + 1)
                    else:
                        dve.wait_ge(weights_free, chunk_done + RING)
                    v.scalar_tensor_tensor(dst(t), ps[:, NH * t:NH * t + NH, :].rearrange("p a b -> p (a b)"),
                                           rstd[:, t:t + 1], bias[:], ALU.mult, ALU.add).then_inc(acc_free[t], 1)

            with dve.Fori(0, 2) as i:
                for kt in range(KT):
                    ahead(i * 2 * KT + CH_TL, kt)
                    pool_group(kt, i * 2)
                for t in range(TT):
                    dve.wait_ge(nz_sig, i * 2 + (t + 1))
                    v.scalar_tensor_tensor(n_tok[:, t, :], ps[:, NH * t:NH * t + NH, :].rearrange("p a b -> p (a b)"),
                                           rstd[:, t:t + 1], n_tok[:, t, :], ALU.mult, ALU.mult).then_inc(acc_free[t], 1)
                for t in range(TT):
                    dve.wait_ge(acc_free[t], i * 2 + (Q_TL + 2))
                    k = v.tensor_tensor(n_tok[:, t, :].rearrange("p (a b) -> p a b", a=2),
                                        n_tok[:, t, :].rearrange("p (a b) -> p a b", a=2),
                                        kvq[:, bass.ds(i * 2 + 6, 2), t, :], ALU.mult)
                k.then_inc(n_ready, 1)
                for kt in range(KT):
                    ahead(i * 2 * KT + CH_TL + KT, kt)
                    if kt in (1, 3, 5, 7):
                        b = kt // 2
                        dve.wait_ge(nt_hi, i * 4 + (b + 1))
                        at_ = bass.ds(i * 8 + 2 * b, 2)
                        v.tensor_tensor(nsa_lo[:, at_, :], ps[:, 6 + b % 2, :].rearrange("p (a b) -> p a b", a=2),
                                        up(nsa_hi[:, at_, :]), ALU.subtract).then_inc(nt_lo, 1)
                    pool_group(kt, i * 2 + 1)
                gate_leave(i, i * 2 * KT + (CH_TL + 2 * KT), i * 2 + (Q_TL + 1),
                           lambda t: ys[:, bass.ds(i * -1 + 1, 1), t, :])

            def times(y, t):
                return v.tensor_tensor(y, y, ps[:, NH * t:NH * t + NH, :].rearrange("p a b -> p (a b)"), ALU.mult)

            def pool_leave(chunk_done, q, n, y):
                dve.wait_ge(gate_out, n * 4 + 4)
                dve.wait_ge(acc_done, q + 1)
                times(y(0), 0).then_inc(acc_free[0], 1)
                dve.wait_ge(weights_free, chunk_done + RING)
                times(y(1), 1).then_inc(acc_free[1], 1)

            def nsa_leave(chunk_done, q, y):
                dve.wait_ge(acc_done, q + 1)
                times(ys[:, 0, 0, :], 0).then_inc(acc_free[0], 1)
                dve.wait_ge(weights_free, chunk_done + RING)
                times(ys[:, 0, 1, :], 1).then_inc(acc_free[1], 1)
                for t in range(TT):
                    dve.wait_ge(acc_free[t], q + 2)
                    k = v.tensor_tensor(y(t), y(t), ys[:, 0, t, :], ALU.add)
                k.then_inc(y_sum, 1)

            with dve.Fori(0, N_Y - 1) as i:
                for kt in range(UT):
                    ahead(i * PER3 + CH_P3, kt)
                y = lambda t: ys[:, bass.ds(i + 1, 1), t, :]
                pool_leave(i * PER3 + (CH_P3 + UT), i * 4 + Q_P3, i, y)
                for kt in range(UT):
                    ahead(i * PER3 + CH_P3 + UT, kt)
                nsa_leave(i * PER3 + (CH_P3 + 2 * UT), i * 4 + (Q_P3 + 1), y)
                for which in range(2):
                    for kt in range(KT):
                        ahead(i * PER3 + CH_P3 + 2 * UT + which * KT, kt)
                    gate_leave(i * 2 + (2 + which), i * PER3 + (CH_P3 + 2 * UT + (which + 1) * KT),
                               i * 4 + (Q_P3 + 2 + which),
                               (lambda t: ys[:, bass.ds(i + 2, 1), t, :]) if which == 0 else (lambda t: ys[:, 0, t, :]))

            def turn_y(b):
                dve.wait_ge(yt_hi, b + 1)
                v.tensor_tensor(act_lo[:, 2 * b:2 * b + 2, :], ps[:, 4 + b % 4, :].rearrange("p (a b) -> p a b", a=2),
                                up(act_hi[:, 2 * b:2 * b + 2, :]), ALU.subtract).then_inc(yt_lo, 1)

            y_last = lambda t: ys[:, N_Y, t, :]
            for kt in range(2 * UT):
                ahead(CH_EP, kt)
                if kt in EARLY_Y:
                    turn_y(EARLY_Y.index(kt))
                if kt == UT - 1:
                    pool_leave(CH_EP + UT, Q_EP, N_Y - 1, y_last)
            nsa_leave(CH_EP + 2 * UT, Q_EP + 1, y_last)

            def out_leave(q, chunk_done, xo):
                for t in range(TT):
                    if t == 0:
                        dve.wait_ge(acc_done, q + 1)
                    else:
                        dve.wait_ge(weights_free, chunk_done + RING)
                    v.tensor_tensor(xo(t), xo(t), ps[:, NH * t:NH * t + NH, :].rearrange("p a b -> p (a b)"),
                                    ALU.add).then_inc(acc_free[t], 1)

            for kt in range(KT):
                ahead(CH_P4, kt)
                if kt in LAST_Y:
                    turn_y(len(EARLY_Y) + LAST_Y.index(kt))
            dve.wait_ge(xo_landed, 16 * N_Y)
            out_leave(Q_P4, CH_P4 + KT, lambda t: x_out[:, 0, t, :])
            with dve.Fori(1, N_Y - 1) as i:
                for kt in range(KT):
                    ahead(i * KT + CH_P4, kt)
                out_leave(i + Q_P4, i * KT + (CH_P4 + KT), lambda t: x_out[:, bass.ds(i, 1), t, :])
            for kt in range(KT):
                ahead(CH_P4 + (N_Y - 1) * KT, kt, last=True)
            out_leave(Q_P4 + N_Y - 1, CHUNKS, lambda t: x_out[:, N_Y - 1, t, :])

        @block.tensor
        def _(pe):
            pe.sem_inc(weights_free, RING)
            mm, tr = nc.tensor.matmul, nc.tensor.transpose

            def product(first, q, hi, lo, side=None, before=None):
                tiles = hi.shape[1]
                order = [(kt, t) for kt in range(2, tiles - 2) for t in range(TT)]
                ends = [[(k, t) for t in range(TT) for k in (kt, kt + 1)] for kt in (0, tiles - 2)]
                for kt, t in ends[0] + order + ends[1]:
                    slot = kt % RING
                    if t == 0:
                        if before:
                            before(kt)
                        pe.wait_ge(split_done, first + (kt + 1 + RING))
                    if kt == 0:
                        pe.wait_ge(acc_free[t], q + 1)
                    for part, (a_, w_) in enumerate(((hi, w_hi), (hi, w_lo), (lo, w_hi))):
                        for n in range(NH):
                            m = mm(ps[:, NH * t + n, :], a_[:, kt, t * P:(t + 1) * P],
                                   w_[:, slot, n * BANK:(n + 1) * BANK],
                                   start=(kt == 0 and part == 0), stop=(kt == tiles - 1 and part == 2))
                    if t == 0 and kt == tiles - 1:
                        m.then_inc(acc_done, 1)
                    if t == TT - 1:
                        m.then_inc(weights_free, 1)
                        if side:
                            side(kt)

            def keep_warm(n):
                for _ in range(n):
                    tr(ps[:, 6, 0:P], ident[:], ident[:])

            pe.wait_ge(const_ready, 1)
            keep_warm(16)
            pe.wait_ge(norm_landed, 16)
            tr(ps[:, 7, 0:KT], vec_rows[V_NORM:V_NORM + KT, :], ident[0:KT, 0:KT]).then_inc(vec_psum, 1)

            def turn_x(b):
                if 2 * b * P in X_CUTS:
                    pe.wait_ge(x_landed[X_CUTS.index(2 * b * P)], 16)
                if b == 3:
                    pe.wait_ge(vec_ready, 1)
                if b >= 4:
                    pe.wait_ge(xt_lo, b - 3)
                for e in range(2):
                    for t in range(TT):
                        k = tr(ps[:, 4 + b % 4, (2 * e + t) * P:(2 * e + t + 1) * P],
                               x_tok[:, t, (2 * b + e) * P:(2 * b + e + 1) * P], ident[:])
                k.then_inc(x_psum, 1)

            def turn_beside(kt):
                if kt % 2 == 0 and kt // 2 + 2 < KT // 2:
                    turn_x(kt // 2 + 2)
                if kt == SMALL_AT:
                    pe.wait_ge(vec_landed, 16 * 5)
                    pe.wait_ge(xt_lo, KT // 2)
                    tr(ps[:, 7, 0:V_END], vec_rows[0:V_END, :], ident[0:V_END, 0:V_END]).then_inc(vec_psum, 1)

            turn_x(0)
            keep_warm(12)
            turn_x(1)
            keep_warm(12)
            product(0, 0, act_hi, act_lo, turn_beside,
                    before=lambda kt: kt % 2 == 0 and pe.wait_ge(xt_lo, kt // 2 + 1))
            with pe.Fori(1, N_PROJ - 1) as i:
                product(i * KT, i, act_hi, act_lo)

            def gates_and_compression(kt):
                if kt == 0:
                    pe.wait_ge(wg_lo_done, 1)
                    pe.wait_ge(wg_padded, 2)
                if kt < KT // 2:
                    for g in (2 * kt, 2 * kt + 1):
                        for part, (w_, a_) in enumerate(((wg_hi, act_hi), (wg_lo, act_hi), (wg_hi, act_lo))):
                            k = mm(ps[:, 4, 0:T], w_[:, g * GATES:g * GATES + P], a_[:, g, :],
                                   start=(g == 0 and part == 0), stop=(g == KT - 1 and part == 2))
                if kt == KT // 2 - 1:
                    k.then_inc(gate_psum, 1)
                if kt == 18:
                    pe.wait_ge(gate_lin, 1)
                    for t in range(TT):
                        k = tr(ps[:, 5, t * GATES:(t + 1) * GATES], gate_t[:, t * P:(t + 1) * P],
                               ident[0:GATES, 0:GATES])
                    k.then_inc(gate_turned, 1)
                if kt in (2, 6):
                    n = (kt - 2) // 4
                    if n == 0:
                        pe.wait_ge(acc_free[0], 1 + 1)
                        pe.wait_ge(acc_free[1], 1 + 1)
                    else:
                        pe.wait_ge(ct_sbuf, 1)
                    for h in range(KVH):
                        for t in range(TT):
                            k = tr(ps[:, 6 + h // 2, ((h % 2) * TT + t) * P:((h % 2) * TT + t + 1) * P],
                                   kvq[:, n, t, h * HD:(h + 1) * HD], ident[:])
                    k.then_inc(ct_psum, 1)
                if 10 <= kt < 20:
                    if kt == 10:
                        pe.wait_ge(ct_sbuf, 2)
                        pe.wait_ge(w1_landed, 16 * 9)
                    js = range((kt - 10) * 16 // 5, (kt - 9) * 16 // 5)
                    for j in js:
                        late = j // CMP_STRIDE
                        for n, kb in enumerate((kb_k, kb_v)):
                            k = mm(ps[:, 6 + n, 0:(KVH + 1) * NC], w1[:, n, j, :],
                                   kb[:, j % CMP_STRIDE, :, late:late + NC],
                                   start=(j == 0), stop=(j == CMP_BLOCK - 1))
                    if kt == 19:
                        k.then_inc(hid_psum, 1)
                if kt == 24:
                    pe.wait_ge(hid_step, 5)
                    mm(ps[0:KVH * NC, 6, 128:256], hid[:, 0, :], w2[:, 0, :], start=True, stop=True)
                    for h in range(KVH):
                        k = mm(ps[0:NC, 7, h * HD:(h + 1) * HD], hid[:, 1, h * NC:(h + 1) * NC], w2[:, 1, :],
                               start=True, stop=True)
                    k.then_inc(w2_psum, 1)
                if kt == 27:
                    pe.wait_ge(kc_step, 4)
                    tr(ps[:, 6, 0:KVH * NC], kc_n[:], ident[0:KVH * NC, 0:KVH * NC]).then_inc(kct_psum, 1)

            product((N_PROJ - 1) * KT, N_PROJ - 1, act_hi, act_lo, gates_and_compression)
            pe.wait_ge(kct_ready, 1)
            pe.wait_ge(vc_ready, 1)
            pe.wait_ge(gate_ready, 2)

            with pe.Fori(0, KVH) as j:
                def attention(kt):
                    if kt == 2:
                        pe.wait_ge(qk_normed, j + 1)
                        pe.wait_ge(head_out, j * GQ + 1)
                        for m in range(6):
                            for t in range(TT):
                                k = tr(ps[:, 4 + m // 2, ((m % 2) * TT + t) * P:((m % 2) * TT + t + 1) * P],
                                       qk[:, t, m, :], ident[:])
                        k.then_inc(qkt_psum, 1)
                    if kt in SCORES:
                        h = SCORES.index(kt)
                        if h == 0:
                            pe.wait_ge(qkt_act, j + 1)
                            pe.wait_ge(qkt_dve, j + 1)
                        pe.wait_ge(head_out, j * GQ + (h + 1))
                        for br in range(2):
                            mm(ps[:, 4 + br, 0:P], qk_t[:, h, 0:P], qk_t[:, 4 + br, 0:P], start=True, stop=True)
                            mm(ps[:, 4 + br, P:3 * P], qk_t[:, h, P:2 * P], qk_t[:, 4 + br, :], start=True, stop=True)
                        for t in range(TT):
                            k = mm(ps[:, 4 + t, 3 * P:3 * P + NC], qk_t[:, h, t * P:(t + 1) * P],
                                   kc_t[:, bass.ds(j * NC, NC)], start=True, stop=True)
                        k.then_inc(scores_done, 1)
                    if kt in TURNS:
                        h = TURNS.index(kt)
                        pe.wait_ge(probs_ready, j * GQ + (h + 1))
                        for br in range(2):
                            for b in range(3):
                                tr(ps[:, 6 + br, b * P:(b + 1) * P], s[:, br, b * P:(b + 1) * P], ident[:])
                        for t in range(TT):
                            k = tr(ps[0:NC, 6 + t, 3 * P:4 * P], s_cmp[:, t, :], ident[:])
                        k.then_inc(probt_psum, 1)
                    if kt in VALUES:
                        h = VALUES.index(kt)
                        pe.wait_ge(probt_ready, j * GQ + (h + 1))
                        vals = lambda half, t: kvq[:, half, t, bass.ds(j * HD, HD)]
                        for t in range(TT):
                            o = ps[:, 4 + t, 3 * P:4 * P]
                            first = True
                            for br, half in ((0, 3), (1, 5)):
                                for kb in range(t + 1):
                                    mm(o, prob_t[:, br, (t + kb) * P:(t + kb + 1) * P], vals(half, kb),
                                       start=first, stop=False)
                                    first = False
                            k = mm(o, prob_ct[:, t, :], vc[:, bass.ds(j, 1), :], start=False, stop=True)
                        k.then_inc(pv_done, 1)

                product(j * KT + CH_L2, j + Q_L2, act_hi, act_lo, attention)

            def pool_group(kt, n):
                if kt == POOL_MIX:
                    pe.wait_ge(band_built, BAND_STEPS)
                    pe.wait_ge(uz_copied, n + 1)
                    for c in range(PG // P):
                        o = ps[:, 4 + c // 2, (c % 2) * T:(c % 2 + 1) * T]
                        for t in range(TT):
                            mm(o[:, t * P:(t + 1) * P], u_g[:, t, c * P:(c + 1) * P], band[:, bass.ds(n, 1), t, :],
                               start=True, stop=(t == 0))
                        k = mm(o[:, P:P + max(WINDOWS)], u_g[:, 0, c * P:(c + 1) * P], band_x[:, bass.ds(n, 1), :],
                               start=False, stop=True)
                    k.then_inc(mix_psum, 1)
                    for c in range(PG // P):
                        for t in range(TT):
                            k = tr(ps[:, 6 + c // 2, ((c % 2) * TT + t) * P:((c % 2) * TT + t + 1) * P],
                                   z_g[:, t, c * P:(c + 1) * P], ident[:])
                    k.then_inc(zt_psum, 1)
                if kt in POOL_PRODUCTS:
                    d = POOL_PRODUCTS.index(kt)
                    if d == 0:
                        pe.wait_ge(mix_lo_done, n * 2 + 2)
                        pe.wait_ge(pw_lo_done, n * 2 + 2)
                    for c in range(PG // P):
                        for part, (w_, m_) in enumerate(((pw_hi, mix_hi), (pw_hi, mix_lo), (pw_lo, mix_hi))):
                            k = mm(ps[:, 4 + d // 2, (d % 2) * T:(d % 2 + 1) * T], w_[:, c, d * P:(d + 1) * P],
                                   m_[:, c, :], start=(c == 0 and part == 0), stop=(c == PG // P - 1 and part == 2))
                    if d % 2:
                        k.then_inc(pwt_psum, 1)

            with pe.Fori(0, 2) as i:
                product(i * 2 * KT + CH_TL, i * 2 + Q_TL, act_hi, act_lo, lambda kt: pool_group(kt, i * 2))

                def turn_and_pool(kt):
                    if kt in (1, 3, 5, 7):
                        b = kt // 2
                        if b == 0:
                            pe.wait_ge(n_ready, i + 1)
                            pe.wait_ge(pool_lo_done, i * 4 + 4)
                        pe.wait_ge(nt_lo, i * 4 + (b + 1))
                        for e in range(2):
                            for t in range(TT):
                                k = tr(ps[:, 6 + b % 2, (2 * e + t) * P:(2 * e + t + 1) * P],
                                       n_tok[:, t, (2 * b + e) * P:(2 * b + e + 1) * P], ident[:])
                        k.then_inc(nt_psum, 1)
                    if kt == POOL_MIX:
                        pe.wait_ge(nt_lo, i * 4 + 6)
                    pool_group(kt, i * 2 + 1)

                product(i * 2 * KT + CH_TL + KT, i * 2 + (Q_TL + 1), act_hi, act_lo, turn_and_pool)

            pe.wait_ge(pool_lo_done, 2 + 8)
            pe.wait_ge(nt_lo, 2 + 8)
            with pe.Fori(0, N_Y - 1) as i:
                product(i * PER3 + CH_P3, i * 4 + Q_P3, pool_hi, pool_lo)
                product(i * PER3 + (CH_P3 + UT), i * 4 + (Q_P3 + 1), nsa_hi, nsa_lo)
                for which in range(2):
                    product(i * PER3 + (CH_P3 + 2 * UT + which * KT), i * 4 + (Q_P3 + 2 + which), act_hi, act_lo)

            def turn_y(b):
                g, e0 = b // 4, 2 * (b % 4)
                if b >= 4:
                    pe.wait_ge(yt_lo, b - 3)
                for e in range(2):
                    for t in range(TT):
                        k = tr(ps[:, 4 + b % 4, (2 * e + t) * P:(2 * e + t + 1) * P],
                               ys[:, 1 + g, t, (e0 + e) * P:(e0 + e + 1) * P], ident[:])
                k.then_inc(yt_psum, 1)

            def turn_from(start):
                def side(kt):
                    if kt + start in EARLY_Y:
                        if kt + start == EARLY_Y[0]:
                            pe.wait_ge(y_sum, N_Y - 1)
                        turn_y(EARLY_Y.index(kt + start))
                return side

            product(CH_EP, Q_EP, pool_hi, pool_lo, turn_from(0))
            product(CH_EP + UT, Q_EP + 1, nsa_hi, nsa_lo, turn_from(UT))

            def turn_last(kt):
                if kt in LAST_Y:
                    if kt == LAST_Y[1]:
                        pe.wait_ge(y_sum, N_Y)
                    turn_y(len(EARLY_Y) + LAST_Y.index(kt))

            product(CH_P4, Q_P4, act_hi, act_lo, turn_last,
                    before=lambda kt: kt in (0, 2 * len(EARLY_Y)) and pe.wait_ge(yt_lo, KT // 2 if kt else len(EARLY_Y)))
            with pe.Fori(1, N_Y) as i:
                product(i * KT + CH_P4, i + Q_P4, act_hi, act_lo)


_INS = ["x", "norm_g", "w_in", "merge_bias", "pool_w", "pool_scale", "q_norm_g", "k_norm_g", "cmp_pe", "cmp_w1",
        "cmp_b1", "cmp_w2", "w_pool_up", "w_nsa_up", "w_out"]


def kernel(**inputs):
    import numpy as np
    from concourse import bacc
    from concourse.bass_utils import run_bass_kernel_spmd

    nc = bacc.Bacc("TRN2", target_bir_lowering=False, num_devices=1, dynamic_dma_scratch_size=1024)
    arrays, args = {}, []
    for name in _INS:
        a = np.ascontiguousarray(inputs[name])
        arrays[f"in_{name}"] = a
        args.append(nc.dram_tensor(f"in_{name}", a.shape, mybir.dt.from_np(a.dtype), kind="ExternalInput").ap())
    out = nc.dram_tensor("out_y", inputs["x"].shape, F32, kind="ExternalOutput").ap()
    trunk(nc, *args, out)
    r = run_bass_kernel_spmd(nc, [arrays], core_ids=[0])
    return r.results[0]["out_y"]
```
